# Optimizing a Trainium2 kernel written in Bass

```python
import math
import jax
import jax.numpy as jnp
from jax import lax
import numpy as np
import jax, jax.numpy as jnp

D_MODEL = 1024
BATCH = 1
SEQ = 256
DEPTH = 2

MEM_LEN = 256
GRID_W = 64
CHUNK = 128
Q_BLOCK = 128
EPS = 1e-6
GM_GROUPS = 4
GM_GROUP_DIM = 128
GM_WIDTH = GM_GROUPS * GM_GROUP_DIM
HEAD_DIM = 64
N_Q_HEADS = 8
N_KV_HEADS = 2
Q_PER_KV = N_Q_HEADS // N_KV_HEADS
ATT_WIDTH = N_Q_HEADS * HEAD_DIM
KV_WIDTH = N_KV_HEADS * HEAD_DIM
ROPE_THETA = 10000.0
MIX_WIDTH = GM_WIDTH + ATT_WIDTH
IN_WIDTH = 2 * GM_WIDTH + ATT_WIDTH + 2 * KV_WIDTH
SPLITS = (GM_WIDTH, 2 * GM_WIDTH, 2 * GM_WIDTH + ATT_WIDTH, 2 * GM_WIDTH + ATT_WIDTH + KV_WIDTH)
X_HEADS = 4
X_HEAD_DIM = D_MODEL // X_HEADS
N_EXPERTS = 16
EC_FACTOR = 2
EXPERT_FF = 1024


def rms_norm(x, g):
    xf = x.astype(jnp.float32)
    y = xf * lax.rsqrt(jnp.mean(xf * xf, axis=-1, keepdims=True) + EPS)
    return (y * g.astype(jnp.float32)).astype(x.dtype)

def axial_rope_tables(seq_len):
    rows = seq_len // GRID_W
    row_id = jnp.repeat(jnp.arange(rows, dtype=jnp.float32), GRID_W)
    col_id = jnp.tile(jnp.arange(GRID_W, dtype=jnp.float32), rows)
    n_pairs = HEAD_DIM // 4
    freqs = jnp.exp(-math.log(ROPE_THETA) * jnp.arange(n_pairs, dtype=jnp.float32) / n_pairs)
    ang = jnp.concatenate([row_id[:, None] * freqs[None, :], col_id[:, None] * freqs[None, :]], axis=-1)
    return jnp.cos(ang), jnp.sin(ang)

def apply_rope(x, cos, sin):
    b, s, h, d = x.shape
    xf = x.astype(jnp.float32).reshape(b, s, h, d // 2, 2)
    x0, x1 = xf[..., 0], xf[..., 1]
    c = cos[None, :, None, :]
    sn = sin[None, :, None, :]
    out = jnp.stack([x0 * c - x1 * sn, x0 * sn + x1 * c], axis=-1)
    return out.reshape(b, s, h, d).astype(x.dtype)

def gmlp_group(u, v, v_norm_g, w_s, b_s):
    b, s, _ = u.shape
    v = rms_norm(v, v_norm_g).reshape(b, s // CHUNK, CHUNK, GM_GROUPS, GM_GROUP_DIM)
    mixed = jnp.einsum('gij,bnjgc->bnigc', w_s, v) + b_s.T[None, None, :, :, None]
    return u * mixed.reshape(b, s, GM_WIDTH)

def gqa_group(q, k, v, q_norm_g, k_norm_g, cos, sin):
    b, s, _ = q.shape
    q = q.reshape(b, s, N_Q_HEADS, HEAD_DIM)
    k = k.reshape(b, s, N_KV_HEADS, HEAD_DIM)
    v = v.reshape(b, s, N_KV_HEADS, HEAD_DIM)
    q = apply_rope(rms_norm(q, q_norm_g), cos, sin) * (HEAD_DIM ** -0.5)
    k = apply_rope(rms_norm(k, k_norm_g), cos, sin)
    n_blk = s // Q_BLOCK
    q_blocks = q.reshape(b, n_blk, Q_BLOCK, N_KV_HEADS, Q_PER_KV, HEAD_DIM).transpose(1, 0, 3, 4, 2, 5)

    def attend(qb):
        sc = jnp.einsum('bkgqd,bskd->bkgqs', qb, k, preferred_element_type=jnp.float32)
        p = jax.nn.softmax(sc, axis=-1).astype(v.dtype)
        return jnp.einsum('bkgqs,bskd->bkgqd', p, v)

    o = lax.map(attend, q_blocks)
    return o.transpose(1, 0, 4, 2, 3, 5).reshape(b, s, ATT_WIDTH)

def memory_cross_attention(h, mem_n, w_q, w_kv, w_o):
    b, s, _ = h.shape
    m = mem_n.shape[1]
    q = (h @ w_q).reshape(b, s, X_HEADS, X_HEAD_DIM) * (X_HEAD_DIM ** -0.5)
    kv = (mem_n @ w_kv).reshape(b, m, 2, X_HEADS, X_HEAD_DIM)
    k, v = kv[:, :, 0], kv[:, :, 1]
    sc = jnp.einsum('bshd,bmhd->bhsm', q, k, preferred_element_type=jnp.float32)
    p = jax.nn.softmax(sc, axis=-1).astype(v.dtype)
    o = jnp.einsum('bhsm,bmhd->bshd', p, v).reshape(b, s, D_MODEL)
    return o @ w_o

def expert_choice_moe(h, w_router, w_gate, w_up, w_down):
    b, s, _ = h.shape
    cap = EC_FACTOR * s // N_EXPERTS
    logits = jnp.einsum('bsd,de->bse', h, w_router, preferred_element_type=jnp.float32)
    aff = jax.nn.softmax(logits, axis=-1)
    gates, idx = lax.top_k(aff.transpose(0, 2, 1), cap)
    b_ix = jnp.arange(b)[:, None, None]
    xs = h[b_ix, idx]
    a = jnp.einsum('becd,edf->becf', xs, w_gate)
    u = jnp.einsum('becd,edf->becf', xs, w_up)
    y = jnp.einsum('becf,efd->becd', jax.nn.silu(a) * u, w_down)
    y = y * gates[..., None].astype(y.dtype)
    return jnp.zeros_like(h).at[b_ix, idx].add(y)

def first_inputs(seed: int = 0) -> dict:
    key = jax.random.key(seed)
    ks = jax.random.split(key, 24)

    def nrm(k, shape, scale):
        return jax.random.normal(k, shape, jnp.float32) * scale

    def gain(k, shape):
        return 1.0 + 0.05 * jax.random.normal(k, shape, jnp.float32)

    L, D = DEPTH, D_MODEL
    return {
        'x': nrm(ks[0], (BATCH, SEQ, D), 1.0),
        'mem': nrm(ks[1], (BATCH, MEM_LEN, D), 1.0),
        'mix_norm_g': gain(ks[2], (L, D)),
        'w_in': nrm(ks[3], (L, D, IN_WIDTH), D ** -0.5),
        'gm_v_norm_g': gain(ks[4], (L, GM_WIDTH)),
        'gm_w_s': nrm(ks[5], (L, GM_GROUPS, CHUNK, CHUNK), CHUNK ** -0.5),
        'gm_b_s': gain(ks[6], (L, GM_GROUPS, CHUNK)),
        'q_norm_g': gain(ks[7], (L, HEAD_DIM)),
        'k_norm_g': gain(ks[8], (L, HEAD_DIM)),
        'branch_norm_g': gain(ks[9], (L, 2, GM_WIDTH)),
        'w_out': nrm(ks[10], (L, MIX_WIDTH, D), MIX_WIDTH ** -0.5),
        'xattn_norm_g': gain(ks[11], (L, D)),
        'mem_norm_g': gain(ks[12], (D,)),
        'xattn_w_q': nrm(ks[13], (L, D, D), D ** -0.5),
        'xattn_w_kv': nrm(ks[14], (L, D, 2 * D), D ** -0.5),
        'xattn_w_o': nrm(ks[15], (L, D, D), D ** -0.5),
        'ffn_norm_g': gain(ks[16], (L, D)),
        'w_router': nrm(ks[17], (L, D, N_EXPERTS), D ** -0.5),
        'w_gate': nrm(ks[18], (L, N_EXPERTS, D, EXPERT_FF), D ** -0.5),
        'w_up': nrm(ks[19], (L, N_EXPERTS, D, EXPERT_FF), D ** -0.5),
        'w_down': nrm(ks[20], (L, N_EXPERTS, EXPERT_FF, D), EXPERT_FF ** -0.5),
        'final_norm_g': gain(ks[21], (D,)),
    }

def first_block(x, mem, mix_norm_g, w_in, gm_v_norm_g, gm_w_s, gm_b_s, q_norm_g, k_norm_g,
              branch_norm_g, w_out, xattn_norm_g, mem_norm_g, xattn_w_q, xattn_w_kv, xattn_w_o,
              ffn_norm_g, w_router, w_gate, w_up, w_down, final_norm_g):
    cos, sin = axial_rope_tables(x.shape[1])
    mem_n = rms_norm(mem, mem_norm_g)
    for l in range(DEPTH):
        h = rms_norm(x, mix_norm_g[l])
        proj = h @ w_in[l]
        u, v, q, k, vv = jnp.split(proj, SPLITS, axis=-1)
        gm = gmlp_group(jax.nn.gelu(u), jax.nn.gelu(v), gm_v_norm_g[l], gm_w_s[l], gm_b_s[l])
        at = gqa_group(q, k, vv, q_norm_g[l], k_norm_g[l], cos, sin)
        merged = jnp.concatenate([rms_norm(gm, branch_norm_g[l, 0]), rms_norm(at, branch_norm_g[l, 1])], axis=-1)
        x = x + merged @ w_out[l]
        x = x + memory_cross_attention(rms_norm(x, xattn_norm_g[l]), mem_n,
                                       xattn_w_q[l], xattn_w_kv[l], xattn_w_o[l])
        x = x + expert_choice_moe(rms_norm(x, ffn_norm_g[l]), w_router[l], w_gate[l], w_up[l], w_down[l])
    return rms_norm(x, final_norm_g)


SB_HEADS = 4
DIL_HEADS = 4
HGRN_HEADS = 4
HGRN_DK = 128
HGRN_DV = 128
SB_WIDTH = SB_HEADS * HEAD_DIM
DIL_WIDTH = DIL_HEADS * HEAD_DIM
HGRN_WIDTH = HGRN_HEADS * HGRN_DV
HGRN_KDIM = HGRN_HEADS * HGRN_DK
MIX_WIDTH_2 = SB_WIDTH + DIL_WIDTH + HGRN_WIDTH
IN_SPLITS = (SB_WIDTH, SB_WIDTH, SB_WIDTH, DIL_WIDTH, DIL_WIDTH, DIL_WIDTH, HGRN_KDIM, HGRN_KDIM, HGRN_WIDTH, HGRN_WIDTH)
IN_WIDTH_2 = 3 * SB_WIDTH + 3 * DIL_WIDTH + 2 * HGRN_KDIM + 2 * HGRN_WIDTH
D_FF = 2816
QBLK = 128
HGRN_CHUNK = 64
DIL_PATTERNS = ((128, 1), (512, 4), (2048, 16))
LB_FLOOR = 1e-30
NEG_BIG = -1e30
N_MOD = 9
HALF_STEP = 0.5


def _rmsnorm(x):
    xf = x.astype(jnp.float32)
    return (xf * lax.rsqrt(jnp.mean(xf * xf, axis=-1, keepdims=True) + EPS)).astype(x.dtype)

def _split_heads(x, n_heads):
    b, s, w = x.shape
    return x.reshape(b, s, n_heads, w // n_heads).transpose(0, 2, 1, 3)

def _merge_heads(x):
    b, h, s, d = x.shape
    return x.transpose(0, 2, 1, 3).reshape(b, s, h * d)

def _rope(x):
    s, d = x.shape[2], x.shape[3]
    half = d // 2
    inv_freq = ROPE_THETA ** (-jnp.arange(half, dtype=jnp.float32) * 2.0 / d)
    ang = jnp.arange(s, dtype=jnp.float32)[:, None] * inv_freq[None, :]
    cos, sin = jnp.cos(ang), jnp.sin(ang)
    xf = x.astype(jnp.float32)
    x1, x2 = xf[..., :half], xf[..., half:]
    return jnp.concatenate([x1 * cos - x2 * sin, x2 * cos + x1 * sin], axis=-1).astype(x.dtype)

def _swiglu(h, w_gate, w_up, w_down):
    return (jax.nn.silu(h @ w_gate) * (h @ w_up)) @ w_down

def _stick_breaking(q, k, v):
    b, h, s, d = q.shape
    nb = s // QBLK
    qf = q.astype(jnp.float32) * (d ** -0.5)
    kf = k.astype(jnp.float32)
    vf = v.astype(jnp.float32)
    q_blocks = qf.reshape(b, h, nb, QBLK, d).transpose(2, 0, 1, 3, 4)
    starts = jnp.arange(nb, dtype=jnp.int32) * QBLK
    kpos = jnp.arange(s, dtype=jnp.int32)

    def block(args):
        qb, start = args
        z = jnp.einsum('bhqd,bhkd->bhqk', qb, kf)
        qpos = start + jnp.arange(QBLK, dtype=jnp.int32)
        causal = kpos[None, :] < qpos[:, None]
        log_not_beta = jnp.where(causal, jax.nn.log_sigmoid(-z), 0.0)
        tail = lax.cumsum(log_not_beta, axis=3, reverse=True) - log_not_beta
        log_w = jnp.where(causal, jax.nn.log_sigmoid(z) + tail, NEG_BIG)
        w = jnp.exp(log_w)
        return jnp.einsum('bhqk,bhkd->bhqd', w, vf)

    out = lax.map(block, (q_blocks, starts))
    return out.transpose(1, 2, 0, 3, 4).reshape(b, h, s, d)

def _dilated_partial(q, k, v, window, dilation):
    b, h, s, d = q.shape
    steps = window // dilation
    sub_len = -(-s // (QBLK * dilation)) * QBLK
    pad = sub_len * dilation - s
    nb = sub_len // QBLK

    def to_residue(x):
        x = jnp.pad(x.astype(jnp.float32), ((0, 0), (0, 0), (0, pad), (0, 0)))
        x = x.reshape(b, h, sub_len, dilation, d).transpose(0, 1, 3, 2, 4)
        return x.reshape(b, h, dilation, nb, QBLK, d)

    qr, kr, vr = to_residue(q), to_residue(k), to_residue(v)

    def with_prev_block(x):
        prev = jnp.pad(x, ((0, 0), (0, 0), (0, 0), (1, 0), (0, 0), (0, 0)))[:, :, :, :-1]
        return jnp.concatenate([prev, x], axis=4)

    kw, vw = with_prev_block(kr), with_prev_block(vr)
    scores = jnp.einsum('bhrnqd,bhrnkd->bhrnqk', qr, kw)
    a_idx = jnp.arange(QBLK)[:, None]
    k_idx = jnp.arange(2 * QBLK)[None, :]
    dist = a_idx + QBLK - k_idx
    band = (dist >= 0) & (dist <= steps)
    valid = band[None] & ((jnp.arange(nb)[:, None, None] > 0) | (k_idx[None] >= QBLK))
    scores = jnp.where(valid, scores, NEG_BIG)
    mx = jnp.max(scores, axis=-1)
    p = jnp.where(valid, jnp.exp(scores - mx[..., None]), 0.0)
    den = jnp.sum(p, axis=-1)
    num = jnp.einsum('bhrnqk,bhrnkd->bhrnqd', p, vw)

    def back(x):
        x = x.reshape((b, h, dilation, sub_len) + x.shape[5:])
        perm = (0, 1, 3, 2) + tuple(range(4, x.ndim))
        x = x.transpose(perm).reshape((b, h, sub_len * dilation) + x.shape[4:])
        return x[:, :, :s]

    return back(num), back(den), back(mx)

def _dilated_mixture(q, k, v):
    parts = [_dilated_partial(q, k, v, w, r) for (w, r) in DIL_PATTERNS]
    m_all = parts[0][2]
    for _, _, m in parts[1:]:
        m_all = jnp.maximum(m_all, m)
    num = 0.0
    den = 0.0
    for n_i, d_i, m_i in parts:
        scale = jnp.exp(m_i - m_all)
        num = num + n_i * scale[..., None]
        den = den + d_i * scale
    return num / den[..., None]

def _hgrn2_chunkwise(q, k, v, log_f):
    b, h, s, dk = q.shape
    dv = v.shape[-1]
    n = s // HGRN_CHUNK

    def chunks(x):
        return x.astype(jnp.float32).reshape(b, h, n, HGRN_CHUNK, x.shape[-1]).transpose(2, 0, 1, 3, 4)

    qc, kc, vc = chunks(q), chunks(k), chunks(v)
    g_cum = jnp.cumsum(chunks(log_f), axis=3)
    causal = jnp.tril(jnp.ones((HGRN_CHUNK, HGRN_CHUNK), dtype=bool))[:, :, None]

    def step(state, xs):
        qb, kb, vb, gb = xs
        diff = gb[:, :, :, None, :] - gb[:, :, None, :, :]
        decay = jnp.where(causal, jnp.exp(jnp.where(causal, diff, 0.0)), 0.0)
        scores = jnp.einsum('bhtd,bhsd,bhtsd->bhts', qb, kb, decay)
        o = jnp.einsum('bhts,bhsv->bhtv', scores, vb) + jnp.einsum('bhtd,bhdv->bhtv', qb * jnp.exp(gb), state)
        g_last = gb[:, :, -1, :]
        new_state = jnp.exp(g_last)[..., None] * state + jnp.einsum('bhsd,bhsv->bhdv', kb * jnp.exp(g_last[:, :, None, :] - gb), vb)
        return new_state, o

    state0 = jnp.zeros((b, h, dk, dv), jnp.float32)
    _, o = lax.scan(step, state0, (qc, kc, vc, g_cum))
    return o.transpose(1, 2, 0, 3, 4).reshape(b, h, s, dv)

def _hybrid_mixer(h, w_in, w_out, q_norm_g, k_norm_g, hgrn_norm_g, lower_bound):
    dt = h.dtype
    proj = h @ w_in
    offsets = []
    acc = 0
    for wdt in IN_SPLITS[:-1]:
        acc += wdt
        offsets.append(acc)
    qa, ka, va, qd, kd, vd, qh, fh, ih, gh = jnp.split(proj, offsets, axis=-1)

    o_a = _stick_breaking(_split_heads(qa, SB_HEADS), _split_heads(ka, SB_HEADS), _split_heads(va, SB_HEADS))

    qd = _rope(_rmsnorm(_split_heads(qd, DIL_HEADS)) * q_norm_g) * (HEAD_DIM ** -0.5)
    kd = _rope(_rmsnorm(_split_heads(kd, DIL_HEADS)) * k_norm_g)
    o_d = _dilated_mixture(qd, kd, _split_heads(vd, DIL_HEADS))

    lb = lower_bound.reshape(HGRN_HEADS, 1, HGRN_DK).astype(jnp.float32)
    z = _split_heads(fh, HGRN_HEADS).astype(jnp.float32)
    log_f = jnp.logaddexp(jnp.log(jnp.maximum(lb, LB_FLOOR)), jnp.log1p(-lb) + jax.nn.log_sigmoid(z))
    k_h = -jnp.expm1(log_f)
    q_h = jax.nn.silu(_split_heads(qh, HGRN_HEADS))
    o_h = _hgrn2_chunkwise(q_h, k_h, _split_heads(ih, HGRN_HEADS), log_f)
    o_h = _rmsnorm(o_h) * hgrn_norm_g * jax.nn.silu(_split_heads(gh, HGRN_HEADS).astype(jnp.float32))

    y = jnp.concatenate([_merge_heads(o_a).astype(dt), _merge_heads(o_d).astype(dt), _merge_heads(o_h).astype(dt)], axis=-1)
    return y @ w_out

def second_inputs(seed: int = 0) -> dict:
    key = jax.random.key(seed)
    ks = jax.random.split(key, 16)

    def nrm(k, shape, scale):
        return jax.random.normal(k, shape, jnp.float32) * scale

    return {
        "x": nrm(ks[0], (BATCH, SEQ, D_MODEL), 1.0),
        "c": nrm(ks[1], (BATCH, D_MODEL), 1.0),
        "w_mod": nrm(ks[2], (DEPTH, D_MODEL, N_MOD * D_MODEL), D_MODEL ** -0.5),
        "b_mod": nrm(ks[3], (DEPTH, N_MOD * D_MODEL), 0.02),
        "ffn1_w_gate": nrm(ks[4], (DEPTH, D_MODEL, D_FF), D_MODEL ** -0.5),
        "ffn1_w_up": nrm(ks[5], (DEPTH, D_MODEL, D_FF), D_MODEL ** -0.5),
        "ffn1_w_down": nrm(ks[6], (DEPTH, D_FF, D_MODEL), D_FF ** -0.5),
        "w_in": nrm(ks[7], (DEPTH, D_MODEL, IN_WIDTH_2), D_MODEL ** -0.5),
        "w_out": nrm(ks[8], (DEPTH, MIX_WIDTH_2, D_MODEL), MIX_WIDTH_2 ** -0.5),
        "q_norm_g": 1.0 + nrm(ks[9], (DEPTH, HEAD_DIM), 0.02),
        "k_norm_g": 1.0 + nrm(ks[10], (DEPTH, HEAD_DIM), 0.02),
        "hgrn_norm_g": 1.0 + nrm(ks[11], (DEPTH, HGRN_DV), 0.02),
        "hgrn_lb_logits": nrm(ks[12], (DEPTH, HGRN_KDIM), 0.5),
        "ffn2_w_gate": nrm(ks[13], (DEPTH, D_MODEL, D_FF), D_MODEL ** -0.5),
        "ffn2_w_up": nrm(ks[14], (DEPTH, D_MODEL, D_FF), D_MODEL ** -0.5),
        "ffn2_w_down": nrm(ks[15], (DEPTH, D_FF, D_MODEL), D_FF ** -0.5),
    }

def second_block(x, c, w_mod, b_mod, ffn1_w_gate, ffn1_w_up, ffn1_w_down, w_in, w_out, q_norm_g, k_norm_g, hgrn_norm_g, hgrn_lb_logits, ffn2_w_gate, ffn2_w_up, ffn2_w_down):
    lb_sm = jax.nn.softmax(hgrn_lb_logits.astype(jnp.float32), axis=0)
    lower_bounds = jnp.clip(jnp.cumsum(lb_sm, axis=0) - lb_sm[0:1], 0.0, 1.0 - EPS)
    for l in range(DEPTH):
        mod = jax.nn.silu(c) @ w_mod[l] + b_mod[l]
        sh1, sc1, g1, sh2, sc2, g2, sh3, sc3, g3 = jnp.split(mod[:, None, :], N_MOD, axis=-1)
        h = _rmsnorm(x) * (1.0 + sc1) + sh1
        x = x + HALF_STEP * g1 * _swiglu(h, ffn1_w_gate[l], ffn1_w_up[l], ffn1_w_down[l])
        h = _rmsnorm(x) * (1.0 + sc2) + sh2
        x = x + g2 * _hybrid_mixer(h, w_in[l], w_out[l], q_norm_g[l], k_norm_g[l], hgrn_norm_g[l], lower_bounds[l])
        h = _rmsnorm(x) * (1.0 + sc3) + sh3
        x = x + HALF_STEP * g3 * _swiglu(h, ffn2_w_gate[l], ffn2_w_up[l], ffn2_w_down[l])
    return x


def setup_inputs(seed=0):
    out = dict(first_inputs(seed))
    for name, value in second_inputs(seed + 1).items():
        if name != "x":
            out[name + "_2"] = value
    return out


def reference(
    x, mem, mix_norm_g, w_in, gm_v_norm_g, gm_w_s, gm_b_s, q_norm_g, k_norm_g, branch_norm_g,
    w_out, xattn_norm_g, mem_norm_g, xattn_w_q, xattn_w_kv, xattn_w_o, ffn_norm_g, w_router,
    w_gate, w_up, w_down, final_norm_g, c_2, w_mod_2, b_mod_2, ffn1_w_gate_2, ffn1_w_up_2,
    ffn1_w_down_2, w_in_2, w_out_2, q_norm_g_2, k_norm_g_2, hgrn_norm_g_2, hgrn_lb_logits_2,
    ffn2_w_gate_2, ffn2_w_up_2, ffn2_w_down_2,
):
    x = first_block(
        x, mem, mix_norm_g, w_in, gm_v_norm_g, gm_w_s, gm_b_s, q_norm_g, k_norm_g,
        branch_norm_g, w_out, xattn_norm_g, mem_norm_g, xattn_w_q, xattn_w_kv, xattn_w_o,
        ffn_norm_g, w_router, w_gate, w_up, w_down, final_norm_g,
    )
    return second_block(
        x, c_2, w_mod_2, b_mod_2, ffn1_w_gate_2, ffn1_w_up_2, ffn1_w_down_2, w_in_2, w_out_2,
        q_norm_g_2, k_norm_g_2, hgrn_norm_g_2, hgrn_lb_logits_2, ffn2_w_gate_2, ffn2_w_up_2,
        ffn2_w_down_2,
    )


_drawn_inputs = setup_inputs


def setup_inputs(seed=0):
    import zlib

    import numpy as np

    out = dict(_drawn_inputs(seed))
    spreads = {}
    factors = {'xattn_norm_g': 5.376,
     'mem_norm_g': 3.352,
     'q_norm_g_2': 8.0,
     'k_norm_g_2': 8.0,
     'hgrn_norm_g_2': 6.237,
     'hgrn_lb_logits_2': 8.0}
    for name, (base, spread) in spreads.items():
        noise = np.random.default_rng([zlib.crc32(name.encode()), seed]).standard_normal(out[name].shape)
        drawn = base * np.exp(spread * noise) if base else spread * noise
        out[name] = jnp.asarray(drawn.astype(out[name].dtype))
    for name, factor in factors.items():
        out[name] = (out[name] * factor).astype(out[name].dtype)
    return out
```

```python
from contextlib import ExitStack

import numpy as np

import concourse.bass as bass
from concourse import mybir

F32 = mybir.dt.float32
U32 = mybir.dt.uint32
ALU = mybir.AluOpType
ACT = mybir.ActivationFunctionType
AX = mybir.AxisListType

P = 128
D = 1024
KT = D // P
S = 256
HALVES = S // P
LAYERS = 2
EPS = 1e-6
GM = 512
HD = 64
QH, KVH = 8, 2
XH, XD = 4, 256
NE, FF = 16, 1024
CAP = 2 * S // NE
GROUP = P // CAP
GROUPS = NE // GROUP
DFF = 2816
NMOD = 9
HH, HK = 4, 128
LB_FLOOR = 1e-30
NEG = -1e30
SLOTS = 4
CHUNK = 512
FFC = [min(CHUNK, DFF - c) for c in range(0, DFF, CHUNK)]
FKT = DFF // P
DOWN = [(k, min(KT, FKT - k)) for k in range(0, FKT, KT)]
LEVELS = 8


CONSTS = {}


def constant_table():
    parts, at = [], 0

    def put(name, a):
        nonlocal at
        a = np.asarray(a, np.float32).reshape(P, -1)
        CONSTS[name] = (at, a.shape[1])
        parts.append(a)
        at += a.shape[1]

    i = np.arange(P)
    put("ident", np.eye(P))
    put("ones", np.ones((P, P)))
    put("iota", np.tile(np.arange(CAP), (P, NE)))
    put("tri_ge", i[:, None] >= i[None, :])
    put("key_before_query", i[:, None] < i[None, :])
    pos = np.arange(S)
    pairs = HD // 4
    freqs = np.exp(np.float32(-np.log(10000.0)) * np.arange(pairs, dtype=np.float32) / pairs).astype(np.float32)
    ang = np.concatenate([(pos // 64).astype(np.float32)[:, None] * freqs, (pos % 64).astype(np.float32)[:, None] * freqs], -1)
    inv = (np.float32(10000.0) ** (-np.arange(HD // 2, dtype=np.float32) * np.float32(2.0) / HD)).astype(np.float32)
    ang2 = pos.astype(np.float32)[:, None] * inv[None, :]
    for name, a in (("cos1", np.cos(ang)), ("sin1", np.sin(ang)), ("cos2", np.cos(ang2)), ("sin2", np.sin(ang2))):
        put(name, a.reshape(HALVES, P, HD // 2).transpose(1, 0, 2))
    dist = pos[:, None] - pos[None, :]
    count = ((dist >= 0) & (dist <= 128)) * 1.0 + ((dist >= 0) & (dist % 4 == 0)) + ((dist >= 0) & (dist % 16 == 0))
    put("dil_count", count.reshape(HALVES, P, S).transpose(1, 0, 2))
    put("dil_neg", np.where(count > 0, 0.0, NEG).reshape(HALVES, P, S).transpose(1, 0, 2))
    mats, masks = [], []
    j, t = i[:, None], i[None, :]
    for b in (64, 32, 16, 8, 4, 2, 1):
        odd = (t // b) % 2 == 1
        start = (t // b) * b
        mats.append(np.where(odd, (j >= start) & (j <= t), (j > t) & (j < start + b)))
        masks.append((i[None, :] // b % 2 == 1) & (i[:, None] // b == i[None, :] // b - 1))
    mats += [j > t, j <= t]
    masks.append(np.eye(P))
    put("decay_sum", np.stack([m.astype(np.float32) for m in mats], 1))
    put("level_mask", np.stack([np.asarray(m, np.float32) for m in masks], 1))
    return np.ascontiguousarray(np.concatenate(parts, 1))


class Order:

    def __init__(self, head, group, tail, step0, pair0, tile0):
        self.parts, self.step0, self.pair0, self.tile0 = [head, group, tail], step0, pair0, tile0
        self.step, self.result, self.tile = {}, {}, {}
        steps, uses, tiles, n = 0, [0] * 4, 0, 0
        self.tiles = []
        self.size, self.use_size = [], []
        for part, items in enumerate(self.parts):
            s0, u0 = steps, list(uses)
            for name, new, tile in items:
                self.step[name] = (part, steps)
                if new:
                    self.result[name] = (part, n % 4, uses[n % 4])
                    uses[n % 4] += 1
                    n += 1
                if tile:
                    self.tile[name] = (part, tiles)
                    self.tiles.append((name, part, steps))
                    tiles += 1
                steps += 1
            self.size.append(steps - s0)
            self.use_size.append([a - b for a, b in zip(uses, u0)])
            if part == 1 and items:
                assert len({tuple(self.use_size[1])}) == 1 and n % 4 == 0, "a group uses every pair alike"
                self.group_steps, self.group_uses = self.size[1], list(self.use_size[1])
                steps += (GROUPS - 1) * self.size[1]
                uses = [a + (GROUPS - 1) * b for a, b in zip(uses, self.group_uses)]
                gt = [x for x in self.tiles if x[1] == 1]
                self.group_tiles = len(gt)
                self.head_tiles = tiles - self.group_tiles
                tiles += (GROUPS - 1) * self.group_tiles
        self.steps, self.uses = steps, uses
        self.layer_tiles = tiles + -tiles % SLOTS
        n_head = self.head_tiles if self.parts[1] else tiles
        used = list(range(tiles))
        self.slot_uses = [sum(p % SLOTS == s for p in used) for s in range(SLOTS)]
        self.position = {t[0]: p for p, t in enumerate(self.tiles)}
        self.n_tiles, self.n_head = tiles, n_head

    def done(self, l, name, g=0):
        part, i = self.step[name]
        return self.step0 + l * self.steps + i + 1 + (g * self.group_steps if part == 1 else 0)

    def slot(self, name):
        return self.position[name] % SLOTS

    def landings(self, l, name, g=0):
        p = self.position[name]
        k = sum(q % SLOTS == p % SLOTS for q in range(p))
        per_group = self.group_tiles // SLOTS if self.parts[1] else 0
        return 16 * (self.tile0[p % SLOTS] + l * self.slot_uses[p % SLOTS] + k + 1 + g * per_group)

    def slot_free(self, l, name, g=0):
        p = self.position[name]
        part = self.tiles[p][1]
        if part == 1 and p - SLOTS < self.n_head:
            return self.done(l, self.tiles[p - SLOTS + self.group_tiles][0], g - 1)
        if p >= SLOTS:
            return self.done(l, self.tiles[p - SLOTS][0], g)
        last = max(q for q in range(self.n_tiles) if q % SLOTS == p % SLOTS)
        if self.parts[1]:
            return self.done(l - 1, self.tiles[last - (GROUPS - 1) * self.group_tiles][0], GROUPS - 1)
        return self.done(l - 1, self.tiles[last][0])

    def pair(self, name):
        return self.result[name][1]

    def free(self, l, name, g=0):
        part, q, i = self.result[name]
        return 2 + 2 * (self.pair0[q] + l * self.uses[q] + i + (g * self.group_uses[q] if part == 1 else 0))


def head_one():
    new = [("T0a", 1, 0), ("T0b", 1, 0)]
    new += [(n, 1, 1) for n in ("in_u", "in_v", "in_q", "in_kv", "xk0", "xk1", "xv0", "xv1")]
    new += [(n, 1, 0) for n in ("ws", "mix", "qT", "kT")]
    new += [(n, 1, 0) for n in ("S0", "S1", "P0", "V0", "S2", "P1", "V1", "S3", "P2", "V2", "P3", "V3")]
    new += [("Ma", 1, 0), ("Mb", 1, 0), ("out0", 1, 1), ("out1", 1, 1), ("T1a", 1, 0), ("T1b", 1, 0)]
    new += [("xq0", 1, 1), ("xq1", 1, 1), ("XS0", 1, 0), ("XS1", 1, 0), ("XP0", 1, 0), ("XP1", 1, 0)]
    new += [("XOa", 1, 0), ("XOb", 1, 0), ("xo0", 1, 1), ("xo1", 1, 1), ("T2a", 1, 0), ("T2b", 1, 0)]
    new += [("route", 1, 0), ("affT", 1, 0), ("posT", 1, 0), ("gateT", 1, 0)]
    return new


SPARE = 6
N_SMALL = 18


def group_one():
    items = [("gather", 1, 0)]
    for k in range(KT):
        items += [(f"g{k}", k == 0, 1), (f"u{k}", k == 0, 1)]
    items += [("midT", 1, 0)]
    items += [(f"d{k}", k == 0, 1) for k in range(KT)]
    items += [(f"spare{i}", i < 3, 0) for i in range(SPARE)]
    return items


def ffn_items(f, mods):
    mods, items = list(mods), []
    for c in range(len(FFC)):
        items += [(f"{f}g{c}", 1, 1), (f"{f}u{c}", 1, 1)]
        for m in [mods.pop(0)] if mods else []:
            items += mod_items(m)
    for m in mods:
        items += mod_items(m)
    for n in range(D // CHUNK):
        items += [(f"{f}d{n}_{i}", i == 0, 1) for i in range(len(DOWN))]
    return items


def mod_items(m):
    return [(f"m{m}_0", 1, 1), (f"m{m}_1", 0, 1), (f"mb{m}", 1, 0)]


def head_two():
    items = mod_items(0) + mod_items(1)
    items += [("T0a", 1, 0), ("T0b", 1, 0)] + ffn_items("A", range(2, NMOD))
    items += [("T1a", 1, 0), ("T1b", 1, 0)]
    items += [(n, 1, 1) for n in ("in_qka", "in_vaqd", "in_kdvd", "in_qh", "in_fh", "in_ih", "in_gh")]
    items += [(n, 1, 0) for n in ("SZ0", "SZ1", "SC0", "SC1", "SV", "DT", "DS0", "DS1", "DP0", "DV0", "DP1", "DV1", "HL")]
    items += [("HE0", 1, 0), ("HE1", 1, 0)]
    for i in range(LEVELS):
        items += [(f"HS{i}", 1, 0)] + ([(f"HE{i + 2}", 1, 0)] if i + 2 < LEVELS else [])
    items += [("HD", 1, 0), ("HO", 1, 0), ("Ya", 1, 0), ("Yb", 1, 0), ("out0", 1, 1), ("out1", 1, 1)]
    items += [("T2a", 1, 0), ("T2b", 1, 0)] + ffn_items("B", [])
    return items


def place(j):
    return 2 * (j % 2) + j // 2


STEP0 = 512


def two_blocks(nc: bass.Bass, w, out):
    ones_order = Order([("T0a", 1, 0), ("T0b", 1, 0)], [], [], STEP0, [0] * 4, [0] * SLOTS)
    pre_steps = ones_order.steps
    one = Order(head_one(), group_one(), [("C0", 1, 0), ("C1", 1, 0)], STEP0 + pre_steps,
                [ones_order.uses[q] for q in range(4)], [0] * SLOTS)
    two = Order(head_two(), [], [], one.step0 + LAYERS * one.steps,
                [one.pair0[q] + LAYERS * one.uses[q] for q in range(4)], [LAYERS * n for n in one.slot_uses])

    with ExitStack() as ctx:
        def sb(name, shape):
            return ctx.enter_context(nc.sbuf_tensor(name, shape, F32))

        def sem(name):
            return ctx.enter_context(nc.semaphore(name))

        n_const = sum(n for _, n in CONSTS.values())
        consts = sb("consts", [P, n_const])

        def const(name, *dims):
            a, n = CONSTS[name]
            ap = consts[:, a:a + n]
            if len(dims) == 2:
                ap = ap.rearrange("p (a b) -> p a b", a=dims[0])
            return ap

        ident, ones = const("ident"), const("ones")
        ring = sb("ring", [P, SLOTS, KT * CHUNK])
        x = sb("x", [P, HALVES, D])
        xn = sb("xn", [P, HALVES, D])
        hT = sb("hT", [P, KT, S])
        work = sb("work", [P, 15104])
        g_mix, g_xa, g_ffn, g_br = (sb(n, [P, LAYERS * KT]) for n in ("g_mix", "g_xa", "g_ffn", "g_br"))
        g_mem = sb("g_mem", [P, KT])
        g_final = sb("g_final", [P, D])
        g_v = sb("g_v", [P, LAYERS, GM])
        g_q1, g_k1, g_q2, g_k2 = (sb(n, [P, LAYERS, HD]) for n in ("g_q1", "g_k1", "g_q2", "g_k2"))
        g_h = sb("g_h", [P, LAYERS, HK])
        b_s = sb("b_s", [P, LAYERS * 4])
        w_s = sb("w_s", [P, LAYERS, 4 * P])
        b_mod = sb("b_mod", [2 * NMOD, LAYERS, CHUNK])
        w_s_now = sb("w_s_now", [P, 4 * P])
        router = sb("router", [P, LAYERS * KT, NE])
        lbl = sb("lbl", [P, LAYERS * HH])
        lb_ln, lb_ln1m, lb_1m = (sb(n, [P, LAYERS * HH]) for n in ("lb_ln", "lb_ln1m", "lb_1m"))
        lbt, quarter = sb("lbt", [P, 4, HH]), sb("quarter", [P, LAYERS * HH])
        cT = sb("cT", [P, KT])
        c32 = sb("c32", [P, KT, 32])
        bm_now = sb("bm_now", [2 * NMOD, CHUNK])
        part = sb("part", [P, 2, CHUNK])
        mcol = sb("mcol", [P, NMOD, KT])
        gate_b = sb("gate_b", [P, 3, D])
        eps = sb("eps", [P, 2])
        ss, ms, rstd = sb("ss", [P, 2]), sb("ms", [P, 2]), sb("rstd", [P, 2])
        mhalf = sb("mhalf", [P, 32])
        var, inv = sb("var", [P, 32]), sb("inv", [P, 32])
        smax, ssum, rsum = sb("smax", [P, 4, 4]), sb("ssum", [P, 4, 4]), sb("rsum", [P, 4, 4])
        nmax = sb("nmax", [P, 4, 4])
        small = sb("small", [P, 64])

        def cut(at, *dims):
            n = int(np.prod(dims))
            ap = work[:, at:at + n]
            if len(dims) == 2:
                return ap.rearrange("p (a b) -> p a b", a=dims[0])
            if len(dims) == 3:
                return ap.rearrange("p (a b c) -> p a b c", a=dims[0], b=dims[1])
            return ap

        memT = gate_b[:, 0:2, :].rearrange("p a b -> p (a b)").rearrange("p (k s) -> p k s", k=KT)
        ug, vg = cut(0, HALVES, GM), cut(1024, HALVES, GM)
        qk, vv = cut(2048, HALVES, 640), cut(3328, HALVES, KVH * HD)
        rq, kdup = cut(3584, HALVES, 640), cut(4864, HALVES, 256)
        t1, t2 = cut(5376, HALVES, 320), cut(6016, HALVES, 320)
        qkT = cut(5376, 6, S)
        pr, pTr = cut(6912, 2, 1024), cut(8960, 2, 1024)
        sq1 = cut(6912, 1280)
        kxT, vx = cut(11008, KT, S), cut(13056, HALVES, D)
        qxT, px, pxT, oxT = cut(0, KT, S), cut(2048, HALVES, 1024), cut(4096, XH, 2, S), cut(6912, KT, S)
        sel, selg = cut(0, HALVES, NE * CAP), cut(1024, HALVES, NE * CAP)
        gateT = cut(2048, GROUPS, HALVES, P)
        aw = [work[0:NE, 3072 + 256 * i:3328 + 256 * i] for i in range(6)]
        xsT, act_mid, mid, midT = cut(4608, KT, P), cut(5632, FF), cut(6656, FF), cut(7680, KT, P)
        ys = cut(8704, GROUPS, D)
        aff, posn = cut(12800, HALVES, NE), cut(12832, HALVES, NE)
        hmT, sg, tmp = cut(0, FKT, S), cut(5632, 2, 1024), cut(7680, HALVES, CHUNK)
        qkaT, vq, kv = cut(0, 4, S), cut(1024, HALVES, 512), cut(2048, HALVES, 512)
        qhT, lfT, khT = cut(3072, HH, S), cut(4096, HH, S), cut(5120, HH, S)
        ih, gh = cut(6144, HALVES, 512), cut(7168, HALVES, 512)
        fz, fa, fm, fs, fx, fd = (cut(8192 + 1024 * i, 1024) for i in range(6))
        z0, z1, l0, l1 = cut(8192, 4, S), cut(9216, 4, P), cut(9728, 4, S), cut(10752, 4, P)
        sp0, sp1 = cut(11264, 4, S), cut(12288, 4, P)
        dq, dt1, dt2, dr = cut(8192, HALVES, 512), cut(9216, HALVES, 256), cut(9728, HALVES, 256), cut(10240, HALVES, 512)
        dsq = cut(9216, 1024)
        dT, dp, dpT = cut(11264, 4, S), cut(12288, 2, 1024), cut(8192, 2, 1024)
        lfn, he, hq = cut(10240, HALVES, 512), cut(8192, 2, 1024), cut(11264, 2, 1024)
        at_, at2 = cut(13312, 8, P), cut(14336, HH, P)
        ho, hsq = cut(8192, HALVES, 512), cut(9216, 1024)

        ps = [ctx.enter_context(nc.psum_tensor(f"ps{q}", [P, 2, CHUNK], F32)) for q in range(4)]

        load_c, load_x, load_m, load_p, stored = (sem(n) for n in ("load_c", "load_x", "load_m", "load_p", "stored"))
        landed = [sem(f"landed{i}") for i in range(SLOTS)]
        pe_step = sem("pe_step")
        pair_free = [sem(f"pair_free{q}") for q in range(4)]
        ss_ready, rstd_ready, xn_ready, x_ready = (sem(n) for n in ("ss_ready", "rstd_ready", "xn_ready", "x_ready"))
        var_ready, inv_ready, setup = sem("var_ready"), sem("inv_ready"), sem("setup")
        names = """ws_now v_ready rope_ready smax_ready merged xmax_ready xpn_ready rmax_ready aff_ready
        pos_ready sel_ready bm_ready c_ready c_silu lb_exp lb_sum lb_floor lb_root lb_log fab_ready flog fd_ready fl2 kh_ready
        sp_in st_log sp_ready w_arg w_exp dexp w_ready drope_ready dmax_ready dp_ready lf_ready hq_ready
        y_dve f_kh""".split()
        sm = {n: sem(n) for n in names}
        begin = ones_order

        block = ctx.enter_context(nc.Block())

        def read_out(eng, order, l, *names, g=0):
            for name in names:
                eng.wait_ge(pair_free[order.pair(name)], order.free(l, name, g) + 2)

        def finished(eng, order, l, name, g=0):
            eng.wait_ge(pe_step, order.done(l, name, g))

        @block.sync
        def _(sp):
            sp.dma_start(consts[:, :], w["consts"]).then_inc(load_c, 16)
            sp.dma_start(xn[:, :, :], w["mem"][0].rearrange("(h p) d -> p h d", p=P)).then_inc(load_m, 16)
            sp.dma_start(x[:, :, :], w["x"][0].rearrange("(h p) d -> p h d", p=P)).then_inc(load_x, 16)

            def tile(order, l, name, src, g=0):
                slot, cols = order.slot(name), src.shape[2]
                sp.wait_ge(pe_step, order.slot_free(l, name, g))
                sp.dma_start(ring[:, slot, 0:src.shape[1] * cols].rearrange("p (k n) -> p k n", n=cols),
                             src).then_inc(landed[slot], 16)

            def columns(name, l, c0, n, k0=0, nk=KT):
                return w[name][bass.ds(l, 1), k0 * P:(k0 + nk) * P, c0:c0 + n].rearrange("l (k p) n -> p (l k) n", p=P)

            with sp.Fori(0, LAYERS) as l:
                for i, (n, width) in enumerate((("in_u", 512), ("in_v", 512), ("in_q", 512), ("in_kv", 256))):
                    tile(one, l, n, columns("w_in", l, 512 * i, width))
                for i, n in enumerate(("xk0", "xk1", "xv0", "xv1")):
                    tile(one, l, n, columns("xattn_w_kv", l, 512 * i, CHUNK))
                for src, pre in (("w_out", "out"), ("xattn_w_q", "xq"), ("xattn_w_o", "xo")):
                    for i in range(2):
                        tile(one, l, f"{pre}{i}", columns(src, l, 512 * i, CHUNK))
                with sp.Fori(0, GROUPS) as g:
                    def experts(name, k):
                        return w[name][bass.ds(l, 1), bass.ds(g * GROUP, GROUP), k * P:(k + 1) * P, :].rearrange(
                            "l e p n -> p (l e) n")
                    for k in range(KT):
                        tile(one, l, f"g{k}", experts("w_gate", k), g)
                        tile(one, l, f"u{k}", experts("w_up", k), g)
                    for k in range(KT):
                        tile(one, l, f"d{k}", experts("w_down", k), g)

            def mod_tiles(l, m):
                for i in range(2):
                    tile(two, l, f"m{m}_{i}", columns("w_mod_2", l, m * D + i * CHUNK, CHUNK))

            def ffn_tiles(l, f, name, mods):
                mods = list(mods)
                for c, n in enumerate(FFC):
                    tile(two, l, f"{f}g{c}", columns(name + "_w_gate_2", l, c * CHUNK, n))
                    tile(two, l, f"{f}u{c}", columns(name + "_w_up_2", l, c * CHUNK, n))
                    if mods:
                        mod_tiles(l, mods.pop(0))
                for m in mods:
                    mod_tiles(l, m)
                for n in range(D // CHUNK):
                    for i, (k0, nk) in enumerate(DOWN):
                        tile(two, l, f"{f}d{n}_{i}", columns(name + "_w_down_2", l, n * CHUNK, CHUNK, k0, nk))

            with sp.Fori(0, LAYERS) as l:
                mod_tiles(l, 0)
                mod_tiles(l, 1)
                ffn_tiles(l, "A", "ffn1", range(2, NMOD))
                for i, n in enumerate(("in_qka", "in_vaqd", "in_kdvd", "in_qh", "in_fh", "in_ih", "in_gh")):
                    tile(two, l, n, columns("w_in_2", l, 512 * i, CHUNK))
                for i in range(2):
                    tile(two, l, f"out{i}", columns("w_out_2", l, 512 * i, CHUNK))
                ffn_tiles(l, "B", "ffn2", [])
            sp.wait_ge(x_ready, 8 + 3 * LAYERS)
            sp.dma_start(out[0].rearrange("(h p) d -> p h d", p=P), x[:, :, :]).then_inc(stored, 16)
            sp.wait_ge(stored, 16)

        @block.tensor
        def _(pe):
            pe.sem_inc(pe_step, STEP0)
            for q in range(4):
                pe.sem_inc(pair_free[q], 2)

            def result(order, l, name, g=0):
                pe.wait_ge(pair_free[order.pair(name)], order.free(l, name, g))
                return ps[order.pair(name)]

            def weights(order, l, name, cols=CHUNK, g=0, nk=KT):
                pe.wait_ge(landed[order.slot(name)], order.landings(l, name, g))
                return ring[:, order.slot(name), 0:nk * cols].rearrange("p (k n) -> p k n", n=cols)

            def step(ins, n=1):
                ins.then_inc(pe_step, n)

            def transposes(order, l, name, pieces, width=P, g=0):
                ps_ = result(order, l, name, g)
                for src, m, bank, col in pieces:
                    rows = src.shape[0]
                    last = pe.transpose(ps_[0:m, bank, col:col + rows], src, ident[0:rows, 0:rows])
                step(last)

            def rows_to_hT(order, l, ab, src=xn):
                for i in range(2):
                    transposes(order, l, ab[i], [
                        (src[:, h, (4 * i + 2 * b + kk) * P:(4 * i + 2 * b + kk + 1) * P], P, b, kk * S + h * P)
                        for b in range(2) for kk in range(2) for h in range(HALVES)])

            def by_token(order, l, name, aT, cols=CHUNK, first=True):
                w_, ps_ = weights(order, l, name, cols), result(order, l, name)
                for h in range(HALVES):
                    for k in range(KT):
                        last = pe.matmul(ps_[:, h, 0:cols], aT[:, k, h * P:(h + 1) * P], w_[:, k, :],
                                         start=(k == 0), stop=(k == KT - 1))
                step(last)

            def by_feature(order, l, name, aT, cols=CHUNK):
                w_, ps_ = weights(order, l, name, cols), result(order, l, name)
                for b in range(cols // P):
                    for k in range(KT):
                        last = pe.matmul(ps_[:, b // 2, (b % 2) * S:(b % 2 + 1) * S], w_[:, k, b * P:(b + 1) * P],
                                         aT[:, k, :], start=(k == 0), stop=(k == KT - 1))
                step(last)

            pe.wait_ge(load_c, 16)
            pe.wait_ge(xn_ready, 2)
            rows_to_hT(begin, 0, ("T0a", "T0b"))
            read_out(pe, begin, 0, "T0a", "T0b")

            with pe.Fori(0, LAYERS) as l:
                def norm_T(j, ab):
                    pe.wait_ge(xn_ready, 2 * (1 + 3 * l + j) + 2)
                    rows_to_hT(one, l, ab)
                    read_out(pe, one, l, *ab)

                norm_T(0, ("T0a", "T0b"))
                for n, cols in (("in_u", 512), ("in_v", 512), ("in_q", 512), ("in_kv", 256)):
                    by_token(one, l, n, hT, cols)
                for n in ("xk0", "xk1"):
                    by_feature(one, l, n, memT)
                for n in ("xv0", "xv1"):
                    by_token(one, l, n, memT)
                pe.wait_ge(sm["ws_now"], l + 1)
                transposes(one, l, "ws", [(w_s_now[:, i * P:(i + 1) * P], P, 0, i * P) for i in range(4)])
                pe.wait_ge(sm["v_ready"], l + 1)
                read_out(pe, one, l, "ws")
                ps_ = result(one, l, "mix")
                for h in range(HALVES):
                    for i in range(4):
                        last = pe.matmul(ps_[:, h, i * P:(i + 1) * P], w_s_now[:, i * P:(i + 1) * P],
                                         vg[:, h, i * P:(i + 1) * P], start=True, stop=True)
                step(last)
                pe.wait_ge(sm["rope_ready"], l + 1)
                transposes(one, l, "qT", [(rq[:, h, b * P:(b + 1) * P], P, b // 2, (b % 2) * S + h * P)
                                          for b in range(4) for h in range(HALVES)])
                transposes(one, l, "kT", [(kdup[:, h, b * P:(b + 1) * P], P, 0, b * S + h * P)
                                          for b in range(KVH) for h in range(HALVES)])

                def att_scores(b):
                    h, hg = b // 2, b % 2
                    if b == 0:
                        read_out(pe, one, l, "qT", "kT")
                    ps_ = result(one, l, f"S{b}")
                    for j in range(4):
                        hd, at = 4 * hg + j, HD * (j % 2)
                        last = pe.matmul(ps_[:, j % 2, (j // 2) * S:(j // 2 + 1) * S],
                                         qkT[at:at + HD, hd // 2, h * P:(h + 1) * P],
                                         qkT[at:at + HD, 4 + hd // 4, :], start=True, stop=True)
                    step(last)

                def att_turn(b):
                    read_out(pe, one, l, f"S{b}")
                    transposes(one, l, f"P{b}", [(pr[:, b % 2, j * S + t * P:j * S + (t + 1) * P], P, j // 2, (j % 2) * S + t * P)
                                                 for j in range(4) for t in range(2)])

                def att_values(b):
                    hg = b % 2
                    read_out(pe, one, l, f"P{b}", *(["in_kv"] if b == 0 else []))
                    ps_ = result(one, l, f"V{b}")
                    for j in range(4):
                        for t in range(2):
                            last = pe.matmul(ps_[:, 0, j * HD:(j + 1) * HD],
                                             pTr[:, b % 2, j * S + t * P:j * S + (t + 1) * P],
                                             vv[:, t, hg * HD:(hg + 1) * HD], start=(t == 0), stop=(t == 1))
                    step(last)

                att_scores(0)
                att_scores(1)
                att_turn(0)
                att_values(0)
                att_scores(2)
                att_turn(1)
                att_values(1)
                att_scores(3)
                att_turn(2)
                att_values(2)
                att_turn(3)
                att_values(3)
                pe.wait_ge(sm["merged"], l + 1)
                rows_to_hT(one, l, ("Ma", "Mb"))
                read_out(pe, one, l, "Ma", "Mb")
                for n in ("out0", "out1"):
                    by_token(one, l, n, hT)
                norm_T(1, ("T1a", "T1b"))
                for n in ("xq0", "xq1"):
                    by_feature(one, l, n, hT)
                read_out(pe, one, l, "xq0", "xq1", "xk0", "xk1")
                for h in range(HALVES):
                    ps_ = result(one, l, f"XS{h}")
                    for j in range(XH):
                        for t in range(2):
                            last = pe.matmul(ps_[:, j // 2, (j % 2) * S:(j % 2 + 1) * S],
                                             qxT[:, 2 * j + t, h * P:(h + 1) * P], kxT[:, 2 * j + t, :],
                                             start=(t == 0), stop=(t == 1))
                    step(last)
                for h in range(HALVES):
                    pe.wait_ge(sm["xpn_ready"], 2 * l + h + 1)
                    transposes(one, l, f"XP{h}", [(px[:, h, j * S + t * P:j * S + (t + 1) * P], P, j // 2, (j % 2) * S + t * P)
                                                  for j in range(XH) for t in range(2)])
                read_out(pe, one, l, "XP0", "XP1", "xv0", "xv1")
                for a in range(2):
                    ps_ = result(one, l, ("XOa", "XOb")[a])
                    for b in range(4):
                        d = 4 * a + b
                        for t in range(2):
                            last = pe.matmul(ps_[:, b // 2, (b % 2) * S:(b % 2 + 1) * S],
                                             vx[:, t, d * P:(d + 1) * P], pxT[:, d // 2, t, :],
                                             start=(t == 0), stop=(t == 1))
                    step(last)
                read_out(pe, one, l, "XOa", "XOb")
                for n in ("xo0", "xo1"):
                    by_token(one, l, n, oxT)
                norm_T(2, ("T2a", "T2b"))
                ps_ = result(one, l, "route")
                for h in range(HALVES):
                    for k in range(KT):
                        last = pe.matmul(ps_[:, 0, h * NE:(h + 1) * NE], hT[:, k, h * P:(h + 1) * P],
                                         router[:, bass.ds(l * KT + k, 1), :].rearrange("p a e -> p (a e)"),
                                         start=(k == 0), stop=(k == KT - 1))
                step(last)
                pe.wait_ge(sm["aff_ready"], l + 1)
                transposes(one, l, "affT", [(aff[:, h, :], NE, 0, h * P) for h in range(HALVES)])
                pe.wait_ge(sm["pos_ready"], l + 1)
                ps_ = result(one, l, "posT")
                for h in range(HALVES):
                    last = pe.matmul(ps_[:, 0, h * NE:(h + 1) * NE], aw[5][:, h * P:(h + 1) * P], ident[0:NE, 0:NE],
                                     start=True, stop=True)
                step(last)
                pe.wait_ge(sm["sel_ready"], l + 1)
                transposes(one, l, "gateT", [(selg[:, h, g * P:(g + 1) * P], P, g // 2, (g % 2) * S + h * P)
                                             for g in range(GROUPS) for h in range(HALVES)])
                with pe.Fori(0, GROUPS) as g:
                    ps_ = result(one, l, "gather", g)
                    for k in range(KT):
                        for h in range(HALVES):
                            last = pe.matmul(ps_[:, k // 4, (k % 4) * P:(k % 4 + 1) * P], xn[:, h, k * P:(k + 1) * P],
                                             sel[:, h, bass.ds(g * P, P)], start=(h == 0), stop=(h == 1))
                    step(last)
                    read_out(pe, one, l, "gather", g=g)

                    def experts(name, k, ps_, lhs, more=1):
                        w_ = weights(one, l, name, FF, g, GROUP)
                        for n in range(FF // CHUNK):
                            for e in range(GROUP):
                                last = pe.matmul(ps_[e * CAP:(e + 1) * CAP, n, :], lhs[:, k, e * CAP:(e + 1) * CAP],
                                                 w_[:, e, n * CHUNK:(n + 1) * CHUNK],
                                                 start=(k == 0), stop=(k == KT - 1))
                        step(last, more)

                    pg, pu = result(one, l, "g0", g), result(one, l, "u0", g)
                    for k in range(KT):
                        experts(f"g{k}", k, pg, xsT)
                        experts(f"u{k}", k, pu, xsT)
                    read_out(pe, one, l, "u0", g=g)
                    transposes(one, l, "midT", [(mid[:, k * P:(k + 1) * P], P, k // 4, (k % 4) * P) for k in range(KT)], g=g)
                    read_out(pe, one, l, "midT", g=g)
                    pd = result(one, l, "d0", g)
                    for k in range(KT):
                        experts(f"d{k}", k, pd, midT, 1 if k < KT - 1 else 1 + SPARE)
                    for i in range(3):
                        pe.sem_inc(pair_free[one.pair(f"spare{i}")], 2)
                read_out(pe, one, l, "gateT")
                read_out(pe, one, l, "d0", g=GROUPS - 1)
                for h in range(HALVES):
                    ps_ = result(one, l, f"C{h}")
                    for n in range(D // CHUNK):
                        for g in range(GROUPS):
                            last = pe.matmul(ps_[:, n, :], gateT[:, g, h, :], ys[:, g, n * CHUNK:(n + 1) * CHUNK],
                                             start=(g == 0), stop=(g == GROUPS - 1))
                    step(last)

            pe.wait_ge(sm["c_ready"], 1)
            with pe.Fori(0, LAYERS) as l:
                def norm_T2(j, ab):
                    pe.wait_ge(xn_ready, 2 * (8 + 3 * l + j) + 2)
                    rows_to_hT(two, l, ab)
                    read_out(pe, two, l, *ab)

                def mod(m):
                    for i in range(2):
                        w_ = weights(two, l, f"m{m}_{i}")
                        ps_ = result(two, l, f"m{m}_0") if i == 0 else ps_
                        for r in range(2):
                            for j in range(4):
                                k = 4 * r + j
                                last = pe.matmul(ps_[32 * j:32 * j + 32, i, :], c32[:, k, :], w_[:, k, :],
                                                 start=(r == 0), stop=(r == 1))
                        step(last)

                def mod_sum(m):
                    read_out(pe, two, l, f"m{m}_0")
                    if m == 0:
                        pe.wait_ge(sm["bm_ready"], l + 1)
                    ps_ = result(two, l, f"mb{m}")
                    for i in range(2):
                        u = 2 * m + i
                        if m % 3 == 2:
                            pe.matmul(ps_[:, i, :], ones, part[:, i, :], start=True, stop=False)
                            last = pe.matmul(ps_[:, i, :], ident[0:2 * NMOD, u:u + 1].broadcast_to([2 * NMOD, P]),
                                             bm_now[:, :], start=False, stop=True)
                        else:
                            for b in range(4):
                                c = 4 * i + b
                                pe.matmul(ps_[:, 0, c:c + 1], part[:, i, b * P:(b + 1) * P], ones[:, 0:1],
                                          start=True, stop=False)
                                last = pe.matmul(ps_[:, 0, c:c + 1], bm_now[:, b * P:(b + 1) * P],
                                                 ident[0:2 * NMOD, u:u + 1], start=False, stop=True)
                    step(last)

                def ffn(f, j, mods):
                    mods = list(mods)
                    for c, n in enumerate(FFC):
                        by_feature(two, l, f"{f}g{c}", hT, n)
                        by_feature(two, l, f"{f}u{c}", hT, n)
                        if mods:
                            m = mods.pop(0)
                            mod(m)
                            mod_sum(m)
                    for m in mods:
                        mod(m)
                        mod_sum(m)
                    for n in range(D // CHUNK):
                        for i, (k0, nk) in enumerate(DOWN):
                            w_ = weights(two, l, f"{f}d{n}_{i}", nk=nk)
                            if n == 0:
                                read_out(pe, two, l, *(f"{f}u{c}" for c in range(k0 * P // CHUNK, -(-(k0 + nk) * P // CHUNK))))
                            if i == 0:
                                ps_ = result(two, l, f"{f}d{n}_0")
                            for h in range(HALVES):
                                for k in range(nk):
                                    last = pe.matmul(ps_[:, h, :], hmT[:, k0 + k, h * P:(h + 1) * P], w_[:, k, :],
                                                     start=(k0 + k == 0), stop=(k0 + k == FKT - 1))
                            step(last)

                for m in range(2):
                    mod(m)
                    mod_sum(m)
                norm_T2(0, ("T0a", "T0b"))
                ffn("A", 0, range(2, NMOD))
                norm_T2(1, ("T1a", "T1b"))
                by_feature(two, l, "in_qka", hT)
                by_token(two, l, "in_vaqd", hT)
                by_token(two, l, "in_kdvd", hT)
                by_feature(two, l, "in_qh", hT)
                by_feature(two, l, "in_fh", hT)
                by_token(two, l, "in_ih", hT)
                by_token(two, l, "in_gh", hT)
                read_out(pe, two, l, "in_qka")
                ps_ = result(two, l, "SZ0")
                for j in range(4):
                    at = HD * (j % 2)
                    last = pe.matmul(ps_[:, j % 2, (j // 2) * S:(j // 2 + 1) * S], qkaT[at:at + HD, 2 + j // 2, 0:P],
                                     qkaT[at:at + HD, j // 2, :], start=True, stop=True)
                step(last)
                ps_ = result(two, l, "SZ1")
                for j in range(4):
                    at = HD * (j % 2)
                    last = pe.matmul(ps_[:, j % 2, (j // 2) * P:(j // 2 + 1) * P], qkaT[at:at + HD, 2 + j // 2, P:S],
                                     qkaT[at:at + HD, j // 2, P:S], start=True, stop=True)
                step(last)
                pe.wait_ge(sm["sp_ready"], l + 1)
                ps_ = result(two, l, "SC0")
                for j in range(4):
                    bank, col = j // 2, (j % 2) * S
                    pe.matmul(ps_[:, bank, col:col + S], const("tri_ge"), sp0[:, j, :], start=True, stop=True)
                    last = pe.matmul(ps_[:, bank, col + P:col + S], ones, sp1[:, j, :], start=False, stop=True,
                                     skip_group_check=True)
                step(last)
                ps_ = result(two, l, "SC1")
                for j in range(4):
                    last = pe.matmul(ps_[:, 0, j * P:(j + 1) * P], const("tri_ge"), sp1[:, j, :], start=True, stop=True)
                step(last)
                pe.wait_ge(sm["w_ready"], l + 1)
                read_out(pe, two, l, "in_vaqd")
                ps_ = result(two, l, "SV")
                for j in range(4):
                    cols = slice(j * HD, (j + 1) * HD)
                    i = place(j)
                    pe.matmul(ps_[:, 0, cols], z0[:, i, 0:P], vq[:, 0, cols], start=True, stop=True)
                    pe.matmul(ps_[:, 1, cols], z0[:, i, P:S], vq[:, 0, cols], start=True, stop=False)
                    last = pe.matmul(ps_[:, 1, cols], z1[:, i, :], vq[:, 1, cols], start=False, stop=True)
                step(last)
                pe.wait_ge(sm["drope_ready"], l + 1)
                transposes(two, l, "DT", [(dr[:, h, b * P:(b + 1) * P], P, b // 2, (b % 2) * S + h * P)
                                          for b in range(4) for h in range(HALVES)])
                read_out(pe, two, l, "DT")
                for h in range(HALVES):
                    ps_ = result(two, l, f"DS{h}")
                    for j in range(4):
                        at = HD * (j % 2)
                        last = pe.matmul(ps_[:, j % 2, (j // 2) * S:(j // 2 + 1) * S],
                                         dT[at:at + HD, j // 2, h * P:(h + 1) * P], dT[at:at + HD, 2 + j // 2, :],
                                         start=True, stop=True)
                    step(last)
                for h in range(HALVES):
                    pe.wait_ge(sm["dp_ready"], 2 * l + h + 1)
                    transposes(two, l, f"DP{h}", [(dp[:, h, j * S + t * P:j * S + (t + 1) * P], P, j // 2, (j % 2) * S + t * P)
                                                  for j in range(4) for t in range(2)])
                    read_out(pe, two, l, f"DP{h}", *(["in_kdvd"] if h == 0 else []))
                    ps_ = result(two, l, f"DV{h}")
                    for i in range(4):
                        j = place(i)
                        for t in range(2):
                            last = pe.matmul(ps_[:, 0, i * HD:(i + 1) * HD], dpT[:, h, i * S + t * P:i * S + (t + 1) * P],
                                             kv[:, t, 256 + j * HD:256 + (j + 1) * HD], start=(t == 0), stop=(t == 1))
                    step(last)
                pe.wait_ge(sm["lf_ready"], l + 1)
                transposes(two, l, "HL", [(lfT[:, j, h * P:(h + 1) * P], P, h, j * P) for h in range(HALVES) for j in range(HH)])
                read_out(pe, two, l, "HL")
                decay = const("decay_sum", LEVELS + 1, P)

                def decays(i):
                    ps_ = result(two, l, f"HE{i}")
                    for j in range(HH):
                        for h in range(HALVES):
                            m = i if i < LEVELS - 1 else i + h
                            last = pe.matmul(ps_[:, j // 2, (j % 2) * S + h * P:(j % 2) * S + (h + 1) * P],
                                             lfn[:, h, j * HK:(j + 1) * HK], decay[:, m, :], start=True, stop=True)
                    step(last)

                def level(i):
                    pe.wait_ge(sm["hq_ready"], LEVELS * l + i + 1)
                    q_ = hq[:, i % 2, :].rearrange("p (j s) -> p j s", j=HH)
                    ps_ = result(two, l, f"HS{i}")
                    if i < LEVELS - 1:
                        for j in range(HH):
                            for h in range(HALVES):
                                both = q_[:, j, h * P:(h + 1) * P]
                                last = pe.matmul(ps_[:, j // 2, (j % 2) * S + h * P:(j % 2) * S + (h + 1) * P],
                                                 both, both, start=True, stop=True)
                    else:
                        for j in range(HH):
                            last = pe.matmul(ps_[:, 0, j * P:(j + 1) * P], q_[:, j, 0:P], q_[:, j, P:S],
                                             start=True, stop=True)
                    step(last)

                decays(0)
                decays(1)
                for i in range(LEVELS):
                    level(i)
                    if i + 2 < LEVELS:
                        decays(i + 2)
                pe.wait_ge(sm["kh_ready"], l + 1)
                read_out(pe, two, l, "in_qh")
                ps_ = result(two, l, "HD")
                for j in range(HH):
                    for h in range(HALVES):
                        last = pe.matmul(ps_[:, j // 2, (j % 2) * S + h * P:(j % 2) * S + (h + 1) * P],
                                         khT[:, j, h * P:(h + 1) * P], qhT[:, j, h * P:(h + 1) * P], start=True, stop=True)
                step(last)
                read_out(pe, two, l, "HD", f"HS{LEVELS - 1}", "in_ih")
                ps_ = result(two, l, "HO")
                for j in range(HH):
                    cols = slice(j * HK, (j + 1) * HK)
                    pe.matmul(ps_[:, 0, cols], at_[:, 2 * j, :], ih[:, 0, cols], start=True, stop=True)
                    pe.matmul(ps_[:, 1, cols], at_[:, 2 * j + 1, :], ih[:, 1, cols], start=True, stop=False)
                    last = pe.matmul(ps_[:, 1, cols], at2[:, j, :], ih[:, 0, cols], start=False, stop=True)
                step(last)
                pe.wait_ge(sm["y_dve"], l + 1)
                read_out(pe, two, l, "SV")
                rows_to_hT(two, l, ("Ya", "Yb"))
                read_out(pe, two, l, "Ya", "Yb")
                for n in ("out0", "out1"):
                    by_token(two, l, n, hT)
                norm_T2(2, ("T2a", "T2b"))
                ffn("B", 2, [])

        @block.scalar
        def _(act):
            def col(v, n):
                return v.rearrange("(n p) -> p n", p=P)

            small_loads = [
                (g_mem[:, :], col(w["mem_norm_g"], KT)),
                (g_mix[:, :], w["mix_norm_g"].rearrange("l (k p) -> p (l k)", p=P)),
                (g_xa[:, :], w["xattn_norm_g"].rearrange("l (k p) -> p (l k)", p=P)),
                (g_ffn[:, :], w["ffn_norm_g"].rearrange("l (k p) -> p (l k)", p=P)),
                (g_br[:, :], w["branch_norm_g"].rearrange("l b (k p) -> p (l b k)", p=P)),
                (b_s[:, :], w["gm_b_s"].rearrange("l g p -> p (l g)")),
                (w_s[:, :, :], w["gm_w_s"].rearrange("l g i j -> i (l g) j").rearrange("i (l g) j -> i l g j", l=LAYERS)),
                (router[:, :, :], w["w_router"].rearrange("l (k p) e -> p (l k) e", p=P)),
                (g_v[:, :, :], w["gm_v_norm_g"].partition_broadcast(P)),
                (g_q1[:, :, :], w["q_norm_g"].partition_broadcast(P)),
                (g_k1[:, :, :], w["k_norm_g"].partition_broadcast(P)),
                (g_q2[:, :, :], w["q_norm_g_2"].partition_broadcast(P)),
                (g_k2[:, :, :], w["k_norm_g_2"].partition_broadcast(P)),
                (g_h[:, :, :], w["hgrn_norm_g_2"].partition_broadcast(P)),
                (g_final[:, :], w["final_norm_g"].partition_broadcast(P)),
                (lbl[:, :], w["hgrn_lb_logits_2"].rearrange("l (h p) -> p (l h)", p=P)),
                (cT[:, :], w["c_2"].rearrange("o (k p) -> p (o k)", p=P)),
                (b_mod[:, :, :], w["b_mod_2"].rearrange("l (u n) -> u l n", n=CHUNK)),
            ]
            assert len(small_loads) == N_SMALL
            for dst, src in small_loads:
                if len(dst.shape) == 3 and len(src.shape) == 4:
                    dst = dst.rearrange("p l (g j) -> p l g j", g=4)
                act.dma_start(dst, src, allow_slow_non_contiguous=True).then_inc(load_p, 16)

            def squares(r, src, scratch):
                for h in range(HALVES):
                    last = act.activation(scratch[:, h, :], src[:, h, :], ACT.Square, scale=D ** -0.5,
                                          accum_out=ss[:, h:h + 1])
                last.then_inc(ss_ready, 1)

            def copy(order, l, name, dst, src, func=ACT.Copy, after=None, n=2, g=0, **kw):
                finished(act, order, l, after or name, g)
                act.activation(dst, src(ps[order.pair(name)]), func, **kw).then_inc(pair_free[order.pair(name)], n)

            def flat(p):
                return p[:, :, :].rearrange("p a b -> p (a b)")

            def second_bank(order, l, name, dst, after=None, g=0):
                copy(order, l, name, dst, lambda p: p[:, 1, :], after=after, n=1, g=g)

            def hT_bank(order, l, ab, scale, bias=None, dst=hT):
                for i in range(2):
                    finished(act, order, l, ab[i])
                    p = ps[order.pair(ab[i])]
                    for kk in range(2):
                        k = 4 * i + 2 + kk
                        if bias is None:
                            last = act.activation(dst[:, k, :], p[:, 1, kk * S:(kk + 1) * S], ACT.Copy, scale=scale(k))
                        else:
                            last = act.activation(dst[:, k, :], p[:, 1, kk * S:(kk + 1) * S], ACT.Identity,
                                                  scale=scale(k), bias=bias(k))
                    last.then_inc(pair_free[order.pair(ab[i])], 1)

            def exps(order, l, name, b, dst):
                scale = {"S": HD ** -0.5, "X": XD ** -0.5}[name[0]]
                p = flat(ps[order.pair(name)])
                for j in range(4):
                    last = act.activation(dst[:, j * S:(j + 1) * S], p[:, j * S:(j + 1) * S], ACT.Exp,
                                          bias=nmax[:, b, j:j + 1], scale=scale, accum_out=ssum[:, b, j:j + 1])
                last.then_inc(pair_free[order.pair(name)], 2)

            act.wait_ge(load_m, 16)
            squares(0, xn, cut(0, HALVES, D))
            act.wait_ge(load_p, 16 * N_SMALL)
            hT_bank(begin, 0, ("T0a", "T0b"), lambda k: g_mem[:, k:k + 1], dst=memT)
            act.wait_ge(sm["c_silu"], 1)
            act.activation(c32[:, :, 0:1].rearrange("p k o -> p (k o)"), cT[:, :], ACT.Silu).then_inc(sm["c_ready"], 1)
            act.wait_ge(sm["lb_exp"], 1)
            act.activation(lbl[:, :], lbl[:, :], ACT.Exp).then_inc(sm["lb_sum"], 1)
            act.wait_ge(sm["lb_root"], 1)
            act.activation(lb_ln[:, :], lb_ln[:, :], ACT.Ln)
            act.activation(lb_ln1m[:, :], lb_1m[:, :], ACT.Ln).then_inc(sm["lb_log"], 1)

            with act.Fori(0, LAYERS) as l:
                def norm(j, ab, gain):
                    act.wait_ge(x_ready, 1 + 3 * l + j)
                    squares(1 + 3 * l + j, x, xn)
                    hT_bank(one, l, ab, lambda k: gain[:, bass.ds(l * KT + k, 1)])

                norm(0, ("T0a", "T0b"), g_mix)
                copy(one, l, "in_u", ug[:, :, :], lambda p: p[:, :, :], ACT.Gelu_apprx_tanh)
                copy(one, l, "in_v", vg[:, :, :], lambda p: p[:, :, :], ACT.Gelu_apprx_tanh)
                copy(one, l, "in_q", qk[:, :, 0:512], lambda p: p[:, :, :])
                finished(act, one, l, "in_kv")
                p = ps[one.pair("in_kv")]
                act.activation(qk[:, :, 512:640], p[:, :, 0:P], ACT.Copy)
                act.activation(vv[:, :, :], p[:, :, P:2 * P], ACT.Copy).then_inc(pair_free[one.pair("in_kv")], 2)
                for i in range(2):
                    copy(one, l, f"xk{i}", kxT[:, 4 * i:4 * i + 4, :].rearrange("p k s -> p (k s)"), flat)
                for i in range(2):
                    copy(one, l, f"xv{i}", vx[:, :, i * 512:(i + 1) * 512], lambda p: p[:, :, :])
                copy(one, l, "ws", w_s_now[:, :], lambda p: p[:, 0, :])
                second_bank(one, l, "qT", qkT[:, 2:4, :].rearrange("p a b -> p (a b)"))
                copy(one, l, "kT", qkT[:, 4:6, :].rearrange("p a b -> p (a b)"), lambda p: p[:, 0, :])

                def att_exp(b):
                    act.wait_ge(sm["smax_ready"], 4 * l + b + 1)
                    exps(one, l, f"S{b}", b, pr[:, b % 2, :])

                def att_turn(b):
                    second_bank(one, l, f"P{b}", pTr[:, b % 2, 512:1024])

                att_exp(0)
                att_exp(1)
                att_turn(0)
                att_exp(2)
                att_turn(1)
                att_exp(3)
                att_turn(2)
                att_turn(3)
                hT_bank(one, l, ("Ma", "Mb"), lambda k: g_br[:, bass.ds(l * KT + k, 1)])
                norm(1, ("T1a", "T1b"), g_xa)
                for i in range(2):
                    copy(one, l, f"xq{i}", qxT[:, 4 * i:4 * i + 4, :].rearrange("p k s -> p (k s)"), flat)
                for h in range(HALVES):
                    act.wait_ge(sm["xmax_ready"], 2 * l + h + 1)
                    exps(one, l, f"XS{h}", h, px[:, h, :])
                for h in range(HALVES):
                    copy(one, l, f"XP{h}", pxT[:, 2:4, :, h * P:(h + 1) * P],
                         lambda p: p[:, 1, :].rearrange("p (j t q) -> p j t q", j=2, t=2), n=1)
                for i in range(2):
                    second_bank(one, l, ("XOa", "XOb")[i], oxT[:, 4 * i + 2:4 * i + 4, :].rearrange("p a b -> p (a b)"))
                norm(2, ("T2a", "T2b"), g_ffn)
                act.wait_ge(sm["rmax_ready"], l + 1)
                p = ps[one.pair("route")]
                for h in range(HALVES):
                    last = act.activation(aff[:, h, :], p[:, 0, h * NE:(h + 1) * NE], ACT.Exp,
                                          bias=nmax[:, 0, h:h + 1], accum_out=ssum[:, 0, h:h + 1])
                last.then_inc(pair_free[one.pair("route")], 2)
                second_bank(one, l, "gateT", gateT[:, 2:4, :, :].rearrange("p g h t -> p (g h t)"))
                with act.Fori(0, GROUPS) as g:
                    copy(one, l, "g0", act_mid[:, :], flat, ACT.Silu, after=f"g{KT - 1}", g=g)
                    second_bank(one, l, "midT", midT[:, 4:8, :].rearrange("p a b -> p (a b)"), g=g)
                    copy(one, l, "d0", ys[:, bass.ds(g, 1), :].rearrange("p a d -> p (a d)"), flat, after=f"d{KT - 1}", g=g)
            act.wait_ge(x_ready, 1 + 3 * LAYERS)
            squares(1 + 3 * LAYERS, x, xn)

            with act.Fori(0, LAYERS) as l:
                def norm2(j, ab):
                    act.wait_ge(x_ready, 8 + 3 * l + j)
                    squares(8 + 3 * l + j, x, xn)
                    read_out(act, two, l, f"mb{3 * j}", f"mb{3 * j + 1}")
                    hT_bank(two, l, ab, lambda k: mcol[:, 3 * j + 1, k:k + 1], lambda k: mcol[:, 3 * j, k:k + 1])

                def mod(m):
                    if m:
                        finished(act, two, l, f"mb{m - 1}")
                    copy(two, l, f"m{m}_0", part[:, :, :], lambda p: p[:, :, :], after=f"m{m}_1")

                def ffn(f, mods):
                    mods = list(mods)
                    for c, n in enumerate(FFC):
                        if c >= 2:
                            read_out(act, two, l, f"{f}u{c - 2}")
                        copy(two, l, f"{f}g{c}", sg[:, c % 2, 0:2 * n], lambda p: flat(p)[:, 0:2 * n], ACT.Silu)
                        if mods:
                            mod(mods.pop(0))
                    for m in mods:
                        mod(m)

                mod(0)
                mod(1)
                norm2(0, ("T0a", "T0b"))
                ffn("A", range(2, NMOD))
                norm2(1, ("T1a", "T1b"))
                copy(two, l, "in_qka", qkaT[:, :, :].rearrange("p a b -> p (a b)"), flat)
                copy(two, l, "in_vaqd", vq[:, :, :], lambda p: p[:, :, :])
                copy(two, l, "in_kdvd", kv[:, :, :], lambda p: p[:, :, :])
                copy(two, l, "in_qh", qhT[:, :, :].rearrange("p a b -> p (a b)"), flat, ACT.Silu)
                copy(two, l, "in_fh", fz, flat)
                copy(two, l, "in_ih", ih[:, :, :], lambda p: p[:, :, :])
                copy(two, l, "in_gh", gh[:, :, :], lambda p: p[:, :, :], ACT.Silu)
                act.wait_ge(sm["fab_ready"], l + 1)
                act.activation(fa, fa, ACT.Exp, scale=-1.0)
                act.drain()
                act.activation(fa, fa, ACT.Ln, bias=1.0).then_inc(sm["flog"], 1)
                act.wait_ge(sm["fd_ready"], l + 1)
                act.activation(fd, fd, ACT.Exp, scale=-1.0)
                act.activation(khT[:, :, :].rearrange("p a b -> p (a b)"), fs, ACT.Exp, scale=-1.0)
                act.drain()
                act.activation(fd, fd, ACT.Ln, bias=1.0).then_inc(sm["fl2"], 1)
                act.wait_ge(sm["sp_in"], l + 1)
                l_both = work[:, 9728:9728 + 1536]
                act.activation(l_both, l_both, ACT.Exp, scale=-1.0)
                act.drain()
                act.activation(l_both, l_both, ACT.Ln, bias=1.0).then_inc(sm["st_log"], 1)
                act.wait_ge(sm["w_arg"], l + 1)
                z_both = work[:, 8192:8192 + 1536]
                act.activation(z_both, z_both, ACT.Exp).then_inc(sm["w_exp"], 1)
                copy(two, l, "SV", xn[:, :, 0:256], lambda p: p[:, :, 0:256])
                second_bank(two, l, "DT", dT[:, 2:4, :].rearrange("p a b -> p (a b)"))
                for h in range(HALVES):
                    act.wait_ge(sm["dmax_ready"], 2 * l + h + 1)
                    for j in range(4):
                        last = act.activation(dp[:, h, j * S:(j + 1) * S], dp[:, h, j * S:(j + 1) * S], ACT.Exp,
                                              bias=nmax[:, h, j:j + 1], scale=HD ** -0.5)
                    last.then_inc(sm["dexp"], 1)
                for h in range(HALVES):
                    second_bank(two, l, f"DP{h}", dpT[:, h, 512:1024])
                copy(two, l, "HL", lfn[:, :, :], lambda p: p[:, :, :])
                for i in range(LEVELS):
                    if i >= 2:
                        act.wait_ge(sm["hq_ready"], LEVELS * l + i - 1)
                    copy(two, l, f"HE{i}", he[:, i % 2, :], flat, ACT.Exp)
                copy(two, l, f"HS{LEVELS - 1}", at2[:, :, :].rearrange("p a b -> p (a b)"), lambda p: p[:, 0, :])
                for i in range(2):
                    second_bank(two, l, ("Ya", "Yb")[i], hT[:, 4 * i + 2:4 * i + 4, :].rearrange("p a b -> p (a b)"))
                norm2(2, ("T2a", "T2b"))
                ffn("B", [])

        @block.gpsimd
        def _(pool):
            pool.memset(mhalf[:, :], -0.5)
            pool.memset(eps[:, :], EPS)
            pool.memset(quarter[:, :], 0.25)
            pool.memset(c32[:, :, :], 0.0).then_inc(sm["c_silu"], 1)

            def rms(r):
                pool.wait_ge(ss_ready, r + 1)
                pool.tensor_tensor(ms[:, :], ss[:, :], eps[:, :], ALU.add)
                pool.drain()
                pool.tensor_tensor(rstd[:, :], ms[:, :], mhalf[:, 0:2], ALU.pow).then_inc(rstd_ready, 1)

            def root(n, width):
                pool.wait_ge(var_ready, n + 1)
                pool.tensor_tensor(inv[:, 0:width], var[:, 0:width], mhalf[:, 0:width], ALU.pow).then_inc(inv_ready, 1)

            pool.drain()
            rms(0)
            pool.wait_ge(load_p, 16 * N_SMALL)
            pool.wait_ge(sm["lb_floor"], 1)
            pool.tensor_tensor(lb_ln[:, :], lb_ln[:, :], quarter[:, :], ALU.pow).then_inc(sm["lb_root"], 1)
            with pool.Fori(0, LAYERS) as l:
                finished(pool, one, l - 1, "mix")
                pool.tensor_copy(w_s_now[:, :], w_s[:, bass.ds(l, 1), :].rearrange("p a b -> p (a b)")).then_inc(sm["ws_now"], 1)
                rms(1 + 3 * l)
                root(3 * l, 2)
                root(3 * l + 1, 20)
                root(3 * l + 2, 4)
                rms(2 + 3 * l)
                rms(3 + 3 * l)
            rms(1 + 3 * LAYERS)
            with pool.Fori(0, LAYERS) as l:
                finished(pool, two, l - 1, f"mb{NMOD - 1}")
                pool.tensor_copy(bm_now[:, :], b_mod[:, bass.ds(l, 1), :].rearrange("p a b -> p (a b)")).then_inc(sm["bm_ready"], 1)
                rms(8 + 3 * l)
                rms(9 + 3 * l)
                root(3 * LAYERS + 2 * l, 16)
                root(3 * LAYERS + 2 * l + 1, 8)
                rms(10 + 3 * l)

        @block.vector
        def _(v):
            def flat(p):
                return p[:, :, :].rearrange("p a b -> p (a b)")

            def free(order, name, ins, n=2):
                ins.then_inc(pair_free[order.pair(name)], n)

            def norm_rows(r, src):
                v.wait_ge(rstd_ready, r + 1)
                for h in range(HALVES):
                    last = v.tensor_scalar(xn[:, h, :], src[:, h, :], rstd[:, h:h + 1], None, ALU.mult)
                last.then_inc(xn_ready, 2)

            def hT_bank(order, l, ab, scale, bias=None, dst=hT):
                for i in range(2):
                    finished(v, order, l, ab[i])
                    p = ps[order.pair(ab[i])]
                    for kk in range(2):
                        k = 4 * i + kk
                        if bias is None:
                            last = v.tensor_scalar(dst[:, k, :], p[:, 0, kk * S:(kk + 1) * S], scale(k), None, ALU.mult)
                        else:
                            last = v.tensor_scalar(dst[:, k, :], p[:, 0, kk * S:(kk + 1) * S], scale(k), bias(k), ALU.mult, ALU.add)
                    free(order, ab[i], last, 1)

            def first_bank(order, l, name, dst, g=0):
                finished(v, order, l, name, g)
                free(order, name, v.tensor_copy(dst, ps[order.pair(name)][:, 0, :]), 1)

            def add_to_x(order, l, names, last_steps):
                for i, n in enumerate(names):
                    finished(v, order, l, last_steps[i])
                    cols = slice(i * CHUNK, (i + 1) * CHUNK)
                    free(order, n, v.tensor_tensor(x[:, :, cols], x[:, :, cols], ps[order.pair(n)][:, :, :], ALU.add))
                v.drain().then_inc(x_ready, 1)

            def add_gated(order, l, names, last_steps, gate):
                for i, n in enumerate(names):
                    finished(v, order, l, last_steps[i])
                    cols = slice(i * CHUNK, (i + 1) * CHUNK)
                    g_ = gate_b[:, gate:gate + 1, cols].broadcast_to([P, HALVES, CHUNK])
                    free(order, n, v.tensor_tensor(tmp[:, :, :], ps[order.pair(n)][:, :, :], g_, ALU.mult))
                    v.drain()
                    v.tensor_tensor(x[:, :, cols], x[:, :, cols], tmp[:, :, :], ALU.add)
                    v.drain()
                v.drain().then_inc(x_ready, 1)

            def inverse_root(n, width, count):
                v.drain()
                v.tensor_scalar(var[:, 0:count], var[:, 0:count], 1.0 / width, EPS, ALU.mult, ALU.add).then_inc(var_ready, 1)
                v.wait_ge(inv_ready, n + 1)

            def sum_squares(src, scratch, out_):
                v.tensor_tensor(scratch, src, src, ALU.mult)
                v.drain()
                v.tensor_reduce(out_, scratch, AX.X, ALU.add)

            def rope(dst, src, cos, sin, a, b, ta, tb):
                heads = src.shape[1]
                c = cos.rearrange("p (o n) -> p o n", o=1).broadcast_to([P, heads, HD // 2])
                s_ = sin.rearrange("p (o n) -> p o n", o=1).broadcast_to([P, heads, HD // 2])
                v.tensor_tensor(ta, a(src), c, ALU.mult)
                v.tensor_tensor(tb, b(src), s_, ALU.mult)
                v.drain()
                v.tensor_tensor(a(dst), ta, tb, ALU.subtract)
                v.drain()
                v.tensor_tensor(ta, a(src), s_, ALU.mult)
                v.tensor_tensor(tb, b(src), c, ALU.mult)
                v.drain()
                v.tensor_tensor(b(dst), ta, tb, ALU.add)
                v.drain()

            def by_place(r):
                return r.rearrange("p (b a o) -> p b a o", b=2, o=1).broadcast_to([P, 2, 2, HD])

            def row_max(order, l, name, b, scale, ready):
                finished(v, order, l, name)
                v.tensor_reduce(smax[:, b, :], flat(ps[order.pair(name)]).rearrange("p (j s) -> p j s", j=4), AX.X, ALU.max)
                v.drain()
                v.tensor_scalar(nmax[:, b, :], smax[:, b, :], -scale, None, ALU.mult).then_inc(ready, 1)

            v.wait_ge(load_c, 16)
            v.wait_ge(load_p, 16 * N_SMALL)
            v.wait_ge(load_x, 16)
            v.wait_ge(load_m, 16)
            norm_rows(0, xn)
            hT_bank(begin, 0, ("T0a", "T0b"), lambda k: g_mem[:, k:k + 1], dst=memT)
            a0, a1 = lbl[:, 0:HH], lbl[:, HH:2 * HH]
            v.tensor_tensor(lbt[:, 0, :], a0, a1, ALU.max)
            v.drain()
            v.tensor_tensor(a0, a0, lbt[:, 0, :], ALU.subtract)
            v.tensor_tensor(a1, a1, lbt[:, 0, :], ALU.subtract).then_inc(sm["lb_exp"], 1)
            v.wait_ge(sm["lb_sum"], 1)
            v.tensor_tensor(lbt[:, 0, :], a0, a1, ALU.add)
            v.drain()
            v.reciprocal(lbt[:, 1, :], lbt[:, 0, :])
            v.drain()
            v.tensor_tensor(a0, a0, lbt[:, 1, :], ALU.mult)
            v.tensor_tensor(a1, a1, lbt[:, 1, :], ALU.mult)
            v.drain()
            v.tensor_tensor(lbt[:, 2, :], a0, a1, ALU.add)
            v.drain()
            v.tensor_tensor(lb_ln[:, 0:HH], a0, a0, ALU.subtract)
            v.tensor_tensor(lb_ln[:, HH:2 * HH], lbt[:, 2, :], a0, ALU.subtract)
            v.drain()
            v.tensor_scalar(lb_ln[:, :], lb_ln[:, :], 0.0, 1.0 - EPS, ALU.max, ALU.min)
            v.drain()
            v.tensor_scalar(lb_1m[:, :], lb_ln[:, :], -1.0, 1.0, ALU.mult, ALU.add)
            v.tensor_scalar(lb_ln[:, :], lb_ln[:, :], LB_FLOOR, None, ALU.max).then_inc(sm["lb_floor"], 1)
            v.wait_ge(sm["lb_log"], 1)
            v.tensor_scalar(lb_ln[:, :], lb_ln[:, :], 4.0, None, ALU.mult)
            v.drain().then_inc(x_ready, 1)

            with v.Fori(0, LAYERS) as l:
                def norm(j, ab, gain):
                    norm_rows(1 + 3 * l + j, x)
                    hT_bank(one, l, ab, lambda k: gain[:, bass.ds(l * KT + k, 1)])

                norm(0, ("T0a", "T0b"), g_mix)
                read_out(v, one, l, "in_u", "in_v")
                sq_ = sq1[:, 0:1024].rearrange("p (h n) -> p h n", h=HALVES)
                sum_squares(vg[:, :, :], sq_, var[:, 0:2])
                inverse_root(3 * l, GM, 2)
                for h in range(HALVES):
                    v.scalar_tensor_tensor(vg[:, h, :], vg[:, h, :], inv[:, h:h + 1],
                                           g_v[:, bass.ds(l, 1), :].rearrange("p a n -> p (a n)"), ALU.mult, ALU.mult)
                v.drain().then_inc(sm["v_ready"], 1)
                read_out(v, one, l, "in_q", "in_kv")
                heads = QH + KVH
                qk4 = qk[:, :, :].rearrange("p h (n d) -> p (h n) d", d=HD)
                sum_squares(qk4, sq1.rearrange("p (n d) -> p n d", d=HD), var[:, 0:2 * heads])
                inverse_root(3 * l + 1, HD, 2 * heads)
                v.tensor_tensor(qk4, qk4, inv[:, 0:2 * heads].rearrange("p (n o) -> p n o", o=1).broadcast_to([P, 2 * heads, HD]), ALU.mult)
                v.drain()
                for h in range(HALVES):
                    q3, k3 = (qk[:, h, a:b].rearrange("p (n d) -> p n d", d=HD) for a, b in ((0, 512), (512, 640)))
                    v.tensor_tensor(q3, q3, g_q1[:, bass.ds(l, 1), :].broadcast_to([P, QH, HD]), ALU.mult)
                    v.tensor_tensor(k3, k3, g_k1[:, bass.ds(l, 1), :].broadcast_to([P, KVH, HD]), ALU.mult)
                v.drain()
                for h in range(HALVES):
                    rope(rq[:, h, :].rearrange("p (n d) -> p n d", d=HD), qk[:, h, :].rearrange("p (n d) -> p n d", d=HD),
                         const("cos1", 2, 32)[:, h, :], const("sin1", 2, 32)[:, h, :],
                         lambda t: t[:, :, 0:HD:2], lambda t: t[:, :, 1:HD:2],
                         t1[:, h, :].rearrange("p (n d) -> p n d", d=HD // 2), t2[:, h, :].rearrange("p (n d) -> p n d", d=HD // 2))
                for h in range(HALVES):
                    for j in range(KVH):
                        last = v.tensor_copy(kdup[:, h, j * P:(j + 1) * P].rearrange("p (n d) -> p n d", d=HD),
                                             rq[:, h, 512 + j * HD:512 + (j + 1) * HD].rearrange("p (o d) -> p o d", o=1).broadcast_to([P, 2, HD]))
                last.then_inc(sm["rope_ready"], 1)
                finished(v, one, l, "mix")
                for h in range(HALVES):
                    for i in range(4):
                        cols = slice(i * P, (i + 1) * P)
                        last = v.scalar_tensor_tensor(ug[:, h, cols], ps[one.pair("mix")][:, h, cols],
                                                      b_s[:, bass.ds(l * 4 + i, 1)], ug[:, h, cols], ALU.add, ALU.mult)
                free(one, "mix", last)
                first_bank(one, l, "qT", qkT[:, 0:2, :].rearrange("p a b -> p (a b)"))

                def att_max(b):
                    row_max(one, l, f"S{b}", b, HD ** -0.5, sm["smax_ready"])

                def att_turn(b):
                    first_bank(one, l, f"P{b}", pTr[:, b % 2, 0:512])

                def att_out(b):
                    h, hg = b // 2, b % 2
                    read_out(v, one, l, f"S{b}")
                    v.reciprocal(rsum[:, b, :], ssum[:, b, :])
                    v.drain()
                    finished(v, one, l, f"V{b}")
                    free(one, f"V{b}", v.tensor_tensor(
                        xn[:, h, 512 + 256 * hg:768 + 256 * hg].rearrange("p (a b d) -> p b a d", b=2, d=HD),
                        ps[one.pair(f"V{b}")][:, 0, 0:256].rearrange("p (b a d) -> p b a d", b=2, d=HD),
                        by_place(rsum[:, b, :]), ALU.mult))

                att_max(0)
                att_max(1)
                att_turn(0)
                att_out(0)
                att_max(2)
                att_turn(1)
                att_out(1)
                att_max(3)
                att_turn(2)
                att_out(2)
                att_turn(3)
                att_out(3)
                v.drain()
                sum_squares(ug[:, :, :], qk[:, :, 0:512], var[:, 0:2])
                v.drain()
                sum_squares(xn[:, :, 512:1024], qk[:, :, 0:512], var[:, 2:4])
                inverse_root(3 * l + 2, GM, 4)
                for h in range(HALVES):
                    v.tensor_scalar(xn[:, h, 0:512], ug[:, h, :], inv[:, h:h + 1], None, ALU.mult)
                    v.tensor_scalar(xn[:, h, 512:1024], xn[:, h, 512:1024], inv[:, 2 + h:3 + h], None, ALU.mult)
                v.drain().then_inc(sm["merged"], 1)
                hT_bank(one, l, ("Ma", "Mb"), lambda k: g_br[:, bass.ds(l * KT + k, 1)])
                add_to_x(one, l, ("out0", "out1"), ("out0", "out1"))
                norm(1, ("T1a", "T1b"), g_xa)
                for h in range(HALVES):
                    row_max(one, l, f"XS{h}", h, XD ** -0.5, sm["xmax_ready"])
                for h in range(HALVES):
                    read_out(v, one, l, f"XS{h}")
                    v.reciprocal(rsum[:, h, :], ssum[:, h, :])
                    v.drain()
                    for j in range(XH):
                        last = v.tensor_scalar(px[:, h, j * S:(j + 1) * S], px[:, h, j * S:(j + 1) * S],
                                               rsum[:, h, j:j + 1], None, ALU.mult)
                    last.then_inc(sm["xpn_ready"], 1)
                for h in range(HALVES):
                    finished(v, one, l, f"XP{h}")
                    free(one, f"XP{h}", v.tensor_copy(pxT[:, 0:2, :, h * P:(h + 1) * P],
                                                      ps[one.pair(f"XP{h}")][:, 0, :].rearrange("p (j t q) -> p j t q", j=2, t=2)), 1)
                for i in range(2):
                    first_bank(one, l, ("XOa", "XOb")[i], oxT[:, 4 * i:4 * i + 2, :].rearrange("p a b -> p (a b)"))
                add_to_x(one, l, ("xo0", "xo1"), ("xo0", "xo1"))
                norm(2, ("T2a", "T2b"), g_ffn)
                finished(v, one, l, "route")
                v.tensor_reduce(smax[:, 0, 0:2], ps[one.pair("route")][:, 0, 0:2 * NE].rearrange("p (h e) -> p h e", h=2), AX.X, ALU.max)
                v.drain()
                v.tensor_scalar(nmax[:, 0, 0:2], smax[:, 0, 0:2], -1.0, None, ALU.mult).then_inc(sm["rmax_ready"], 1)
                read_out(v, one, l, "route")
                v.reciprocal(rsum[:, 0, 0:2], ssum[:, 0, 0:2])
                v.drain()
                v.tensor_tensor(aff[:, :, :], aff[:, :, :],
                                rsum[:, 0, 0:2].rearrange("p (n o) -> p n o", o=1).broadcast_to([P, HALVES, NE]), ALU.mult).then_inc(sm["aff_ready"], 1)
                finished(v, one, l, "affT")
                free(one, "affT", v.tensor_copy(aw[0], ps[one.pair("affT")][0:NE, 0, 0:S]))
                v.drain()
                for i in range(CAP // 8):
                    src, dst = aw[i % 2], aw[(i + 1) % 2]
                    v.max(small[0:NE, 8 * i:8 * i + 8], src)
                    v.drain()
                    v.match_replace(dst, small[0:NE, 8 * i:8 * i + 8], src, -1.0)
                    v.drain()
                taken, ones_, count = aw[2], aw[3], aw[4]
                v.tensor_scalar(taken, aw[(CAP // 8) % 2], -1.0, None, ALU.is_equal)
                v.memset(ones_, 1.0)
                v.drain()
                v.tensor_tensor_scan(count, ones_, taken, 0.0, ALU.mult, ALU.add)
                v.drain()
                v.tensor_tensor(count, count, taken, ALU.mult)
                v.drain()
                v.tensor_scalar(aw[5], count, -1.0, None, ALU.add).then_inc(sm["pos_ready"], 1)
                finished(v, one, l, "posT")
                free(one, "posT", v.tensor_copy(posn[:, :, :], ps[one.pair("posT")][:, 0, 0:2 * NE].rearrange("p (h e) -> p h e", h=2)))
                v.drain()
                for h in range(HALVES):
                    v.tensor_tensor(sel[:, h, :].rearrange("p (e c) -> p e c", e=NE),
                                    posn[:, h, :].rearrange("p (e o) -> p e o", o=1).broadcast_to([P, NE, CAP]),
                                    const("iota", NE, CAP), ALU.is_equal)
                v.drain()
                for h in range(HALVES):
                    v.tensor_tensor(selg[:, h, :].rearrange("p (e c) -> p e c", e=NE), sel[:, h, :].rearrange("p (e c) -> p e c", e=NE),
                                    aff[:, h, :].rearrange("p (e o) -> p e o", o=1).broadcast_to([P, NE, CAP]), ALU.mult)
                v.drain().then_inc(sm["sel_ready"], 1)
                first_bank(one, l, "gateT", gateT[:, 0:2, :, :].rearrange("p g h t -> p (g h t)"))
                with v.Fori(0, GROUPS) as g:
                    finished(v, one, l, "gather", g)
                    for b in range(2):
                        last = v.tensor_tensor(xsT[:, 4 * b:4 * b + 4, :], ps[one.pair("gather")][:, b, :].rearrange("p (k s) -> p k s", k=4),
                                               g_ffn[:, bass.ds(l * KT + 4 * b, 4)].rearrange("p (k o) -> p k o", o=1).broadcast_to([P, 4, P]), ALU.mult)
                    free(one, "gather", last)
                    read_out(v, one, l, "g0", g=g)
                    finished(v, one, l, f"u{KT - 1}", g)
                    free(one, "u0", v.tensor_tensor(mid[:, :], act_mid[:, :], flat(ps[one.pair("u0")]), ALU.mult))
                    first_bank(one, l, "midT", midT[:, 0:4, :].rearrange("p a b -> p (a b)"), g)
                for h in range(HALVES):
                    finished(v, one, l, f"C{h}")
                    free(one, f"C{h}", v.tensor_tensor(x[:, h, :], x[:, h, :], flat(ps[one.pair(f"C{h}")]), ALU.add))
                v.drain().then_inc(x_ready, 1)
            r = 1 + 3 * LAYERS
            v.wait_ge(rstd_ready, r + 1)
            for h in range(HALVES):
                v.scalar_tensor_tensor(x[:, h, :], x[:, h, :], rstd[:, h:h + 1], g_final[:, :], ALU.mult, ALU.mult)
            v.drain().then_inc(xn_ready, 2)
            v.drain().then_inc(x_ready, 1)

            with v.Fori(0, LAYERS) as l:
                def norm2(j, ab):
                    norm_rows(8 + 3 * l + j, x)
                    hT_bank(two, l, ab, lambda k: mcol[:, 3 * j + 1, k:k + 1], lambda k: mcol[:, 3 * j, k:k + 1])

                def mod(m):
                    finished(v, two, l, f"mb{m}")
                    p = ps[two.pair(f"mb{m}")]
                    if m % 3 == 2:
                        ins = v.tensor_scalar(gate_b[:, m // 3, :], flat(p), 1.0 if m == 5 else 0.5, None, ALU.mult)
                    else:
                        ins = v.tensor_scalar(mcol[:, m, :], p[:, 0, 0:KT], 1.0 if m % 3 else 0.0, None, ALU.add)
                    free(two, f"mb{m}", ins)

                def ffn(f, mods, gate):
                    mods = list(mods)
                    for c, n in enumerate(FFC):
                        read_out(v, two, l, f"{f}g{c}")
                        finished(v, two, l, f"{f}u{c}")
                        free(two, f"{f}u{c}", v.tensor_tensor(
                            hmT[:, 4 * c:4 * c + n // P, :].rearrange("p a b -> p (a b)"),
                            sg[:, c % 2, 0:2 * n], flat(ps[two.pair(f"{f}u{c}")])[:, 0:2 * n], ALU.mult))
                        if mods:
                            mod(mods.pop(0))
                    for m in mods:
                        mod(m)
                    v.drain()
                    add_gated(two, l, (f"{f}d0_0", f"{f}d1_0"), [f"{f}d{n}_{len(DOWN) - 1}" for n in range(2)], gate)

                mod(0)
                mod(1)
                v.drain()
                norm2(0, ("T0a", "T0b"))
                ffn("A", range(2, NMOD), 0)
                norm2(1, ("T1a", "T1b"))
                read_out(v, two, l, "in_fh")
                v.scalar_tensor_tensor(fa, fz, -1.0, fz, ALU.mult, ALU.max).then_inc(sm["fab_ready"], 1)
                v.wait_ge(sm["flog"], l + 1)
                v.scalar_tensor_tensor(fm, fz, 0.0, fa, ALU.min, ALU.subtract)
                v.scalar_tensor_tensor(fs, fz, 0.0, fa, ALU.max, ALU.add)
                v.drain()
                for j in range(HH):
                    one_, ln_a, ln_b = (t[:, bass.ds(l * HH + j, 1)] for t in (lb_1m, lb_ln, lb_ln1m))
                    c = slice(j * S, (j + 1) * S)
                    v.tensor_scalar(fx[:, c], fm[:, c], ln_b, ln_a, ALU.add, ALU.max)
                    v.tensor_scalar(fd[:, c], fm[:, c], ln_b, ln_a, ALU.add, ALU.subtract)
                v.drain()
                v.scalar_tensor_tensor(fd, fd, -1.0, fd, ALU.mult, ALU.max).then_inc(sm["fd_ready"], 1)
                v.wait_ge(sm["fl2"], l + 1)
                v.tensor_tensor(lfT[:, :, :].rearrange("p a b -> p (a b)"), fx, fd, ALU.add)
                for j in range(HH):
                    v.tensor_scalar(khT[:, j, :], khT[:, j, :], lb_1m[:, bass.ds(l * HH + j, 1)], None, ALU.mult)
                v.drain().then_inc(sm["lf_ready"], 1)
                v.drain().then_inc(sm["kh_ready"], 1)
                z_both, l_both, s_both = (work[:, a:a + 1536] for a in (8192, 9728, 11264))
                finished(v, two, l, "SZ0")
                free(two, "SZ0", v.tensor_scalar(z0[:, :, :].rearrange("p a b -> p (a b)"), flat(ps[two.pair("SZ0")]), HD ** -0.5, None, ALU.mult))
                finished(v, two, l, "SZ1")
                free(two, "SZ1", v.tensor_scalar(z1[:, :, :].rearrange("p (b a) q -> p b (a q)", b=2), ps[two.pair("SZ1")][:, :, 0:2 * P], HD ** -0.5, None, ALU.mult))
                v.drain()
                v.scalar_tensor_tensor(l_both, z_both, -1.0, z_both, ALU.mult, ALU.max).then_inc(sm["sp_in"], 1)
                v.wait_ge(sm["st_log"], l + 1)
                v.scalar_tensor_tensor(s_both, z_both, 0.0, l_both, ALU.max, ALU.add)
                v.drain()
                before = const("key_before_query").rearrange("p (o q) -> p o q", o=1).broadcast_to([P, 4, P])
                v.tensor_tensor(sp0[:, :, 0:P], sp0[:, :, 0:P], before, ALU.mult)
                v.tensor_tensor(sp1[:, :, :], sp1[:, :, :], before, ALU.mult)
                v.drain().then_inc(sm["sp_ready"], 1)
                for name, z_ in (("SC0", z0), ("SC1", z1)):
                    finished(v, two, l, name)
                    zf = z_[:, :, :].rearrange("p a b -> p (a b)")
                    p = flat(ps[two.pair(name)])[:, 0:zf.shape[1]]
                    free(two, name, v.tensor_tensor(zf, zf, p, ALU.subtract))
                v.drain()
                v.tensor_scalar(z_both, z_both, 0.0, None, ALU.min).then_inc(sm["w_arg"], 1)
                v.wait_ge(sm["w_exp"], l + 1)
                v.tensor_tensor(z0[:, :, 0:P], z0[:, :, 0:P], before, ALU.mult)
                v.tensor_tensor(z1[:, :, :], z1[:, :, :], before, ALU.mult)
                v.drain().then_inc(sm["w_ready"], 1)
                finished(v, two, l, "SV")
                for t, c in ((vq, slice(256, 512)), (kv, slice(0, 256))):
                    to = 0 if t is vq else 256
                    v.tensor_copy(dq[:, :, to:to + 256], t[:, :, c])
                v.drain()
                dq4 = dq[:, :, :].rearrange("p h (n d) -> p (h n) d", d=HD)
                sum_squares(dq4, dsq.rearrange("p (n d) -> p n d", d=HD), var[:, 0:16])
                inverse_root(3 * LAYERS + 2 * l, HD, 16)
                v.tensor_tensor(dq4, dq4, inv[:, 0:16].rearrange("p (n o) -> p n o", o=1).broadcast_to([P, 16, HD]), ALU.mult)
                v.drain()
                for h in range(HALVES):
                    for a, gain in ((0, g_q2), (256, g_k2)):
                        t3 = dq[:, h, a:a + 256].rearrange("p (n d) -> p n d", d=HD)
                        v.tensor_tensor(t3, t3, gain[:, bass.ds(l, 1), :].broadcast_to([P, 4, HD]), ALU.mult)
                v.drain()
                for h in range(HALVES):
                    rope(dr[:, h, :].rearrange("p (n d) -> p n d", d=HD), dq[:, h, :].rearrange("p (n d) -> p n d", d=HD),
                         const("cos2", 2, 32)[:, h, :], const("sin2", 2, 32)[:, h, :],
                         lambda t: t[:, :, 0:HD // 2], lambda t: t[:, :, HD // 2:HD],
                         dt1[:, h, :].rearrange("p (n d) -> p n d", d=HD // 2), dt2[:, h, :].rearrange("p (n d) -> p n d", d=HD // 2))
                v.drain().then_inc(sm["drope_ready"], 1)
                first_bank(two, l, "DT", dT[:, 0:2, :].rearrange("p a b -> p (a b)"))
                for h in range(HALVES):
                    finished(v, two, l, f"DS{h}")
                    d3 = dp[:, h, :].rearrange("p (j s) -> p j s", j=4)
                    neg = const("dil_neg", HALVES, S)[:, h:h + 1, :].broadcast_to([P, 4, S])
                    free(two, f"DS{h}", v.tensor_tensor(d3, flat(ps[two.pair(f"DS{h}")]).rearrange("p (j s) -> p j s", j=4), neg, ALU.add))
                    v.drain()
                    v.tensor_reduce(smax[:, h, :], d3, AX.X, ALU.max)
                    v.drain()
                    v.tensor_scalar(nmax[:, h, :], smax[:, h, :], -HD ** -0.5, None, ALU.mult).then_inc(sm["dmax_ready"], 1)
                for h in range(HALVES):
                    v.wait_ge(sm["dexp"], 2 * l + h + 1)
                    d3 = dp[:, h, :].rearrange("p (j s) -> p j s", j=4)
                    v.tensor_tensor(d3, d3, const("dil_count", HALVES, S)[:, h:h + 1, :].broadcast_to([P, 4, S]), ALU.mult)
                    v.drain().then_inc(sm["dp_ready"], 1)
                    v.tensor_reduce(ssum[:, h, :], d3, AX.X, ALU.add)
                    v.drain()
                    v.reciprocal(rsum[:, h, :], ssum[:, h, :])
                    v.drain()
                for h in range(HALVES):
                    first_bank(two, l, f"DP{h}", dpT[:, h, 0:512])
                    finished(v, two, l, f"DV{h}")
                    free(two, f"DV{h}", v.tensor_tensor(
                        xn[:, h, 256:512].rearrange("p (a b d) -> p b a d", b=2, d=HD),
                        ps[two.pair(f"DV{h}")][:, 0, 0:256].rearrange("p (b a d) -> p b a d", b=2, d=HD),
                        by_place(rsum[:, h, :]), ALU.mult))
                v.memset(at_[:, :, :], 0.0)
                q_all, k_all = (t[:, :, :].rearrange("p a b -> p (a b)") for t in (qhT, khT))
                masks = const("level_mask", LEVELS, P).bitcast(U32)

                def products(i):
                    read_out(v, two, l, f"HE{i}", *(["in_qh"] if i == 0 else []))
                    b = 64 >> i if i < LEVELS - 1 else P
                    e_, o_, q_, k_ = (t.rearrange("p (n two b) -> p n two b", two=2, b=b)
                                      for t in (he[:, i % 2, :], hq[:, i % 2, :], q_all, k_all))
                    v.tensor_tensor(o_[:, :, 0, :], e_[:, :, 0, :], k_[:, :, 0, :], ALU.mult)
                    v.tensor_tensor(o_[:, :, 1, :], e_[:, :, 1, :], q_[:, :, 1, :], ALU.mult)
                    v.drain().then_inc(sm["hq_ready"], 1)

                def take(name, i):
                    finished(v, two, l, name)
                    free(two, name, v.copy_predicated(
                        at_[:, :, :], masks[:, i:i + 1, :].broadcast_to([P, 8, P]),
                        flat(ps[two.pair(name)]).rearrange("p (n t) -> p n t", n=8)))
                    v.drain()

                products(0)
                products(1)
                for i in range(LEVELS):
                    if i < LEVELS - 1:
                        take(f"HS{i}", i)
                    if i + 2 < LEVELS:
                        products(i + 2)
                take("HD", LEVELS - 1)
                finished(v, two, l, "HO")
                free(two, "HO", v.tensor_copy(ho[:, :, :], ps[two.pair("HO")][:, :, :]))
                v.drain()
                ho4 = ho[:, :, :].rearrange("p h (n d) -> p (h n) d", d=HK)
                sum_squares(ho4, hsq.rearrange("p (n d) -> p n d", d=HK), var[:, 0:8])
                inverse_root(3 * LAYERS + 2 * l + 1, HK, 8)
                v.tensor_tensor(ho4, ho4, inv[:, 0:8].rearrange("p (n o) -> p n o", o=1).broadcast_to([P, 8, HK]), ALU.mult)
                v.drain()
                v.tensor_tensor(ho4, ho4, g_h[:, bass.ds(l, 1), :].broadcast_to([P, 8, HK]), ALU.mult)
                v.drain()
                read_out(v, two, l, "in_gh")
                v.tensor_tensor(xn[:, :, 512:1024], ho[:, :, :], gh[:, :, :], ALU.mult).then_inc(sm["y_dve"], 1)
                for i in range(2):
                    first_bank(two, l, ("Ya", "Yb")[i], hT[:, 4 * i:4 * i + 2, :].rearrange("p a b -> p (a b)"))
                add_gated(two, l, ("out0", "out1"), ("out0", "out1"), 1)
                norm2(2, ("T2a", "T2b"))
                ffn("B", [], 2)


_INS = ["x", "mem", "mix_norm_g", "w_in", "gm_v_norm_g", "gm_w_s", "gm_b_s", "q_norm_g", "k_norm_g", "branch_norm_g",
        "w_out", "xattn_norm_g", "mem_norm_g", "xattn_w_q", "xattn_w_kv", "xattn_w_o", "ffn_norm_g", "w_router",
        "w_gate", "w_up", "w_down", "final_norm_g", "c_2", "w_mod_2", "b_mod_2", "ffn1_w_gate_2", "ffn1_w_up_2",
        "ffn1_w_down_2", "w_in_2", "w_out_2", "q_norm_g_2", "k_norm_g_2", "hgrn_norm_g_2", "hgrn_lb_logits_2",
        "ffn2_w_gate_2", "ffn2_w_up_2", "ffn2_w_down_2"]


def kernel(**inputs):
    import concourse.bacc as bacc
    from concourse.bass_utils import run_bass_kernel_spmd

    nc = bacc.Bacc("TRN2", target_bir_lowering=False, num_devices=1)
    arrays, w = {}, {}
    for name in _INS + ["consts"]:
        a = constant_table() if name == "consts" else np.ascontiguousarray(inputs[name])
        arrays[f"in_{name}"] = a
        w[name] = nc.dram_tensor(f"in_{name}", a.shape, mybir.dt.from_np(a.dtype), kind="ExternalInput").ap()
    out = nc.dram_tensor("out_0", (1, S, D), F32, kind="ExternalOutput").ap()
    two_blocks(nc, w, out)
    r = run_bass_kernel_spmd(nc, [arrays], core_ids=[0])
    return r.results[0]["out_0"]
```

```python
from contextlib import ExitStack

import numpy as np

import concourse.bass as bass
from concourse import mybir

F32 = mybir.dt.float32
F32R = mybir.dt.float32r
U32 = mybir.dt.uint32
ALU = mybir.AluOpType
ACT = mybir.ActivationFunctionType
AX = mybir.AxisListType

P = 128
D = 1024
KT = D // P
S = 256
HALVES = S // P
LAYERS = 2
EPS = 1e-6
GM = 512
HD = 64
QH, KVH = 8, 2
XH, XD = 4, 256
NE, FF = 16, 1024
CAP = 2 * S // NE
GROUP = P // CAP
GROUPS = NE // GROUP
DFF = 2816
NMOD = 9
HH, HK = 4, 128
LB_FLOOR = 1e-30
NEG = -1e30
SLOTS = 4
CHUNK = 512
FFC = [min(CHUNK, DFF - c) for c in range(0, DFF, CHUNK)]
FKT = DFF // P
DOWN = [(k, min(KT, FKT - k)) for k in range(0, FKT, KT)]
UNIT = 1024
BUFFERS = 3
LEVELS = 8


CONSTS = {}


def constant_table():
    parts, at = [], 0

    def put(name, a):
        nonlocal at
        a = np.asarray(a, np.float32).reshape(P, -1)
        CONSTS[name] = (at, a.shape[1])
        parts.append(a)
        at += a.shape[1]

    i = np.arange(P)
    put("ident", np.eye(P))
    put("ones", np.ones((P, P)))
    put("iota", np.tile(np.arange(CAP), (P, NE)))
    put("tri_ge", i[:, None] >= i[None, :])
    put("key_before_query", i[:, None] < i[None, :])
    pos = np.arange(S)
    pairs = HD // 4
    freqs = np.exp(np.float32(-np.log(10000.0)) * np.arange(pairs, dtype=np.float32) / pairs).astype(np.float32)
    ang = np.concatenate([(pos // 64).astype(np.float32)[:, None] * freqs, (pos % 64).astype(np.float32)[:, None] * freqs], -1)
    inv = (np.float32(10000.0) ** (-np.arange(HD // 2, dtype=np.float32) * np.float32(2.0) / HD)).astype(np.float32)
    ang2 = pos.astype(np.float32)[:, None] * inv[None, :]
    for name, a in (("cos1", np.cos(ang)), ("sin1", np.sin(ang)), ("cos2", np.cos(ang2)), ("sin2", np.sin(ang2))):
        put(name, a.reshape(HALVES, P, HD // 2).transpose(1, 0, 2))
    dist = pos[:, None] - pos[None, :]
    count = ((dist >= 0) & (dist <= 128)) * 1.0 + ((dist >= 0) & (dist % 4 == 0)) + ((dist >= 0) & (dist % 16 == 0))
    put("dil_count", count.reshape(HALVES, P, S).transpose(1, 0, 2))
    put("dil_neg", np.where(count > 0, 0.0, NEG).reshape(HALVES, P, S).transpose(1, 0, 2))
    mats, masks = [], []
    j, t = i[:, None], i[None, :]
    for b in (64, 32, 16, 8, 4, 2, 1):
        odd = (t // b) % 2 == 1
        start = (t // b) * b
        mats.append(np.where(odd, (j >= start) & (j <= t), (j > t) & (j < start + b)))
        masks.append((i[None, :] // b % 2 == 1) & (i[:, None] // b == i[None, :] // b - 1))
    mats += [j > t, j <= t]
    masks.append(np.eye(P))
    put("decay_sum", np.stack([m.astype(np.float32) for m in mats], 1))
    put("level_mask", np.stack([np.asarray(m, np.float32) for m in masks], 1))
    return np.ascontiguousarray(np.concatenate(parts, 1))


class Order:

    def __init__(self, head, group, tail, step0, pair0, tile0):
        self.parts, self.step0, self.pair0, self.tile0 = [head, group, tail], step0, pair0, tile0
        self.step, self.result, self.tile = {}, {}, {}
        steps, uses, tiles, n = 0, [0] * 4, 0, 0
        self.tiles = []
        self.size, self.use_size = [], []
        for part, items in enumerate(self.parts):
            s0, u0 = steps, list(uses)
            for name, new, tile in items:
                self.step[name] = (part, steps)
                if new:
                    self.result[new if isinstance(new, str) else name] = (part, n % 4, uses[n % 4])
                    uses[n % 4] += 1
                    n += 1
                if tile:
                    self.tile[name] = (part, tiles)
                    self.tiles.append((name, part, steps))
                    tiles += 1
                steps += 1
            self.size.append(steps - s0)
            self.use_size.append([a - b for a, b in zip(uses, u0)])
            if part == 1 and items:
                assert len({tuple(self.use_size[1])}) == 1 and n % 4 == 0, "a group uses every pair alike"
                self.group_steps, self.group_uses = self.size[1], list(self.use_size[1])
                steps += (GROUPS - 1) * self.size[1]
                uses = [a + (GROUPS - 1) * b for a, b in zip(uses, self.group_uses)]
                gt = [x for x in self.tiles if x[1] == 1]
                self.group_tiles = len(gt)
                self.head_tiles = tiles - self.group_tiles
                tiles += (GROUPS - 1) * self.group_tiles
        self.steps, self.uses = steps, uses
        self.layer_tiles = tiles + -tiles % SLOTS
        n_head = self.head_tiles if self.parts[1] else tiles
        used = list(range(tiles))
        self.slot_uses = [sum(p % SLOTS == s for p in used) for s in range(SLOTS)]
        self.position = {t[0]: p for p, t in enumerate(self.tiles)}
        self.n_tiles, self.n_head = tiles, n_head

    def done(self, l, name, g=0):
        part, i = self.step[name]
        return self.step0 + l * self.steps + i + 1 + (g * self.group_steps if part == 1 else 0)

    def slot(self, name):
        return self.position[name] % SLOTS

    def landings(self, l, name, g=0):
        p = self.position[name]
        k = sum(q % SLOTS == p % SLOTS for q in range(p))
        per_group = self.group_tiles // SLOTS if self.parts[1] else 0
        return 16 * (self.tile0[p % SLOTS] + l * self.slot_uses[p % SLOTS] + k + 1 + g * per_group)

    def slot_free(self, l, name, g=0):
        p = self.position[name]
        part = self.tiles[p][1]
        if part == 1 and p - SLOTS < self.n_head:
            return self.done(l, self.tiles[p - SLOTS + self.group_tiles][0], g - 1)
        if p >= SLOTS:
            return self.done(l, self.tiles[p - SLOTS][0], g)
        last = max(q for q in range(self.n_tiles) if q % SLOTS == p % SLOTS)
        if self.parts[1]:
            return self.done(l - 1, self.tiles[last - (GROUPS - 1) * self.group_tiles][0], GROUPS - 1)
        return self.done(l - 1, self.tiles[last][0])

    def pair(self, name):
        return self.result[name][1]

    def free(self, l, name, g=0):
        part, q, i = self.result[name]
        return 2 + 2 * (self.pair0[q] + l * self.uses[q] + i + (g * self.group_uses[q] if part == 1 else 0))


def mod_items(m):
    return [(f"m{m}_0", 1, 1), (f"m{m}_1", 0, 1)]


def head_one():
    def tiles(*names):
        return [(n, 1, 1) for n in names]

    def plain(*names):
        return [(n, 1, 0) for n in names]

    new = plain("T0a", "T0b") + tiles("in_q", "in_kv", "in_v", "in_u") + plain("ws", "qT", "kT", "S0", "S1", "mix")
    new += tiles("xk0") + plain("P0", "V0", "S2") + tiles("xk1") + plain("P1", "V1", "S3") + tiles("xv0")
    new += plain("P2", "P3", "V2", "V3") + tiles("xv1") + plain("Ma", "Mb") + tiles("out0", "out1")
    new += mod_items(0) + plain("T1a", "T1b", "mb0") + tiles("xq0", "xq1") + plain("XS0", "XS1")
    new += mod_items(4) + plain("XP0", "XP1", "mb4", "XOa", "XOb") + mod_items(1) + tiles("xo0") + plain("mb1")
    new += tiles("xo1") + mod_items(6) + plain("T2a", "T2b", "mb6", "route")
    new += mod_items(3) + plain("affT", "mb3") + mod_items(7) + plain("posT", "mb7", "gateT")
    return new


SPARE = 3
N_ROWS = 8
N_SMALL = 9


def group_one():
    items = [("gather", 1, 0)]
    for k in range(KT):
        items += [(f"g{k}", k == 0, 1), (f"u{k}", k == 0, 1)]
    items += [("midT", 1, 0)]
    items += [(f"d{k}", k == 0, 1) for k in range(KT)]
    items += [(f"spare{i}", i < 3, 0) for i in range(SPARE)]
    return items


def unit_items(name, units, result):
    return [(f"{name}/{u}" if u < units - 1 else name, result if u == 0 else 0, int(u == units - 1)) for u in range(units)]


def ffn_tiles(f):
    tiles = [(f"{f}{gu}{c}", n // P) for c, n in enumerate(FFC) for gu in "gu"]
    return tiles + [(f"{f}d{n}_{i}", nk // 2) for n in range(D // CHUNK) for i, (_, nk) in enumerate(DOWN)]


def ffn_items(f):
    items = []
    for name, units in ffn_tiles(f):
        result = name if "d" not in name or name.endswith("_0") else 0
        items += unit_items(name, units, result)
    return items


OUT_TILES = [("out0", 4), ("out1", 4)]
STRETCHES = [ffn_tiles("A"), OUT_TILES, ffn_tiles("B")]
UNITS = [(name, u, s, j) for s, tiles in enumerate(STRETCHES)
         for j, (name, u) in enumerate([(name, u) for name, n in tiles for u in range(n)])]


def unit_step(i):
    name, u, s, _ = UNITS[i]
    n = dict(STRETCHES[s])[name]
    return f"{name}/{u}" if u < n - 1 else name


def unit_before(i):
    own = UNITS[i][3] % BUFFERS
    earlier = [k for k in range(len(UNITS)) if UNITS[k][3] % BUFFERS == own]
    at = earlier.index(i)
    return earlier[at - 1], at == 0


def head_two():
    def tiles(*names):
        return [(n, 1, 1) for n in names]

    def plain(*names):
        return [(n, 1, 0) for n in names]

    items = mod_items(2) + plain("T0a", "T0b", "mb2") + ffn_items("A")
    items += mod_items(5) + plain("T1a", "T1b", "mb5")
    items += tiles("in_fh", "in_qka") + plain("SZ0", "SZ1") + tiles("in_qh") + plain("HL", "HE0", "HE1")
    items += tiles("in_vaqd") + plain("SC0", "SC1", "HS0", "HE2", "HS1", "HE3")
    items += tiles("in_kdvd") + plain("SV", "HS2", "HE4", "HS3", "HE5")
    items += tiles("in_ih") + plain("HS4", "HE6", "HS5", "HE7", "DT")
    items += tiles("in_gh") + plain("DS0", "DS1", "HS6", "HS7", "HD", "DP0", "DV0", "HO", "DP1", "DV1", "Ya", "Yb")
    for name, units in OUT_TILES:
        items += unit_items(name, units, name)
    items += mod_items(8) + plain("T2a", "T2b", "mb8") + ffn_items("B")
    return items


def place(j):
    return 2 * (j % 2) + j // 2


STEP0 = 512


def two_blocks(nc: bass.Bass, w, out):
    ones_order = Order([("G", 1, 0), ("T0a", 1, 0), ("T0b", 1, 0)], [], [], STEP0, [0] * 4, [0] * SLOTS)
    pre_steps = ones_order.steps
    one = Order(head_one(), group_one(), [("C0", 1, 0), ("C1", 1, 0)], STEP0 + pre_steps,
                [ones_order.uses[q] for q in range(4)], [0] * SLOTS)
    two = Order(head_two(), [], [], one.step0 + LAYERS * one.steps,
                [one.pair0[q] + LAYERS * one.uses[q] for q in range(4)], [LAYERS * n for n in one.slot_uses])

    with ExitStack() as ctx:
        def sb(name, shape):
            return ctx.enter_context(nc.sbuf_tensor(name, shape, F32))

        def over(name, shapes, words):
            with ExitStack() as inner:
                views = [inner.enter_context(nc.sbuf_tensor(n, shape, F32R)) for n, shape in shapes]
            assert sum(int(np.prod(shape[1:])) for _, shape in shapes) <= words
            return views + [sb(name, [P, words])]

        def sem(name):
            return ctx.enter_context(nc.semaphore(name))

        n_const = sum(n for _, n in CONSTS.values())
        consts = sb("consts", [P, n_const])

        def const(name, *dims):
            a, n = CONSTS[name]
            ap = consts[:, a:a + n]
            if len(dims) == 2:
                ap = ap.rearrange("p (a b) -> p a b", a=dims[0])
            return ap

        ident, ones = const("ident"), const("ones")
        ring = sb("ring", [P, SLOTS, KT * CHUNK])
        x = sb("x", [P, HALVES, D])
        xn = sb("xn", [P, HALVES, D])
        split2, hT_ = over("hT", [("split2", [P, 2, UNIT])], KT * S)
        hT = hT_[:, :].rearrange("p (k s) -> p k s", k=KT)
        hm_hi, hm_lo, split0, split1, work = over(
            "work", [("hm_hi", [P, FKT, S]), ("hm_lo", [P, FKT, S]), ("split0", [P, 2, UNIT]), ("split1", [P, 2, UNIT])], 15360)
        split = [split0, split1, split2]
        rows = sb("rows", [96, P])
        vectors = sb("vectors", [P, 96])
        g_mem, g_mix, g_xa, g_ffn, g_br, b_s, lbl, cT = (
            vectors[:, a:b] for a, b in ((0, 8), (8, 24), (24, 40), (40, 56), (56, 72), (72, 80), (80, 88), (88, 96)))
        hT_hi, hT_lo, shared = over("shared", [("hT_hi", [P, KT, S]), ("hT_lo", [P, KT, S])], 4096)
        w_s = shared[:, 0:1024].rearrange("p (l n) -> p l n", l=LAYERS)
        w_s_now = shared[:, 1024:1536]
        g_v = shared[:, 1536:2560].rearrange("p (l n) -> p l n", l=LAYERS)
        g_final = shared[:, 2560:3584]
        router = shared[:, 3584:3840].rearrange("p (k e) -> p k e", e=NE)
        g_q1, g_k1, g_q2, g_k2 = (sb(n, [P, LAYERS, HD]) for n in ("g_q1", "g_k1", "g_q2", "g_k2"))
        g_h = sb("g_h", [P, LAYERS, HK])
        lb_ln, lb_ln1m, lb_1m = (sb(n, [P, LAYERS * HH]) for n in ("lb_ln", "lb_ln1m", "lb_1m"))
        lbt, quarter = sb("lbt", [P, 4, HH]), sb("quarter", [P, LAYERS * HH])
        c32 = sb("c32", [P, KT, 32])
        bm_now = sb("bm_now", [2 * NMOD, CHUNK])
        part = sb("part", [P, 2, CHUNK])
        mcol = sb("mcol", [P, LAYERS * NMOD * KT])
        gate_b = sb("gate_b", [P, 3, D])
        eps = sb("eps", [P, 2])
        ss, ms, rstd = sb("ss", [P, 2]), sb("ms", [P, 2]), sb("rstd", [P, 2])
        mhalf = sb("mhalf", [P, 32])
        var, inv = sb("var", [P, 32]), sb("inv", [P, 32])
        smax, ssum, rsum = sb("smax", [P, 4, 4]), sb("ssum", [P, 4, 4]), sb("rsum", [P, 4, 4])
        nmax = sb("nmax", [P, 4, 4])
        small = sb("small", [P, 64])

        def cut(at, *dims):
            n = int(np.prod(dims))
            ap = work[:, at:at + n]
            if len(dims) == 2:
                return ap.rearrange("p (a b) -> p a b", a=dims[0])
            if len(dims) == 3:
                return ap.rearrange("p (a b c) -> p a b c", a=dims[0], b=dims[1])
            return ap

        memT = gate_b[:, 0:2, :].rearrange("p a b -> p (a b)").rearrange("p (k s) -> p k s", k=KT)
        ug, vg = cut(0, HALVES, GM), cut(1024, HALVES, GM)
        qk, vv = cut(2048, HALVES, 640), cut(3328, HALVES, KVH * HD)
        rq, kdup = cut(3584, HALVES, 640), cut(4864, HALVES, 256)
        t1, t2 = cut(5376, HALVES, 320), cut(6016, HALVES, 320)
        qkT = cut(5376, 6, S)
        pr, pTr = cut(6912, 2, 1024), cut(8960, 2, 1024)
        sq1 = cut(6912, 1280)
        kxT, vx = cut(11008, KT, S), cut(13056, HALVES, D)
        qxT, px, pxT, oxT = cut(0, KT, S), cut(2048, HALVES, 1024), cut(4096, XH, 2, S), cut(6912, KT, S)
        sel, selg = cut(0, HALVES, NE * CAP), cut(1024, HALVES, NE * CAP)
        gateT = cut(2048, GROUPS, HALVES, P)
        aw = [work[0:NE, 3072 + 256 * i:3328 + 256 * i] for i in range(6)]
        xsT, act_mid, mid, midT = cut(4608, KT, P), cut(5632, FF), cut(6656, FF), cut(7680, KT, P)
        ys = cut(8704, GROUPS, D)
        aff, posn = cut(12800, HALVES, NE), cut(12832, HALVES, NE)
        sg, tmp = xn, xn[:, :, 0:CHUNK]
        qkaT, dq, va_vd = cut(0, 4, S), cut(1024, HALVES, 512), cut(2048, HALVES, 512)
        dpT = cut(0, 2, 1024)
        qhT, lfT, khT = cut(3072, HH, S), cut(4096, HH, S), cut(5120, HH, S)
        dT = cut(4096, 4, S)
        ih, gh = cut(6144, HALVES, 512), cut(7168, HALVES, 512)
        fz, fa, fm, fs, fx, fd = (cut(8192 + 1024 * i, 1024) for i in range(6))
        he, hq, lfn = cut(8192, 2, 1024), cut(10240, 2, 1024), cut(12288, HALVES, 512)
        at_, at2 = cut(13312, 8, P), cut(14336, HH, P)
        ho, hsq = cut(8192, HALVES, 512), cut(9216, 1024)
        z_both, sp_both = shared[:, 0:1536], shared[:, 1536:3072]
        (z0, z1), (sp0, sp1) = ((t[:, 0:1024].rearrange("p (a b) -> p a b", a=4),
                                 t[:, 1024:1536].rearrange("p (a b) -> p a b", a=4)) for t in (z_both, sp_both))
        dr = shared[:, 3072:4096].rearrange("p (h n) -> p h n", h=HALVES)
        dp = shared[:, 0:2048].rearrange("p (h n) -> p h n", h=HALVES)
        dt1, dt2 = part[:, 0, :].rearrange("p (h n) -> p h n", h=HALVES), part[:, 1, :].rearrange("p (h n) -> p h n", h=HALVES)
        dsq = part[:, :, :].rearrange("p a b -> p (a b)")

        ps = [ctx.enter_context(nc.psum_tensor(f"ps{q}", [P, 2, CHUNK], F32)) for q in range(4)]

        load_i, load_c, load_x, load_m, load_r, load_p, stored = (
            sem(n) for n in ("load_i", "load_c", "load_x", "load_m", "load_r", "load_p", "stored"))
        landed = [sem(f"landed{i}") for i in range(SLOTS)]
        pe_step = sem("pe_step")
        pair_free = [sem(f"pair_free{q}") for q in range(4)]
        ss_ready, rstd_ready, xn_ready, x_ready = (sem(n) for n in ("ss_ready", "rstd_ready", "xn_ready", "x_ready"))
        var_ready, inv_ready, setup = sem("var_ready"), sem("inv_ready"), sem("setup")
        names = """ws_now v_ready rope_ready smax_ready merged xmax_ready xpn_ready rmax_ready aff_ready
        pos_ready sel_ready bm_ready c_ready c_silu lb_exp lb_sum lb_floor lb_root lb_log fab_ready flog fd_ready fl2 kh_ready
        sp_in st_log sp_ready w_arg w_exp dexp w_ready drope_ready dmax_ready dp_ready lf_ready hq_ready
        y_dve h_hi h_lo w_hi w_lo m_ready m_hi m_lo""".split()
        sm = {n: sem(n) for n in names}
        begin = ones_order

        def mcol_of(l, m, k, n=1):
            return mcol[:, bass.ds((l * NMOD + m) * KT + k, n)]

        def unit_source(eng, l, i):
            name, u, _, _ = UNITS[i]
            eng.wait_ge(landed[two.slot(name)], two.landings(l, name))
            at = ring[:, two.slot(name), :]
            if name[0] in "AB" and name[1] in "gu":
                n = P * dict(ffn_tiles(name[0]))[name]
                return at[:, 0:KT * n].rearrange("p (k n) -> p k n", n=n)[:, :, u * P:(u + 1) * P]
            return at[:, u * UNIT:(u + 1) * UNIT].rearrange("p (k n) -> p k n", n=CHUNK)

        def unit_part(i, part_, n):
            return split[UNITS[i][3] % BUFFERS][:, part_, :].rearrange("p (k n) -> p k n", n=n)

        def unit_range(name):
            return [i for i, unit in enumerate(UNITS) if unit[0] == name]

        def ahead(name):
            last = unit_range(name)[-1]
            return range(unit_range(name)[0] + BUFFERS, min(last + BUFFERS, stretch_end(last)) + 1)

        def stretch_end(i):
            return max(k for k, unit in enumerate(UNITS) if unit[2] == UNITS[i][2])

        block = ctx.enter_context(nc.Block())

        def read_out(eng, order, l, *names, g=0):
            for name in names:
                eng.wait_ge(pair_free[order.pair(name)], order.free(l, name, g) + 2)

        def finished(eng, order, l, name, g=0):
            eng.wait_ge(pe_step, order.done(l, name, g))

        @block.sync
        def _(sp):
            sp.dma_start(consts[:, 0:2 * P], w["consts"][:, 0:2 * P]).then_inc(load_i, 16)
            sp.dma_start(xn[:, :, :], w["mem"][0].rearrange("(h p) d -> p h d", p=P)).then_inc(load_m, 16)
            sp.dma_start(x[:, :, :], w["x"][0].rearrange("(h p) d -> p h d", p=P)).then_inc(load_x, 16)
            sp.wait_ge(load_r, 16 * N_ROWS)

            def tile(order, l, name, src, g=0):
                slot, cols = order.slot(name), src.shape[2]
                sp.wait_ge(pe_step, order.slot_free(l, name, g))
                sp.dma_start(ring[:, slot, 0:src.shape[1] * cols].rearrange("p (k n) -> p k n", n=cols),
                             src).then_inc(landed[slot], 16)

            def columns(name, l, c0, n, k0=0, nk=KT):
                return w[name][bass.ds(l, 1), k0 * P:(k0 + nk) * P, c0:c0 + n].rearrange("l (k p) n -> p (l k) n", p=P)

            def first_columns(name, l):
                rows_ = w[name].rearrange("l k n -> (l k) n")
                return rows_[bass.ds(l * D, D), 0:CHUNK].rearrange("(k p) n -> p k n", p=P)

            def mod_tiles(order, l, m):
                for i in range(2):
                    tile(order, l, f"m{m}_{i}", columns("w_mod_2", l, m * D + i * CHUNK, CHUNK))

            with sp.Fori(0, LAYERS) as l:
                for n, c0, width in (("in_q", 1024, 512), ("in_kv", 1536, 256), ("in_v", 512, 512), ("in_u", 0, 512)):
                    tile(one, l, n, columns("w_in", l, c0, width) if c0 else first_columns("w_in", l))
                for i, n in enumerate(("xk0", "xk1", "xv0", "xv1")):
                    tile(one, l, n, columns("xattn_w_kv", l, 512 * i, CHUNK))
                for i in range(2):
                    tile(one, l, f"out{i}", columns("w_out", l, 512 * i, CHUNK))
                mod_tiles(one, l, 0)
                for i in range(2):
                    tile(one, l, f"xq{i}", columns("xattn_w_q", l, 512 * i, CHUNK))
                mod_tiles(one, l, 4)
                mod_tiles(one, l, 1)
                for i in range(2):
                    tile(one, l, f"xo{i}", columns("xattn_w_o", l, 512 * i, CHUNK))
                for m in (6, 3, 7):
                    mod_tiles(one, l, m)
                with sp.Fori(0, GROUPS) as g:
                    def experts(name, k):
                        return w[name][bass.ds(l, 1), bass.ds(g * GROUP, GROUP), k * P:(k + 1) * P, :].rearrange(
                            "l e p n -> p (l e) n")
                    for k in range(KT):
                        tile(one, l, f"g{k}", experts("w_gate", k), g)
                        tile(one, l, f"u{k}", experts("w_up", k), g)
                    for k in range(KT):
                        tile(one, l, f"d{k}", experts("w_down", k), g)

            def stream_ffn(l, f, name):
                for c, n in enumerate(FFC):
                    tile(two, l, f"{f}g{c}", columns(name + "_w_gate_2", l, c * CHUNK, n))
                    tile(two, l, f"{f}u{c}", columns(name + "_w_up_2", l, c * CHUNK, n))
                for n in range(D // CHUNK):
                    for i, (k0, nk) in enumerate(DOWN):
                        tile(two, l, f"{f}d{n}_{i}", columns(name + "_w_down_2", l, n * CHUNK, CHUNK, k0, nk))

            finished(sp, one, LAYERS - 1, f"d{KT - 1}", GROUPS - 1)
            with sp.Fori(0, LAYERS) as l:
                mod_tiles(two, l, 2)
                stream_ffn(l, "A", "ffn1")
                mod_tiles(two, l, 5)
                for i, n in ((4, "in_fh"), (0, "in_qka"), (3, "in_qh"), (1, "in_vaqd"), (2, "in_kdvd"), (5, "in_ih"), (6, "in_gh")):
                    tile(two, l, n, columns("w_in_2", l, 512 * i, CHUNK) if i else first_columns("w_in_2", l))
                for i in range(2):
                    tile(two, l, f"out{i}", columns("w_out_2", l, 512 * i, CHUNK))
                mod_tiles(two, l, 8)
                stream_ffn(l, "B", "ffn2")
            sp.wait_ge(x_ready, 8 + 3 * LAYERS)
            sp.dma_start(out[0].rearrange("(h p) d -> p h d", p=P), x[:, :, :]).then_inc(stored, 16)
            sp.wait_ge(stored, 16)

        @block.tensor
        def _(pe):
            pe.sem_inc(pe_step, STEP0)
            for q in range(4):
                pe.sem_inc(pair_free[q], 2)

            def result(order, l, name, g=0):
                pe.wait_ge(pair_free[order.pair(name)], order.free(l, name, g))
                return ps[order.pair(name)]

            def weights(order, l, name, cols=CHUNK, g=0, nk=KT):
                pe.wait_ge(landed[order.slot(name)], order.landings(l, name, g))
                return ring[:, order.slot(name), 0:nk * cols].rearrange("p (k n) -> p k n", n=cols)

            def step(ins, n=1):
                ins.then_inc(pe_step, n)

            def transposes(order, l, name, pieces, width=P, g=0):
                ps_ = result(order, l, name, g)
                for src, m, bank, col in pieces:
                    rows = src.shape[0]
                    last = pe.transpose(ps_[0:m, bank, col:col + rows], src, ident[0:rows, 0:rows])
                step(last)

            def rows_to_hT(order, l, ab, src=xn):
                for i in range(2):
                    transposes(order, l, ab[i], [
                        (src[:, h, (4 * i + 2 * b + kk) * P:(4 * i + 2 * b + kk + 1) * P], P, b, kk * S + h * P)
                        for b in range(2) for kk in range(2) for h in range(HALVES)])

            def by_token(order, l, name, aT, cols=CHUNK, first=True):
                w_, ps_ = weights(order, l, name, cols), result(order, l, name)
                for h in range(HALVES):
                    for k in range(KT):
                        last = pe.matmul(ps_[:, h, 0:cols], aT[:, k, h * P:(h + 1) * P], w_[:, k, :],
                                         start=(k == 0), stop=(k == KT - 1))
                step(last)

            def by_feature(order, l, name, aT, cols=CHUNK):
                w_, ps_ = weights(order, l, name, cols), result(order, l, name)
                for b in range(cols // P):
                    for k in range(KT):
                        last = pe.matmul(ps_[:, b // 2, (b % 2) * S:(b % 2 + 1) * S], w_[:, k, b * P:(b + 1) * P],
                                         aT[:, k, :], start=(k == 0), stop=(k == KT - 1))
                step(last)

            def mod(order, l, m):
                for i in range(2):
                    w_ = weights(order, l, f"m{m}_{i}")
                    ps_ = result(order, l, f"m{m}_0") if i == 0 else ps_
                    for r in range(2):
                        for j in range(4):
                            k = 4 * r + j
                            last = pe.matmul(ps_[32 * j:32 * j + 32, i, :], c32[:, k, :], w_[:, k, :],
                                             start=(r == 0), stop=(r == 1))
                    step(last)

            def mod_sum(order, l, m):
                read_out(pe, order, l, f"m{m}_0")
                if m == 0:
                    pe.wait_ge(sm["bm_ready"], 16 * (l + 1))
                if m == 2:
                    pe.wait_ge(sm["bm_ready"], 16 * (LAYERS + l + 1))
                ps_ = result(order, l, f"mb{m}")
                for i in range(2):
                    u = 2 * m + i
                    if m % 3 == 2:
                        pe.matmul(ps_[:, i, :], ones, part[:, i, :], start=True, stop=False)
                        last = pe.matmul(ps_[:, i, :], ident[0:2 * NMOD, u:u + 1].broadcast_to([2 * NMOD, P]),
                                         bm_now[:, :], start=False, stop=True)
                    else:
                        for b in range(4):
                            c = 4 * i + b
                            pe.matmul(ps_[:, 0, c:c + 1], part[:, i, b * P:(b + 1) * P], ones[:, 0:1],
                                      start=True, stop=False)
                            last = pe.matmul(ps_[:, 0, c:c + 1], bm_now[:, b * P:(b + 1) * P],
                                             ident[0:2 * NMOD, u:u + 1], start=False, stop=True)
                step(last)

            pe.wait_ge(load_i, 16)
            pe.wait_ge(load_r, 16 * N_ROWS)
            transposes(begin, 0, "G", [(rows[:, :], P, 0, 0)])
            pe.wait_ge(xn_ready, 2)
            rows_to_hT(begin, 0, ("T0a", "T0b"))
            read_out(pe, begin, 0, "T0a", "T0b")

            with pe.Fori(0, LAYERS) as l:
                def norm_T(j, ab):
                    pe.wait_ge(xn_ready, 2 * (1 + 3 * l + j) + 2)
                    rows_to_hT(one, l, ab)
                    read_out(pe, one, l, *ab)

                norm_T(0, ("T0a", "T0b"))
                for n, cols in (("in_q", 512), ("in_kv", 256), ("in_v", 512), ("in_u", 512)):
                    by_token(one, l, n, hT, cols)
                pe.wait_ge(sm["ws_now"], l + 1)
                transposes(one, l, "ws", [(w_s_now[:, i * P:(i + 1) * P], P, 0, i * P) for i in range(4)])
                pe.wait_ge(sm["rope_ready"], l + 1)
                transposes(one, l, "qT", [(rq[:, h, b * P:(b + 1) * P], P, b // 2, (b % 2) * S + h * P)
                                          for b in range(4) for h in range(HALVES)])
                transposes(one, l, "kT", [(kdup[:, h, b * P:(b + 1) * P], P, 0, b * S + h * P)
                                          for b in range(KVH) for h in range(HALVES)])

                def att_scores(b):
                    h, hg = b // 2, b % 2
                    if b == 0:
                        read_out(pe, one, l, "qT", "kT")
                    ps_ = result(one, l, f"S{b}")
                    for j in range(4):
                        hd, at = 4 * hg + j, HD * (j % 2)
                        last = pe.matmul(ps_[:, j % 2, (j // 2) * S:(j // 2 + 1) * S],
                                         qkT[at:at + HD, hd // 2, h * P:(h + 1) * P],
                                         qkT[at:at + HD, 4 + hd // 4, :], start=True, stop=True)
                    step(last)

                def att_turn(b):
                    read_out(pe, one, l, f"S{b}")
                    transposes(one, l, f"P{b}", [(pr[:, b % 2, j * S + t * P:j * S + (t + 1) * P], P, j // 2, (j % 2) * S + t * P)
                                                 for j in range(4) for t in range(2)])

                def att_values(b):
                    hg = b % 2
                    read_out(pe, one, l, f"P{b}", *(["in_kv"] if b == 0 else []))
                    ps_ = result(one, l, f"V{b}")
                    for j in range(4):
                        for t in range(2):
                            last = pe.matmul(ps_[:, 0, j * HD:(j + 1) * HD],
                                             pTr[:, b % 2, j * S + t * P:j * S + (t + 1) * P],
                                             vv[:, t, hg * HD:(hg + 1) * HD], start=(t == 0), stop=(t == 1))
                    step(last)

                att_scores(0)
                att_scores(1)
                pe.wait_ge(sm["v_ready"], l + 1)
                read_out(pe, one, l, "ws")
                ps_ = result(one, l, "mix")
                for h in range(HALVES):
                    for i in range(4):
                        last = pe.matmul(ps_[:, h, i * P:(i + 1) * P], w_s_now[:, i * P:(i + 1) * P],
                                         vg[:, h, i * P:(i + 1) * P], start=True, stop=True)
                step(last)
                by_feature(one, l, "xk0", memT)
                att_turn(0)
                att_values(0)
                att_scores(2)
                by_feature(one, l, "xk1", memT)
                att_turn(1)
                att_values(1)
                att_scores(3)
                by_token(one, l, "xv0", memT)
                att_turn(2)
                att_turn(3)
                att_values(2)
                att_values(3)
                by_token(one, l, "xv1", memT)
                pe.wait_ge(sm["merged"], l + 1)
                rows_to_hT(one, l, ("Ma", "Mb"))
                read_out(pe, one, l, "Ma", "Mb")
                for n in ("out0", "out1"):
                    by_token(one, l, n, hT)
                pe.wait_ge(sm["c_ready"], 1)
                mod(one, l, 0)
                norm_T(1, ("T1a", "T1b"))
                mod_sum(one, l, 0)
                for n in ("xq0", "xq1"):
                    by_feature(one, l, n, hT)
                read_out(pe, one, l, "xq0", "xq1", "xk0", "xk1")
                for h in range(HALVES):
                    ps_ = result(one, l, f"XS{h}")
                    for j in range(XH):
                        for t in range(2):
                            last = pe.matmul(ps_[:, j // 2, (j % 2) * S:(j % 2 + 1) * S],
                                             qxT[:, 2 * j + t, h * P:(h + 1) * P], kxT[:, 2 * j + t, :],
                                             start=(t == 0), stop=(t == 1))
                    step(last)
                mod(one, l, 4)
                for h in range(HALVES):
                    pe.wait_ge(sm["xpn_ready"], 2 * l + h + 1)
                    transposes(one, l, f"XP{h}", [(px[:, h, j * S + t * P:j * S + (t + 1) * P], P, j // 2, (j % 2) * S + t * P)
                                                  for j in range(XH) for t in range(2)])
                mod_sum(one, l, 4)
                read_out(pe, one, l, "XP0", "XP1", "xv0", "xv1")
                for a in range(2):
                    ps_ = result(one, l, ("XOa", "XOb")[a])
                    for b in range(4):
                        d = 4 * a + b
                        for t in range(2):
                            last = pe.matmul(ps_[:, b // 2, (b % 2) * S:(b % 2 + 1) * S],
                                             vx[:, t, d * P:(d + 1) * P], pxT[:, d // 2, t, :],
                                             start=(t == 0), stop=(t == 1))
                    step(last)
                mod(one, l, 1)
                read_out(pe, one, l, "XOa", "XOb")
                by_token(one, l, "xo0", oxT)
                mod_sum(one, l, 1)
                by_token(one, l, "xo1", oxT)
                mod(one, l, 6)
                norm_T(2, ("T2a", "T2b"))
                mod_sum(one, l, 6)
                ps_ = result(one, l, "route")
                for h in range(HALVES):
                    for k in range(KT):
                        last = pe.matmul(ps_[:, 0, h * NE:(h + 1) * NE], hT[:, k, h * P:(h + 1) * P],
                                         router[:, bass.ds(l * KT + k, 1), :].rearrange("p a e -> p (a e)"),
                                         start=(k == 0), stop=(k == KT - 1))
                step(last)
                mod(one, l, 3)
                pe.wait_ge(sm["aff_ready"], l + 1)
                transposes(one, l, "affT", [(aff[:, h, :], NE, 0, h * P) for h in range(HALVES)])
                mod_sum(one, l, 3)
                mod(one, l, 7)
                pe.wait_ge(sm["pos_ready"], l + 1)
                ps_ = result(one, l, "posT")
                for h in range(HALVES):
                    last = pe.matmul(ps_[:, 0, h * NE:(h + 1) * NE], aw[5][:, h * P:(h + 1) * P], ident[0:NE, 0:NE],
                                     start=True, stop=True)
                step(last)
                mod_sum(one, l, 7)
                pe.wait_ge(sm["sel_ready"], l + 1)
                transposes(one, l, "gateT", [(selg[:, h, g * P:(g + 1) * P], P, g // 2, (g % 2) * S + h * P)
                                             for g in range(GROUPS) for h in range(HALVES)])
                with pe.Fori(0, GROUPS) as g:
                    ps_ = result(one, l, "gather", g)
                    for k in range(KT):
                        for h in range(HALVES):
                            last = pe.matmul(ps_[:, k // 4, (k % 4) * P:(k % 4 + 1) * P], xn[:, h, k * P:(k + 1) * P],
                                             sel[:, h, bass.ds(g * P, P)], start=(h == 0), stop=(h == 1))
                    step(last)
                    read_out(pe, one, l, "gather", g=g)

                    def experts(name, k, ps_, lhs, more=1):
                        w_ = weights(one, l, name, FF, g, GROUP)
                        for n in range(FF // CHUNK):
                            for e in range(GROUP):
                                last = pe.matmul(ps_[e * CAP:(e + 1) * CAP, n, :], lhs[:, k, e * CAP:(e + 1) * CAP],
                                                 w_[:, e, n * CHUNK:(n + 1) * CHUNK],
                                                 start=(k == 0), stop=(k == KT - 1))
                        step(last, more)

                    pg, pu = result(one, l, "g0", g), result(one, l, "u0", g)
                    for k in range(KT):
                        experts(f"g{k}", k, pg, xsT)
                        experts(f"u{k}", k, pu, xsT)
                    read_out(pe, one, l, "u0", g=g)
                    transposes(one, l, "midT", [(mid[:, k * P:(k + 1) * P], P, k // 4, (k % 4) * P) for k in range(KT)], g=g)
                    read_out(pe, one, l, "midT", g=g)
                    pd = result(one, l, "d0", g)
                    for k in range(KT):
                        experts(f"d{k}", k, pd, midT, 1 if k < KT - 1 else 1 + SPARE)
                    for i in range(3):
                        pe.sem_inc(pair_free[one.pair(f"spare{i}")], 2)
                read_out(pe, one, l, "gateT")
                read_out(pe, one, l, "d0", g=GROUPS - 1)
                for h in range(HALVES):
                    ps_ = result(one, l, f"C{h}")
                    for n in range(D // CHUNK):
                        for g in range(GROUPS):
                            last = pe.matmul(ps_[:, n, :], gateT[:, g, h, :], ys[:, g, n * CHUNK:(n + 1) * CHUNK],
                                             start=(g == 0), stop=(g == GROUPS - 1))
                    step(last)

            with pe.Fori(0, LAYERS) as l:
                def norm_T2(j, ab, m, h=None):
                    mod(two, l, m)
                    pe.wait_ge(xn_ready, 2 * (8 + 3 * l + j) + 2)
                    rows_to_hT(two, l, ab)
                    mod_sum(two, l, m)
                    if h is None:
                        read_out(pe, two, l, *ab)
                    else:
                        pe.wait_ge(sm["h_lo"], 2 * (3 * l + h) + 2)

                def unit(i):
                    pe.wait_ge(sm["w_lo"], l * len(UNITS) + i + 1)

                def parts(out_, w_hi, w_lo, a_hi, a_lo, first, last, weights_stationary):
                    for i, (w_, a_) in enumerate(((w_hi, a_hi), (w_hi, a_lo), (w_lo, a_hi))):
                        l_, r_ = (w_, a_) if weights_stationary else (a_, w_)
                        ins = pe.matmul(out_, l_, r_, start=first and i == 0, stop=last and i == 2)
                    return ins

                def features_by_parts(name):
                    ps_ = result(two, l, name)
                    for b, i in enumerate(unit_range(name)):
                        unit(i)
                        hi, lo = unit_part(i, 0, P), unit_part(i, 1, P)
                        for k in range(KT):
                            last = parts(ps_[:, b // 2, (b % 2) * S:(b % 2 + 1) * S], hi[:, k, :], lo[:, k, :],
                                         hT_hi[:, k, :], hT_lo[:, k, :], k == 0, k == KT - 1, True)
                        step(last)

                def tokens_by_parts(name, ps_, a_hi, a_lo, k0, of):
                    for u, i in enumerate(unit_range(name)):
                        unit(i)
                        hi, lo = unit_part(i, 0, CHUNK), unit_part(i, 1, CHUNK)
                        for h in range(HALVES):
                            for kk in range(2):
                                k, t = k0 + 2 * u + kk, slice(h * P, (h + 1) * P)
                                last = parts(ps_[:, h, :], hi[:, kk, :], lo[:, kk, :], a_hi[:, k, t], a_lo[:, k, t],
                                             k == 0, k == of - 1, False)
                        step(last)

                def ffn(f, j):
                    for c in range(len(FFC)):
                        features_by_parts(f"{f}g{c}")
                        features_by_parts(f"{f}u{c}")
                    for n in range(D // CHUNK):
                        ps_ = result(two, l, f"{f}d{n}_0")
                        for i, (k0, nk) in enumerate(DOWN):
                            pe.wait_ge(sm["m_lo"], (2 * l + j) * len(FFC) + -(-(k0 + nk) * P // CHUNK))
                            tokens_by_parts(f"{f}d{n}_{i}", ps_, hm_hi, hm_lo, k0, FKT)

                norm_T2(0, ("T0a", "T0b"), 2, 0)
                ffn("A", 0)
                norm_T2(1, ("T1a", "T1b"), 5)
                decay = const("decay_sum", LEVELS + 1, P)

                def decays(i):
                    ps_ = result(two, l, f"HE{i}")
                    for j in range(HH):
                        for h in range(HALVES):
                            m = i if i < LEVELS - 1 else i + h
                            last = pe.matmul(ps_[:, j // 2, (j % 2) * S + h * P:(j % 2) * S + (h + 1) * P],
                                             lfn[:, h, j * HK:(j + 1) * HK], decay[:, m, :], start=True, stop=True)
                    step(last)

                def level(i):
                    pe.wait_ge(sm["hq_ready"], LEVELS * l + i + 1)
                    q_ = hq[:, i % 2, :].rearrange("p (j s) -> p j s", j=HH)
                    ps_ = result(two, l, f"HS{i}")
                    if i < LEVELS - 1:
                        for j in range(HH):
                            for h in range(HALVES):
                                both = q_[:, j, h * P:(h + 1) * P]
                                last = pe.matmul(ps_[:, j // 2, (j % 2) * S + h * P:(j % 2) * S + (h + 1) * P],
                                                 both, both, start=True, stop=True)
                    else:
                        for j in range(HH):
                            last = pe.matmul(ps_[:, 0, j * P:(j + 1) * P], q_[:, j, 0:P], q_[:, j, P:S],
                                             start=True, stop=True)
                    step(last)

                def dilated_out(h):
                    pe.wait_ge(sm["dp_ready"], 2 * l + h + 1)
                    transposes(two, l, f"DP{h}", [(dp[:, h, j * S + t * P:j * S + (t + 1) * P], P, j // 2, (j % 2) * S + t * P)
                                                  for j in range(4) for t in range(2)])
                    read_out(pe, two, l, f"DP{h}", *(["in_kdvd"] if h == 0 else []))
                    ps_ = result(two, l, f"DV{h}")
                    for i in range(4):
                        j = place(i)
                        for t in range(2):
                            last = pe.matmul(ps_[:, 0, i * HD:(i + 1) * HD], dpT[:, h, i * S + t * P:i * S + (t + 1) * P],
                                             va_vd[:, t, 256 + j * HD:256 + (j + 1) * HD], start=(t == 0), stop=(t == 1))
                    step(last)

                by_feature(two, l, "in_fh", hT)
                by_feature(two, l, "in_qka", hT)
                read_out(pe, two, l, "in_qka")
                ps_ = result(two, l, "SZ0")
                for j in range(4):
                    at = HD * (j % 2)
                    last = pe.matmul(ps_[:, j % 2, (j // 2) * S:(j // 2 + 1) * S], qkaT[at:at + HD, 2 + j // 2, 0:P],
                                     qkaT[at:at + HD, j // 2, :], start=True, stop=True)
                step(last)
                ps_ = result(two, l, "SZ1")
                for j in range(4):
                    at = HD * (j % 2)
                    last = pe.matmul(ps_[:, j % 2, (j // 2) * P:(j // 2 + 1) * P], qkaT[at:at + HD, 2 + j // 2, P:S],
                                     qkaT[at:at + HD, j // 2, P:S], start=True, stop=True)
                step(last)
                by_feature(two, l, "in_qh", hT)
                pe.wait_ge(sm["lf_ready"], l + 1)
                transposes(two, l, "HL", [(lfT[:, j, h * P:(h + 1) * P], P, h, j * P) for h in range(HALVES) for j in range(HH)])
                read_out(pe, two, l, "HL")
                decays(0)
                decays(1)
                by_token(two, l, "in_vaqd", hT)
                pe.wait_ge(sm["sp_ready"], l + 1)
                ps_ = result(two, l, "SC0")
                for j in range(4):
                    bank, col = j // 2, (j % 2) * S
                    pe.matmul(ps_[:, bank, col:col + S], const("tri_ge"), sp0[:, j, :], start=True, stop=True)
                    last = pe.matmul(ps_[:, bank, col + P:col + S], ones, sp1[:, j, :], start=False, stop=True,
                                     skip_group_check=True)
                step(last)
                ps_ = result(two, l, "SC1")
                for j in range(4):
                    last = pe.matmul(ps_[:, 0, j * P:(j + 1) * P], const("tri_ge"), sp1[:, j, :], start=True, stop=True)
                step(last)
                level(0)
                decays(2)
                level(1)
                decays(3)
                by_token(two, l, "in_kdvd", hT)
                pe.wait_ge(sm["w_ready"], l + 1)
                read_out(pe, two, l, "in_vaqd")
                ps_ = result(two, l, "SV")
                for j in range(4):
                    cols = slice(j * HD, (j + 1) * HD)
                    i = place(j)
                    pe.matmul(ps_[:, 0, cols], z0[:, i, 0:P], va_vd[:, 0, cols], start=True, stop=True)
                    pe.matmul(ps_[:, 1, cols], z0[:, i, P:S], va_vd[:, 0, cols], start=True, stop=False)
                    last = pe.matmul(ps_[:, 1, cols], z1[:, i, :], va_vd[:, 1, cols], start=False, stop=True)
                step(last)
                level(2)
                decays(4)
                level(3)
                decays(5)
                by_token(two, l, "in_ih", hT)
                level(4)
                decays(6)
                level(5)
                decays(7)
                pe.wait_ge(sm["drope_ready"], l + 1)
                transposes(two, l, "DT", [(dr[:, h, b * P:(b + 1) * P], P, b // 2, (b % 2) * S + h * P)
                                          for b in range(4) for h in range(HALVES)])
                by_token(two, l, "in_gh", hT)
                read_out(pe, two, l, "DT")
                for h in range(HALVES):
                    ps_ = result(two, l, f"DS{h}")
                    for j in range(4):
                        at = HD * (j % 2)
                        last = pe.matmul(ps_[:, j % 2, (j // 2) * S:(j // 2 + 1) * S],
                                         dT[at:at + HD, j // 2, h * P:(h + 1) * P], dT[at:at + HD, 2 + j // 2, :],
                                         start=True, stop=True)
                    step(last)
                level(6)
                level(7)
                pe.wait_ge(sm["kh_ready"], l + 1)
                read_out(pe, two, l, "in_qh")
                ps_ = result(two, l, "HD")
                for j in range(HH):
                    for h in range(HALVES):
                        last = pe.matmul(ps_[:, j // 2, (j % 2) * S + h * P:(j % 2) * S + (h + 1) * P],
                                         khT[:, j, h * P:(h + 1) * P], qhT[:, j, h * P:(h + 1) * P], start=True, stop=True)
                step(last)
                dilated_out(0)
                read_out(pe, two, l, "HD", f"HS{LEVELS - 1}", "in_ih")
                ps_ = result(two, l, "HO")
                for j in range(HH):
                    cols = slice(j * HK, (j + 1) * HK)
                    pe.matmul(ps_[:, 0, cols], at_[:, 2 * j, :], ih[:, 0, cols], start=True, stop=True)
                    pe.matmul(ps_[:, 1, cols], at_[:, 2 * j + 1, :], ih[:, 1, cols], start=True, stop=False)
                    last = pe.matmul(ps_[:, 1, cols], at2[:, j, :], ih[:, 0, cols], start=False, stop=True)
                step(last)
                dilated_out(1)
                pe.wait_ge(sm["y_dve"], l + 1)
                read_out(pe, two, l, "SV")
                rows_to_hT(two, l, ("Ya", "Yb"))
                pe.wait_ge(sm["h_lo"], 2 * (3 * l + 1) + 2)
                for n in ("out0", "out1"):
                    tokens_by_parts(n, result(two, l, n), hT_hi, hT_lo, 0, KT)
                norm_T2(2, ("T2a", "T2b"), 8, 2)
                ffn("B", 1)

        @block.scalar
        def _(act):
            at = 0
            for n in ("mem_norm_g", "mix_norm_g", "xattn_norm_g", "ffn_norm_g", "branch_norm_g", "gm_b_s",
                      "hgrn_lb_logits_2", "c_2"):
                names = "abc"[:len(w[n].shape)]
                flat_ = w[n] if len(names) == 1 else w[n].rearrange(f"{' '.join(names)} -> ({' '.join(names)})")
                src = flat_.rearrange("(n p) -> n p", p=P)
                act.dma_start(rows[at:at + src.shape[0], :], src).then_inc(load_r, 16)
                at += src.shape[0]
            small_loads = [
                (g_q1[:, :, :], w["q_norm_g"].partition_broadcast(P)),
                (g_k1[:, :, :], w["k_norm_g"].partition_broadcast(P)),
                (g_v, w["gm_v_norm_g"].partition_broadcast(P)),
                (w_s, w["gm_w_s"].rearrange("l g i j -> i (l g) j").rearrange("i (l g) j -> i l g j", l=LAYERS)),
                (router, w["w_router"].rearrange("l (k p) e -> p (l k) e", p=P)),
                (g_final, w["final_norm_g"].partition_broadcast(P)),
                (g_q2[:, :, :], w["q_norm_g_2"].partition_broadcast(P)),
                (g_k2[:, :, :], w["k_norm_g_2"].partition_broadcast(P)),
                (g_h[:, :, :], w["hgrn_norm_g_2"].partition_broadcast(P)),
            ]
            assert len(small_loads) == N_SMALL
            act.dma_start(consts[:, 2 * P:], w["consts"][:, 2 * P:]).then_inc(load_c, 16)
            for dst, src in small_loads:
                if len(dst.shape) == 3 and len(src.shape) == 4:
                    dst = dst.rearrange("p l (g j) -> p l g j", g=4)
                act.dma_start(dst, src, allow_slow_non_contiguous=True).then_inc(load_p, 16)

            def squares(r, src, scratch):
                for h in range(HALVES):
                    last = act.activation(scratch[:, h, :], src[:, h, :], ACT.Square, scale=D ** -0.5,
                                          accum_out=ss[:, h:h + 1])
                last.then_inc(ss_ready, 1)

            def copy(order, l, name, dst, src, func=ACT.Copy, after=None, n=2, g=0, **kw):
                finished(act, order, l, after or name, g)
                act.activation(dst, src(ps[order.pair(name)]), func, **kw).then_inc(pair_free[order.pair(name)], n)

            def flat(p):
                return p[:, :, :].rearrange("p a b -> p (a b)")

            def second_bank(order, l, name, dst, after=None, g=0):
                copy(order, l, name, dst, lambda p: p[:, 1, :], after=after, n=1, g=g)

            def hT_bank(order, l, ab, scale, bias=None, dst=hT):
                for i in range(2):
                    finished(act, order, l, ab[i])
                    p = ps[order.pair(ab[i])]
                    for kk in range(2):
                        k = 4 * i + 2 + kk
                        if bias is None:
                            last = act.activation(dst[:, k, :], p[:, 1, kk * S:(kk + 1) * S], ACT.Copy, scale=scale(k))
                        else:
                            last = act.activation(dst[:, k, :], p[:, 1, kk * S:(kk + 1) * S], ACT.Identity,
                                                  scale=scale(k), bias=bias(k))
                    last.then_inc(pair_free[order.pair(ab[i])], 1)

            def exps(order, l, name, b, dst):
                scale = {"S": HD ** -0.5, "X": XD ** -0.5}[name[0]]
                p = flat(ps[order.pair(name)])
                for j in range(4):
                    last = act.activation(dst[:, j * S:(j + 1) * S], p[:, j * S:(j + 1) * S], ACT.Exp,
                                          bias=nmax[:, b, j:j + 1], scale=scale, accum_out=ssum[:, b, j:j + 1])
                last.then_inc(pair_free[order.pair(name)], 2)

            act.wait_ge(sm["lb_exp"], 1)
            act.activation(lbl[:, :], lbl[:, :], ACT.Exp).then_inc(sm["lb_sum"], 1)
            act.wait_ge(load_m, 16)
            squares(0, xn, cut(0, HALVES, D))
            hT_bank(begin, 0, ("T0a", "T0b"), lambda k: g_mem[:, k:k + 1], dst=memT)
            act.wait_ge(sm["c_silu"], 1)
            act.activation(c32[:, :, 0:1].rearrange("p k o -> p (k o)"), cT[:, :], ACT.Silu).then_inc(sm["c_ready"], 1)
            act.wait_ge(sm["lb_root"], 1)
            act.activation(lb_ln[:, :], lb_ln[:, :], ACT.Ln)
            act.activation(lb_ln1m[:, :], lb_1m[:, :], ACT.Ln).then_inc(sm["lb_log"], 1)

            def load_biases(l, order, last):
                finished(act, order, l - 1, last)
                act.dma_start(bm_now[:, :], w["b_mod_2"][bass.ds(l, 1), :].rearrange("l (u n) -> (l u) n", n=CHUNK)).then_inc(
                    sm["bm_ready"], 16)

            def mod(order, l, m, before):
                if before is not None:
                    finished(act, order, l, f"mb{before}")
                copy(order, l, f"m{m}_0", part[:, :, :], lambda p: p[:, :, :], after=f"m{m}_1")

            with act.Fori(0, LAYERS) as l:
                def norm(j, ab, gain, m=None, before=None):
                    act.wait_ge(x_ready, 1 + 3 * l + j)
                    squares(1 + 3 * l + j, x, xn)
                    if m is not None:
                        mod(one, l, m, before)
                    hT_bank(one, l, ab, lambda k: gain[:, bass.ds(l * KT + k, 1)])

                norm(0, ("T0a", "T0b"), g_mix)
                load_biases(l, one, "mb7")
                copy(one, l, "in_q", qk[:, :, 0:512], lambda p: p[:, :, :])
                finished(act, one, l, "in_kv")
                p = ps[one.pair("in_kv")]
                act.activation(qk[:, :, 512:640], p[:, :, 0:P], ACT.Copy)
                act.activation(vv[:, :, :], p[:, :, P:2 * P], ACT.Copy).then_inc(pair_free[one.pair("in_kv")], 2)
                copy(one, l, "in_v", vg[:, :, :], lambda p: p[:, :, :], ACT.Gelu_apprx_tanh)
                copy(one, l, "in_u", ug[:, :, :], lambda p: p[:, :, :], ACT.Gelu_apprx_tanh)
                copy(one, l, "ws", w_s_now, lambda p: p[:, 0, :])
                second_bank(one, l, "qT", qkT[:, 2:4, :].rearrange("p a b -> p (a b)"))
                copy(one, l, "kT", qkT[:, 4:6, :].rearrange("p a b -> p (a b)"), lambda p: p[:, 0, :])

                def keys(i):
                    copy(one, l, f"xk{i}", kxT[:, 4 * i:4 * i + 4, :].rearrange("p k s -> p (k s)"), flat)

                def values(i):
                    copy(one, l, f"xv{i}", vx[:, :, i * 512:(i + 1) * 512], lambda p: p[:, :, :])

                def att_exp(b):
                    act.wait_ge(sm["smax_ready"], 4 * l + b + 1)
                    exps(one, l, f"S{b}", b, pr[:, b % 2, :])

                def att_turn(b):
                    second_bank(one, l, f"P{b}", pTr[:, b % 2, 512:1024])

                att_exp(0)
                att_exp(1)
                keys(0)
                att_turn(0)
                att_exp(2)
                keys(1)
                att_turn(1)
                att_exp(3)
                values(0)
                att_turn(2)
                att_turn(3)
                values(1)
                hT_bank(one, l, ("Ma", "Mb"), lambda k: g_br[:, bass.ds(l * KT + k, 1)])
                norm(1, ("T1a", "T1b"), g_xa, 0)
                for i in range(2):
                    copy(one, l, f"xq{i}", qxT[:, 4 * i:4 * i + 4, :].rearrange("p k s -> p (k s)"), flat)
                for h in range(HALVES):
                    act.wait_ge(sm["xmax_ready"], 2 * l + h + 1)
                    exps(one, l, f"XS{h}", h, px[:, h, :])
                mod(one, l, 4, 0)
                for h in range(HALVES):
                    copy(one, l, f"XP{h}", pxT[:, 2:4, :, h * P:(h + 1) * P],
                         lambda p: p[:, 1, :].rearrange("p (j t q) -> p j t q", j=2, t=2), n=1)
                for i in range(2):
                    second_bank(one, l, ("XOa", "XOb")[i], oxT[:, 4 * i + 2:4 * i + 4, :].rearrange("p a b -> p (a b)"))
                mod(one, l, 1, 4)
                norm(2, ("T2a", "T2b"), g_ffn, 6, 1)
                act.wait_ge(sm["rmax_ready"], l + 1)
                p = ps[one.pair("route")]
                for h in range(HALVES):
                    last = act.activation(aff[:, h, :], p[:, 0, h * NE:(h + 1) * NE], ACT.Exp,
                                          bias=nmax[:, 0, h:h + 1], accum_out=ssum[:, 0, h:h + 1])
                last.then_inc(pair_free[one.pair("route")], 2)
                mod(one, l, 3, 6)
                mod(one, l, 7, 3)
                second_bank(one, l, "gateT", gateT[:, 2:4, :, :].rearrange("p g h t -> p (g h t)"))
                with act.Fori(0, GROUPS) as g:
                    copy(one, l, "g0", act_mid[:, :], flat, ACT.Silu, after=f"g{KT - 1}", g=g)
                    second_bank(one, l, "midT", midT[:, 4:8, :].rearrange("p a b -> p (a b)"), g=g)
                    copy(one, l, "d0", ys[:, bass.ds(g, 1), :].rearrange("p a d -> p (a d)"), flat, after=f"d{KT - 1}", g=g)
            act.wait_ge(x_ready, 1 + 3 * LAYERS)
            squares(1 + 3 * LAYERS, x, xn)

            finished(act, one, LAYERS - 1, "C1")
            with act.Fori(0, LAYERS) as l:
                def norm2(j, ab, m, before):
                    act.wait_ge(x_ready, 8 + 3 * l + j)
                    squares(8 + 3 * l + j, x, xn)
                    mod(two, l, m, before)
                    hT_bank(two, l, ab, lambda k: mcol_of(l, 3 * j + 1, k), lambda k: mcol_of(l, 3 * j, k))

                def high_parts(units):
                    for i in units:
                        if UNITS[i][3] == BUFFERS - 1:
                            h = UNITS[i][2]
                            act.wait_ge(sm["h_lo"], 2 * (3 * l + h) + 2)
                        k, wraps = unit_before(i)
                        finished(act, two, l - 1 if wraps else l, unit_step(k))
                        src = unit_source(act, l, i)
                        act.activation(unit_part(i, 0, src.shape[2]), src, ACT.Copy).then_inc(sm["w_hi"], 1)

                def high_hT(ab):
                    for i in range(2):
                        read_out(act, two, l, ab[i])
                        act.activation(hT_hi[:, 4 * i:4 * i + 4, :], hT[:, 4 * i:4 * i + 4, :], ACT.Copy).then_inc(sm["h_hi"], 1)

                def ffn(f, j):
                    for c, n in enumerate(FFC):
                        high_parts(ahead(f"{f}g{c}"))
                        if c >= 2:
                            act.wait_ge(sm["m_lo"], (2 * l + j) * len(FFC) + c - 1)
                        copy(two, l, f"{f}g{c}", sg[:, c % 2, 0:2 * n], lambda p: flat(p)[:, 0:2 * n], ACT.Silu)
                        high_parts(ahead(f"{f}u{c}"))
                        act.wait_ge(sm["m_ready"], (2 * l + j) * len(FFC) + c + 1)
                        act.activation(hm_hi[:, 4 * c:4 * c + n // P, :].rearrange("p a b -> p (a b)"),
                                       sg[:, c % 2, 0:2 * n], ACT.Copy).then_inc(sm["m_hi"], 1)
                    for n in range(D // CHUNK):
                        for i in range(len(DOWN)):
                            high_parts(ahead(f"{f}d{n}_{i}"))

                high_parts(unit_range("Ag0")[0:2])
                load_biases(l, two, "mb8")
                norm2(0, ("T0a", "T0b"), 2, None)
                high_hT(("T0a", "T0b"))
                high_parts(unit_range("Ag0")[2:BUFFERS])
                ffn("A", 0)
                norm2(1, ("T1a", "T1b"), 5, 2)
                def decays(i):
                    if i >= 2:
                        act.wait_ge(sm["hq_ready"], LEVELS * l + i - 1)
                    copy(two, l, f"HE{i}", he[:, i % 2, :], flat, ACT.Exp)

                def two_parts(name, dst_a, dst_b):
                    finished(act, two, l, name)
                    p = ps[two.pair(name)]
                    act.activation(dst_a, p[:, :, 0:256], ACT.Copy)
                    act.activation(dst_b, p[:, :, 256:512], ACT.Copy).then_inc(pair_free[two.pair(name)], 2)

                copy(two, l, "in_fh", fz, flat)
                act.wait_ge(sm["fab_ready"], l + 1)
                act.activation(fa, fa, ACT.Exp, scale=-1.0)
                act.drain()
                act.activation(fa, fa, ACT.Ln, bias=1.0).then_inc(sm["flog"], 1)
                copy(two, l, "in_qka", qkaT[:, :, :].rearrange("p a b -> p (a b)"), flat)
                act.wait_ge(sm["fd_ready"], l + 1)
                act.activation(fd, fd, ACT.Exp, scale=-1.0)
                act.activation(khT[:, :, :].rearrange("p a b -> p (a b)"), fs, ACT.Exp, scale=-1.0)
                act.drain()
                act.activation(fd, fd, ACT.Ln, bias=1.0).then_inc(sm["fl2"], 1)
                act.wait_ge(sm["sp_in"], l + 1)
                act.activation(sp_both, sp_both, ACT.Exp, scale=-1.0)
                act.drain()
                act.activation(sp_both, sp_both, ACT.Ln, bias=1.0).then_inc(sm["st_log"], 1)
                copy(two, l, "in_qh", qhT[:, :, :].rearrange("p a b -> p (a b)"), flat, ACT.Silu)
                copy(two, l, "HL", lfn[:, :, :], lambda p: p[:, :, :])
                decays(0)
                decays(1)
                two_parts("in_vaqd", va_vd[:, :, 0:256], dq[:, :, 0:256])
                act.wait_ge(sm["w_arg"], l + 1)
                act.activation(z_both, z_both, ACT.Exp).then_inc(sm["w_exp"], 1)
                decays(2)
                decays(3)
                two_parts("in_kdvd", dq[:, :, 256:512], va_vd[:, :, 256:512])
                copy(two, l, "SV", xn[:, :, 0:256], lambda p: p[:, :, 0:256])
                decays(4)
                decays(5)
                copy(two, l, "in_ih", ih[:, :, :], lambda p: p[:, :, :])
                decays(6)
                decays(7)
                second_bank(two, l, "DT", dT[:, 2:4, :].rearrange("p a b -> p (a b)"))
                copy(two, l, "in_gh", gh[:, :, :], lambda p: p[:, :, :], ACT.Silu)
                for h in range(HALVES):
                    act.wait_ge(sm["dmax_ready"], 2 * l + h + 1)
                    for j in range(4):
                        last = act.activation(dp[:, h, j * S:(j + 1) * S], dp[:, h, j * S:(j + 1) * S], ACT.Exp,
                                              bias=nmax[:, h, j:j + 1], scale=HD ** -0.5)
                    last.then_inc(sm["dexp"], 1)
                copy(two, l, f"HS{LEVELS - 1}", at2[:, :, :].rearrange("p a b -> p (a b)"), lambda p: p[:, 0, :])
                for h in range(HALVES):
                    second_bank(two, l, f"DP{h}", dpT[:, h, 512:1024])
                finished(act, two, l, "HO")
                high_parts(unit_range("out0")[0:2])
                for i in range(2):
                    second_bank(two, l, ("Ya", "Yb")[i], hT[:, 4 * i + 2:4 * i + 4, :].rearrange("p a b -> p (a b)"))
                high_hT(("Ya", "Yb"))
                high_parts(unit_range("out0")[2:BUFFERS])
                high_parts(ahead("out0"))
                high_parts(ahead("out1"))
                high_parts(unit_range("Bg0")[0:2])
                norm2(2, ("T2a", "T2b"), 8, 5)
                high_hT(("T2a", "T2b"))
                high_parts(unit_range("Bg0")[2:BUFFERS])
                ffn("B", 1)

        @block.gpsimd
        def _(pool):
            pool.memset(mhalf[:, :], -0.5)
            pool.memset(eps[:, :], EPS)
            pool.memset(quarter[:, :], 0.25)
            pool.memset(c32[:, :, :], 0.0).then_inc(sm["c_silu"], 1)

            def rms(r):
                pool.wait_ge(ss_ready, r + 1)
                pool.tensor_tensor(ms[:, :], ss[:, :], eps[:, :], ALU.add)
                pool.drain()
                pool.tensor_tensor(rstd[:, :], ms[:, :], mhalf[:, 0:2], ALU.pow).then_inc(rstd_ready, 1)

            def root(n, width):
                pool.wait_ge(var_ready, n + 1)
                pool.tensor_tensor(inv[:, 0:width], var[:, 0:width], mhalf[:, 0:width], ALU.pow).then_inc(inv_ready, 1)

            pool.drain()
            rms(0)
            pool.wait_ge(sm["lb_floor"], 1)
            pool.tensor_tensor(lb_ln[:, :], lb_ln[:, :], quarter[:, :], ALU.pow).then_inc(sm["lb_root"], 1)
            pool.wait_ge(load_p, 16 * N_SMALL)
            with pool.Fori(0, LAYERS) as l:
                finished(pool, one, l - 1, "mix")
                pool.tensor_copy(w_s_now, w_s[:, bass.ds(l, 1), :].rearrange("p a b -> p (a b)")).then_inc(sm["ws_now"], 1)
                rms(1 + 3 * l)
                root(3 * l, 20)
                root(3 * l + 1, 2)
                root(3 * l + 2, 4)
                rms(2 + 3 * l)
                rms(3 + 3 * l)
            rms(1 + 3 * LAYERS)
            with pool.Fori(0, LAYERS) as l:
                rms(8 + 3 * l)
                rms(9 + 3 * l)
                root(3 * LAYERS + 2 * l, 16)
                root(3 * LAYERS + 2 * l + 1, 8)
                rms(10 + 3 * l)

        @block.vector
        def _(v):
            def flat(p):
                return p[:, :, :].rearrange("p a b -> p (a b)")

            def free(order, name, ins, n=2):
                ins.then_inc(pair_free[order.pair(name)], n)

            def norm_rows(r, src):
                v.wait_ge(rstd_ready, r + 1)
                for h in range(HALVES):
                    last = v.tensor_scalar(xn[:, h, :], src[:, h, :], rstd[:, h:h + 1], None, ALU.mult)
                last.then_inc(xn_ready, 2)

            def hT_bank(order, l, ab, scale, bias=None, dst=hT):
                for i in range(2):
                    finished(v, order, l, ab[i])
                    p = ps[order.pair(ab[i])]
                    for kk in range(2):
                        k = 4 * i + kk
                        if bias is None:
                            last = v.tensor_scalar(dst[:, k, :], p[:, 0, kk * S:(kk + 1) * S], scale(k), None, ALU.mult)
                        else:
                            last = v.tensor_scalar(dst[:, k, :], p[:, 0, kk * S:(kk + 1) * S], scale(k), bias(k), ALU.mult, ALU.add)
                    free(order, ab[i], last, 1)

            def first_bank(order, l, name, dst, g=0):
                finished(v, order, l, name, g)
                free(order, name, v.tensor_copy(dst, ps[order.pair(name)][:, 0, :]), 1)

            def add_to_x(order, l, names, between=None):
                for i, n in enumerate(names):
                    finished(v, order, l, n)
                    cols = slice(i * CHUNK, (i + 1) * CHUNK)
                    free(order, n, v.tensor_tensor(x[:, :, cols], x[:, :, cols], ps[order.pair(n)][:, :, :], ALU.add))
                    if i == 0 and between is not None:
                        shift_or_scale(l, between)
                v.drain().then_inc(x_ready, 1)

            def add_gated(order, l, names, last_steps, gate):
                for i, n in enumerate(names):
                    finished(v, order, l, last_steps[i])
                    cols = slice(i * CHUNK, (i + 1) * CHUNK)
                    g_ = gate_b[:, gate:gate + 1, cols].broadcast_to([P, HALVES, CHUNK])
                    free(order, n, v.tensor_tensor(tmp[:, :, :], ps[order.pair(n)][:, :, :], g_, ALU.mult))
                    v.drain()
                    v.tensor_tensor(x[:, :, cols], x[:, :, cols], tmp[:, :, :], ALU.add)
                    v.drain()
                v.drain().then_inc(x_ready, 1)

            def inverse_root(n, width, count):
                v.drain()
                v.tensor_scalar(var[:, 0:count], var[:, 0:count], 1.0 / width, EPS, ALU.mult, ALU.add).then_inc(var_ready, 1)
                v.wait_ge(inv_ready, n + 1)

            def sum_squares(src, scratch, out_):
                v.tensor_tensor(scratch, src, src, ALU.mult)
                v.drain()
                v.tensor_reduce(out_, scratch, AX.X, ALU.add)

            def rope(dst, src, cos, sin, a, b, ta, tb):
                heads = src.shape[1]
                c = cos.rearrange("p (o n) -> p o n", o=1).broadcast_to([P, heads, HD // 2])
                s_ = sin.rearrange("p (o n) -> p o n", o=1).broadcast_to([P, heads, HD // 2])
                v.tensor_tensor(ta, a(src), c, ALU.mult)
                v.tensor_tensor(tb, b(src), s_, ALU.mult)
                v.drain()
                v.tensor_tensor(a(dst), ta, tb, ALU.subtract)
                v.drain()
                v.tensor_tensor(ta, a(src), s_, ALU.mult)
                v.tensor_tensor(tb, b(src), c, ALU.mult)
                v.drain()
                v.tensor_tensor(b(dst), ta, tb, ALU.add)
                v.drain()

            def by_place(r):
                return r.rearrange("p (b a o) -> p b a o", b=2, o=1).broadcast_to([P, 2, 2, HD])

            def row_max(order, l, name, b, scale, ready):
                finished(v, order, l, name)
                v.tensor_reduce(smax[:, b, :], flat(ps[order.pair(name)]).rearrange("p (j s) -> p j s", j=4), AX.X, ALU.max)
                v.drain()
                v.tensor_scalar(nmax[:, b, :], smax[:, b, :], -scale, None, ALU.mult).then_inc(ready, 1)

            finished(v, begin, 0, "G")
            free(begin, "G", v.tensor_copy(vectors[:, :], ps[begin.pair("G")][:, 0, 0:96]))
            v.drain()
            a0, a1 = lbl[:, 0:HH], lbl[:, HH:2 * HH]
            v.tensor_tensor(lbt[:, 0, :], a0, a1, ALU.max)
            v.drain()
            v.tensor_tensor(a0, a0, lbt[:, 0, :], ALU.subtract)
            v.tensor_tensor(a1, a1, lbt[:, 0, :], ALU.subtract).then_inc(sm["lb_exp"], 1)
            v.wait_ge(sm["lb_sum"], 1)
            v.tensor_tensor(lbt[:, 0, :], a0, a1, ALU.add)
            v.drain()
            v.reciprocal(lbt[:, 1, :], lbt[:, 0, :])
            v.drain()
            v.tensor_tensor(a0, a0, lbt[:, 1, :], ALU.mult)
            v.tensor_tensor(a1, a1, lbt[:, 1, :], ALU.mult)
            v.drain()
            v.tensor_tensor(lbt[:, 2, :], a0, a1, ALU.add)
            v.drain()
            v.tensor_tensor(lb_ln[:, 0:HH], a0, a0, ALU.subtract)
            v.tensor_tensor(lb_ln[:, HH:2 * HH], lbt[:, 2, :], a0, ALU.subtract)
            v.drain()
            v.tensor_scalar(lb_ln[:, :], lb_ln[:, :], 0.0, 1.0 - EPS, ALU.max, ALU.min)
            v.drain()
            v.tensor_scalar(lb_1m[:, :], lb_ln[:, :], -1.0, 1.0, ALU.mult, ALU.add)
            v.tensor_scalar(lb_ln[:, :], lb_ln[:, :], LB_FLOOR, None, ALU.max).then_inc(sm["lb_floor"], 1)
            norm_rows(0, xn)
            hT_bank(begin, 0, ("T0a", "T0b"), lambda k: g_mem[:, k:k + 1], dst=memT)
            v.wait_ge(load_x, 16)
            v.drain().then_inc(x_ready, 1)

            def shift_or_scale(l, m):
                finished(v, one, l, f"mb{m}")
                free(one, f"mb{m}", v.tensor_scalar(mcol_of(l, m, 0, KT), ps[one.pair(f"mb{m}")][:, 0, 0:KT],
                                                    1.0 if m % 3 else 0.0, None, ALU.add))

            with v.Fori(0, LAYERS) as l:
                def norm(j, ab, gain):
                    norm_rows(1 + 3 * l + j, x)
                    hT_bank(one, l, ab, lambda k: gain[:, bass.ds(l * KT + k, 1)])

                norm(0, ("T0a", "T0b"), g_mix)
                v.wait_ge(load_p, 16 * N_SMALL)
                v.wait_ge(load_c, 16)
                read_out(v, one, l, "in_q", "in_kv")
                heads = QH + KVH
                qk4 = qk[:, :, :].rearrange("p h (n d) -> p (h n) d", d=HD)
                sum_squares(qk4, sq1.rearrange("p (n d) -> p n d", d=HD), var[:, 0:2 * heads])
                inverse_root(3 * l, HD, 2 * heads)
                v.tensor_tensor(qk4, qk4, inv[:, 0:2 * heads].rearrange("p (n o) -> p n o", o=1).broadcast_to([P, 2 * heads, HD]), ALU.mult)
                v.drain()
                for h in range(HALVES):
                    q3, k3 = (qk[:, h, a:b].rearrange("p (n d) -> p n d", d=HD) for a, b in ((0, 512), (512, 640)))
                    v.tensor_tensor(q3, q3, g_q1[:, bass.ds(l, 1), :].broadcast_to([P, QH, HD]), ALU.mult)
                    v.tensor_tensor(k3, k3, g_k1[:, bass.ds(l, 1), :].broadcast_to([P, KVH, HD]), ALU.mult)
                v.drain()
                for h in range(HALVES):
                    rope(rq[:, h, :].rearrange("p (n d) -> p n d", d=HD), qk[:, h, :].rearrange("p (n d) -> p n d", d=HD),
                         const("cos1", 2, 32)[:, h, :], const("sin1", 2, 32)[:, h, :],
                         lambda t: t[:, :, 0:HD:2], lambda t: t[:, :, 1:HD:2],
                         t1[:, h, :].rearrange("p (n d) -> p n d", d=HD // 2), t2[:, h, :].rearrange("p (n d) -> p n d", d=HD // 2))
                for h in range(HALVES):
                    for j in range(KVH):
                        last = v.tensor_copy(kdup[:, h, j * P:(j + 1) * P].rearrange("p (n d) -> p n d", d=HD),
                                             rq[:, h, 512 + j * HD:512 + (j + 1) * HD].rearrange("p (o d) -> p o d", o=1).broadcast_to([P, 2, HD]))
                last.then_inc(sm["rope_ready"], 1)
                read_out(v, one, l, "in_v")
                sq_ = sq1[:, 0:1024].rearrange("p (h n) -> p h n", h=HALVES)
                sum_squares(vg[:, :, :], sq_, var[:, 0:2])
                inverse_root(3 * l + 1, GM, 2)
                for h in range(HALVES):
                    v.scalar_tensor_tensor(vg[:, h, :], vg[:, h, :], inv[:, h:h + 1],
                                           g_v[:, bass.ds(l, 1), :].rearrange("p a n -> p (a n)"), ALU.mult, ALU.mult)
                v.drain().then_inc(sm["v_ready"], 1)
                first_bank(one, l, "qT", qkT[:, 0:2, :].rearrange("p a b -> p (a b)"))

                def att_max(b):
                    row_max(one, l, f"S{b}", b, HD ** -0.5, sm["smax_ready"])

                def att_turn(b):
                    first_bank(one, l, f"P{b}", pTr[:, b % 2, 0:512])

                def att_out(b):
                    h, hg = b // 2, b % 2
                    read_out(v, one, l, f"S{b}")
                    v.reciprocal(rsum[:, b, :], ssum[:, b, :])
                    v.drain()
                    finished(v, one, l, f"V{b}")
                    free(one, f"V{b}", v.tensor_tensor(
                        xn[:, h, 512 + 256 * hg:768 + 256 * hg].rearrange("p (a b d) -> p b a d", b=2, d=HD),
                        ps[one.pair(f"V{b}")][:, 0, 0:256].rearrange("p (b a d) -> p b a d", b=2, d=HD),
                        by_place(rsum[:, b, :]), ALU.mult))

                att_max(0)
                att_max(1)
                read_out(v, one, l, "in_u")
                finished(v, one, l, "mix")
                for h in range(HALVES):
                    for i in range(4):
                        cols = slice(i * P, (i + 1) * P)
                        last = v.scalar_tensor_tensor(ug[:, h, cols], ps[one.pair("mix")][:, h, cols],
                                                      b_s[:, bass.ds(l * 4 + i, 1)], ug[:, h, cols], ALU.add, ALU.mult)
                free(one, "mix", last)
                att_turn(0)
                att_out(0)
                att_max(2)
                att_turn(1)
                att_out(1)
                att_max(3)
                att_turn(2)
                att_turn(3)
                att_out(2)
                att_out(3)
                v.drain()
                sum_squares(ug[:, :, :], qk[:, :, 0:512], var[:, 0:2])
                v.drain()
                sum_squares(xn[:, :, 512:1024], qk[:, :, 0:512], var[:, 2:4])
                inverse_root(3 * l + 2, GM, 4)
                for h in range(HALVES):
                    v.tensor_scalar(xn[:, h, 0:512], ug[:, h, :], inv[:, h:h + 1], None, ALU.mult)
                    v.tensor_scalar(xn[:, h, 512:1024], xn[:, h, 512:1024], inv[:, 2 + h:3 + h], None, ALU.mult)
                v.drain().then_inc(sm["merged"], 1)
                hT_bank(one, l, ("Ma", "Mb"), lambda k: g_br[:, bass.ds(l * KT + k, 1)])
                add_to_x(one, l, ("out0", "out1"))
                norm(1, ("T1a", "T1b"), g_xa)
                shift_or_scale(l, 0)
                for h in range(HALVES):
                    row_max(one, l, f"XS{h}", h, XD ** -0.5, sm["xmax_ready"])
                for h in range(HALVES):
                    read_out(v, one, l, f"XS{h}")
                    v.reciprocal(rsum[:, h, :], ssum[:, h, :])
                    v.drain()
                    for j in range(XH):
                        last = v.tensor_scalar(px[:, h, j * S:(j + 1) * S], px[:, h, j * S:(j + 1) * S],
                                               rsum[:, h, j:j + 1], None, ALU.mult)
                    last.then_inc(sm["xpn_ready"], 1)
                for h in range(HALVES):
                    finished(v, one, l, f"XP{h}")
                    free(one, f"XP{h}", v.tensor_copy(pxT[:, 0:2, :, h * P:(h + 1) * P],
                                                      ps[one.pair(f"XP{h}")][:, 0, :].rearrange("p (j t q) -> p j t q", j=2, t=2)), 1)
                shift_or_scale(l, 4)
                for i in range(2):
                    first_bank(one, l, ("XOa", "XOb")[i], oxT[:, 4 * i:4 * i + 2, :].rearrange("p a b -> p (a b)"))
                add_to_x(one, l, ("xo0", "xo1"), 1)
                norm(2, ("T2a", "T2b"), g_ffn)
                shift_or_scale(l, 6)
                finished(v, one, l, "route")
                v.tensor_reduce(smax[:, 0, 0:2], ps[one.pair("route")][:, 0, 0:2 * NE].rearrange("p (h e) -> p h e", h=2), AX.X, ALU.max)
                v.drain()
                v.tensor_scalar(nmax[:, 0, 0:2], smax[:, 0, 0:2], -1.0, None, ALU.mult).then_inc(sm["rmax_ready"], 1)
                read_out(v, one, l, "route")
                v.reciprocal(rsum[:, 0, 0:2], ssum[:, 0, 0:2])
                v.drain()
                v.tensor_tensor(aff[:, :, :], aff[:, :, :],
                                rsum[:, 0, 0:2].rearrange("p (n o) -> p n o", o=1).broadcast_to([P, HALVES, NE]), ALU.mult).then_inc(sm["aff_ready"], 1)
                finished(v, one, l, "affT")
                free(one, "affT", v.tensor_copy(aw[0], ps[one.pair("affT")][0:NE, 0, 0:S]))
                shift_or_scale(l, 3)
                v.drain()
                for i in range(CAP // 8):
                    src, dst = aw[i % 2], aw[(i + 1) % 2]
                    v.max(small[0:NE, 8 * i:8 * i + 8], src)
                    v.drain()
                    v.match_replace(dst, small[0:NE, 8 * i:8 * i + 8], src, -1.0)
                    v.drain()
                taken, ones_, count = aw[2], aw[3], aw[4]
                v.tensor_scalar(taken, aw[(CAP // 8) % 2], -1.0, None, ALU.is_equal)
                v.memset(ones_, 1.0)
                v.drain()
                v.tensor_tensor_scan(count, ones_, taken, 0.0, ALU.mult, ALU.add)
                v.drain()
                v.tensor_tensor(count, count, taken, ALU.mult)
                v.drain()
                v.tensor_scalar(aw[5], count, -1.0, None, ALU.add).then_inc(sm["pos_ready"], 1)
                finished(v, one, l, "posT")
                free(one, "posT", v.tensor_copy(posn[:, :, :], ps[one.pair("posT")][:, 0, 0:2 * NE].rearrange("p (h e) -> p h e", h=2)))
                v.drain()
                for h in range(HALVES):
                    v.tensor_tensor(sel[:, h, :].rearrange("p (e c) -> p e c", e=NE),
                                    posn[:, h, :].rearrange("p (e o) -> p e o", o=1).broadcast_to([P, NE, CAP]),
                                    const("iota", NE, CAP), ALU.is_equal)
                v.drain()
                for h in range(HALVES):
                    v.tensor_tensor(selg[:, h, :].rearrange("p (e c) -> p e c", e=NE), sel[:, h, :].rearrange("p (e c) -> p e c", e=NE),
                                    aff[:, h, :].rearrange("p (e o) -> p e o", o=1).broadcast_to([P, NE, CAP]), ALU.mult)
                v.drain().then_inc(sm["sel_ready"], 1)
                shift_or_scale(l, 7)
                first_bank(one, l, "gateT", gateT[:, 0:2, :, :].rearrange("p g h t -> p (g h t)"))
                with v.Fori(0, GROUPS) as g:
                    finished(v, one, l, "gather", g)
                    for b in range(2):
                        last = v.tensor_tensor(xsT[:, 4 * b:4 * b + 4, :], ps[one.pair("gather")][:, b, :].rearrange("p (k s) -> p k s", k=4),
                                               g_ffn[:, bass.ds(l * KT + 4 * b, 4)].rearrange("p (k o) -> p k o", o=1).broadcast_to([P, 4, P]), ALU.mult)
                    free(one, "gather", last)
                    read_out(v, one, l, "g0", g=g)
                    finished(v, one, l, f"u{KT - 1}", g)
                    free(one, "u0", v.tensor_tensor(mid[:, :], act_mid[:, :], flat(ps[one.pair("u0")]), ALU.mult))
                    first_bank(one, l, "midT", midT[:, 0:4, :].rearrange("p a b -> p (a b)"), g)
                for h in range(HALVES):
                    finished(v, one, l, f"C{h}")
                    free(one, f"C{h}", v.tensor_tensor(x[:, h, :], x[:, h, :], flat(ps[one.pair(f"C{h}")]), ALU.add))
                v.drain().then_inc(x_ready, 1)
            v.wait_ge(sm["lb_log"], 1)
            v.tensor_scalar(lb_ln[:, :], lb_ln[:, :], 4.0, None, ALU.mult)
            r = 1 + 3 * LAYERS
            v.wait_ge(rstd_ready, r + 1)
            for h in range(HALVES):
                v.scalar_tensor_tensor(x[:, h, :], x[:, h, :], rstd[:, h:h + 1], g_final[:, :], ALU.mult, ALU.mult)
            v.drain().then_inc(xn_ready, 2)
            v.drain().then_inc(x_ready, 1)

            with v.Fori(0, LAYERS) as l:
                def norm2(j, ab):
                    norm_rows(8 + 3 * l + j, x)
                    hT_bank(two, l, ab, lambda k: mcol_of(l, 3 * j + 1, k), lambda k: mcol_of(l, 3 * j, k))

                def mod(m):
                    finished(v, two, l, f"mb{m}")
                    free(two, f"mb{m}", v.tensor_scalar(gate_b[:, m // 3, :], flat(ps[two.pair(f"mb{m}")]),
                                                        1.0 if m == 5 else 0.5, None, ALU.mult))

                def low_parts(units):
                    for i in units:
                        v.wait_ge(sm["w_hi"], l * len(UNITS) + i + 1)
                        src = unit_source(v, l, i)
                        n = src.shape[2]
                        v.tensor_tensor(unit_part(i, 1, n), src, unit_part(i, 0, n).bitcast(F32), ALU.subtract).then_inc(sm["w_lo"], 1)

                def low_hT(h):
                    for i in range(2):
                        v.wait_ge(sm["h_hi"], 2 * (3 * l + h) + i + 1)
                        k = slice(4 * i, 4 * i + 4)
                        v.tensor_tensor(hT_lo[:, k, :], hT[:, k, :], hT_hi[:, k, :].bitcast(F32), ALU.subtract).then_inc(sm["h_lo"], 1)

                def ffn(f, j, gate):
                    for c, n in enumerate(FFC):
                        low_parts(ahead(f"{f}g{c}"))
                        low_parts(ahead(f"{f}u{c}"))
                        read_out(v, two, l, f"{f}g{c}")
                        finished(v, two, l, f"{f}u{c}")
                        m = sg[:, c % 2, 0:2 * n]
                        free(two, f"{f}u{c}", v.tensor_tensor(m, m, flat(ps[two.pair(f"{f}u{c}")])[:, 0:2 * n], ALU.mult))
                        v.drain().then_inc(sm["m_ready"], 1)
                        v.wait_ge(sm["m_hi"], (2 * l + j) * len(FFC) + c + 1)
                        hi, lo = (t[:, 4 * c:4 * c + n // P, :].rearrange("p a b -> p (a b)") for t in (hm_hi, hm_lo))
                        v.tensor_tensor(lo, m, hi.bitcast(F32), ALU.subtract).then_inc(sm["m_lo"], 1)
                    for n in range(D // CHUNK):
                        for i in range(len(DOWN)):
                            low_parts(ahead(f"{f}d{n}_{i}"))
                    v.drain()
                    add_gated(two, l, (f"{f}d0_0", f"{f}d1_0"), [f"{f}d{n}_{len(DOWN) - 1}" for n in range(2)], gate)

                low_parts(unit_range("Ag0")[0:2])
                norm2(0, ("T0a", "T0b"))
                low_hT(0)
                low_parts(unit_range("Ag0")[2:BUFFERS])
                mod(2)
                ffn("A", 0, 0)
                norm2(1, ("T1a", "T1b"))
                mod(5)
                read_out(v, two, l, "in_fh")
                v.scalar_tensor_tensor(fa, fz, -1.0, fz, ALU.mult, ALU.max).then_inc(sm["fab_ready"], 1)
                v.wait_ge(sm["flog"], l + 1)
                v.scalar_tensor_tensor(fm, fz, 0.0, fa, ALU.min, ALU.subtract)
                v.scalar_tensor_tensor(fs, fz, 0.0, fa, ALU.max, ALU.add)
                v.drain()
                for j in range(HH):
                    one_, ln_a, ln_b = (t[:, bass.ds(l * HH + j, 1)] for t in (lb_1m, lb_ln, lb_ln1m))
                    c = slice(j * S, (j + 1) * S)
                    v.tensor_scalar(fx[:, c], fm[:, c], ln_b, ln_a, ALU.add, ALU.max)
                    v.tensor_scalar(fd[:, c], fm[:, c], ln_b, ln_a, ALU.add, ALU.subtract)
                v.drain()
                v.scalar_tensor_tensor(fd, fd, -1.0, fd, ALU.mult, ALU.max).then_inc(sm["fd_ready"], 1)
                v.wait_ge(sm["fl2"], l + 1)
                v.tensor_tensor(lfT[:, :, :].rearrange("p a b -> p (a b)"), fx, fd, ALU.add)
                for j in range(HH):
                    v.tensor_scalar(khT[:, j, :], khT[:, j, :], lb_1m[:, bass.ds(l * HH + j, 1)], None, ALU.mult)
                v.drain().then_inc(sm["lf_ready"], 1)
                v.drain().then_inc(sm["kh_ready"], 1)
                def dilated_out(h):
                    first_bank(two, l, f"DP{h}", dpT[:, h, 0:512])
                    finished(v, two, l, f"DV{h}")
                    free(two, f"DV{h}", v.tensor_tensor(
                        xn[:, h, 256:512].rearrange("p (a b d) -> p b a d", b=2, d=HD),
                        ps[two.pair(f"DV{h}")][:, 0, 0:256].rearrange("p (b a d) -> p b a d", b=2, d=HD),
                        by_place(rsum[:, h, :]), ALU.mult))

                q_all, k_all = (t[:, :, :].rearrange("p a b -> p (a b)") for t in (qhT, khT))
                masks = const("level_mask", LEVELS, P).bitcast(U32)

                def products(i):
                    read_out(v, two, l, f"HE{i}", *(["in_qh"] if i == 0 else []))
                    b = 64 >> i if i < LEVELS - 1 else P
                    e_, o_, q_, k_ = (t.rearrange("p (n two b) -> p n two b", two=2, b=b)
                                      for t in (he[:, i % 2, :], hq[:, i % 2, :], q_all, k_all))
                    v.tensor_tensor(o_[:, :, 0, :], e_[:, :, 0, :], k_[:, :, 0, :], ALU.mult)
                    v.tensor_tensor(o_[:, :, 1, :], e_[:, :, 1, :], q_[:, :, 1, :], ALU.mult)
                    v.drain().then_inc(sm["hq_ready"], 1)

                def take(name, i):
                    finished(v, two, l, name)
                    free(two, name, v.copy_predicated(
                        at_[:, :, :], masks[:, i:i + 1, :].broadcast_to([P, 8, P]),
                        flat(ps[two.pair(name)]).rearrange("p (n t) -> p n t", n=8)))
                    v.drain()

                finished(v, two, l, "SZ0")
                free(two, "SZ0", v.tensor_scalar(z0[:, :, :].rearrange("p a b -> p (a b)"), flat(ps[two.pair("SZ0")]), HD ** -0.5, None, ALU.mult))
                finished(v, two, l, "SZ1")
                free(two, "SZ1", v.tensor_scalar(z1[:, :, :].rearrange("p (b a) q -> p b (a q)", b=2), ps[two.pair("SZ1")][:, :, 0:2 * P], HD ** -0.5, None, ALU.mult))
                v.drain()
                v.scalar_tensor_tensor(sp_both, z_both, -1.0, z_both, ALU.mult, ALU.max).then_inc(sm["sp_in"], 1)
                v.wait_ge(sm["st_log"], l + 1)
                v.scalar_tensor_tensor(sp_both, z_both, 0.0, sp_both, ALU.max, ALU.add)
                v.drain()
                before = const("key_before_query").rearrange("p (o q) -> p o q", o=1).broadcast_to([P, 4, P])
                v.tensor_tensor(sp0[:, :, 0:P], sp0[:, :, 0:P], before, ALU.mult)
                v.tensor_tensor(sp1[:, :, :], sp1[:, :, :], before, ALU.mult)
                v.drain().then_inc(sm["sp_ready"], 1)
                products(0)
                products(1)
                v.memset(at_[:, :, :], 0.0)
                v.drain()
                for name, z_ in (("SC0", z0), ("SC1", z1)):
                    finished(v, two, l, name)
                    zf = z_[:, :, :].rearrange("p a b -> p (a b)")
                    p = flat(ps[two.pair(name)])[:, 0:zf.shape[1]]
                    free(two, name, v.tensor_tensor(zf, zf, p, ALU.subtract))
                v.drain()
                v.tensor_scalar(z_both, z_both, 0.0, None, ALU.min).then_inc(sm["w_arg"], 1)
                take("HS0", 0)
                products(2)
                v.wait_ge(sm["w_exp"], l + 1)
                v.tensor_tensor(z0[:, :, 0:P], z0[:, :, 0:P], before, ALU.mult)
                v.tensor_tensor(z1[:, :, :], z1[:, :, :], before, ALU.mult)
                v.drain().then_inc(sm["w_ready"], 1)
                take("HS1", 1)
                products(3)
                take("HS2", 2)
                products(4)
                take("HS3", 3)
                products(5)
                read_out(v, two, l, "in_vaqd", "in_kdvd")
                dq4 = dq[:, :, :].rearrange("p h (n d) -> p (h n) d", d=HD)
                sum_squares(dq4, dsq.rearrange("p (n d) -> p n d", d=HD), var[:, 0:16])
                inverse_root(3 * LAYERS + 2 * l, HD, 16)
                v.tensor_tensor(dq4, dq4, inv[:, 0:16].rearrange("p (n o) -> p n o", o=1).broadcast_to([P, 16, HD]), ALU.mult)
                v.drain()
                for h in range(HALVES):
                    for a, gain in ((0, g_q2), (256, g_k2)):
                        t3 = dq[:, h, a:a + 256].rearrange("p (n d) -> p n d", d=HD)
                        v.tensor_tensor(t3, t3, gain[:, bass.ds(l, 1), :].broadcast_to([P, 4, HD]), ALU.mult)
                v.drain()
                for h in range(HALVES):
                    rope(dr[:, h, :].rearrange("p (n d) -> p n d", d=HD), dq[:, h, :].rearrange("p (n d) -> p n d", d=HD),
                         const("cos2", 2, 32)[:, h, :], const("sin2", 2, 32)[:, h, :],
                         lambda t: t[:, :, 0:HD // 2], lambda t: t[:, :, HD // 2:HD],
                         dt1[:, h, :].rearrange("p (n d) -> p n d", d=HD // 2), dt2[:, h, :].rearrange("p (n d) -> p n d", d=HD // 2))
                v.drain().then_inc(sm["drope_ready"], 1)
                take("HS4", 4)
                products(6)
                take("HS5", 5)
                products(7)
                first_bank(two, l, "DT", dT[:, 0:2, :].rearrange("p a b -> p (a b)"))
                finished(v, two, l, "SV")
                for h in range(HALVES):
                    finished(v, two, l, f"DS{h}")
                    d3 = dp[:, h, :].rearrange("p (j s) -> p j s", j=4)
                    neg = const("dil_neg", HALVES, S)[:, h:h + 1, :].broadcast_to([P, 4, S])
                    free(two, f"DS{h}", v.tensor_tensor(d3, flat(ps[two.pair(f"DS{h}")]).rearrange("p (j s) -> p j s", j=4), neg, ALU.add))
                    v.drain()
                    v.tensor_reduce(smax[:, h, :], d3, AX.X, ALU.max)
                    v.drain()
                    v.tensor_scalar(nmax[:, h, :], smax[:, h, :], -HD ** -0.5, None, ALU.mult).then_inc(sm["dmax_ready"], 1)
                take("HS6", 6)
                for h in range(HALVES):
                    v.wait_ge(sm["dexp"], 2 * l + h + 1)
                    d3 = dp[:, h, :].rearrange("p (j s) -> p j s", j=4)
                    v.tensor_tensor(d3, d3, const("dil_count", HALVES, S)[:, h:h + 1, :].broadcast_to([P, 4, S]), ALU.mult)
                    v.drain().then_inc(sm["dp_ready"], 1)
                    v.tensor_reduce(ssum[:, h, :], d3, AX.X, ALU.add)
                    v.drain()
                    v.reciprocal(rsum[:, h, :], ssum[:, h, :])
                    v.drain()
                take("HD", LEVELS - 1)
                dilated_out(0)
                finished(v, two, l, "HO")
                free(two, "HO", v.tensor_copy(ho[:, :, :], ps[two.pair("HO")][:, :, :]))
                v.drain()
                ho4 = ho[:, :, :].rearrange("p h (n d) -> p (h n) d", d=HK)
                sum_squares(ho4, hsq.rearrange("p (n d) -> p n d", d=HK), var[:, 0:8])
                inverse_root(3 * LAYERS + 2 * l + 1, HK, 8)
                v.tensor_tensor(ho4, ho4, inv[:, 0:8].rearrange("p (n o) -> p n o", o=1).broadcast_to([P, 8, HK]), ALU.mult)
                v.drain()
                v.tensor_tensor(ho4, ho4, g_h[:, bass.ds(l, 1), :].broadcast_to([P, 8, HK]), ALU.mult)
                v.drain()
                dilated_out(1)
                read_out(v, two, l, "in_gh")
                v.tensor_tensor(xn[:, :, 512:1024], ho[:, :, :], gh[:, :, :], ALU.mult).then_inc(sm["y_dve"], 1)
                for i in range(2):
                    first_bank(two, l, ("Ya", "Yb")[i], hT[:, 4 * i:4 * i + 2, :].rearrange("p a b -> p (a b)"))
                low_parts(unit_range("out0")[0:2])
                low_hT(1)
                low_parts(unit_range("out0")[2:BUFFERS])
                low_parts(ahead("out0"))
                low_parts(ahead("out1"))
                add_gated(two, l, ("out0", "out1"), ("out0", "out1"), 1)
                low_parts(unit_range("Bg0")[0:2])
                norm2(2, ("T2a", "T2b"))
                low_hT(2)
                low_parts(unit_range("Bg0")[2:BUFFERS])
                mod(8)
                ffn("B", 1, 2)


_INS = ["x", "mem", "mix_norm_g", "w_in", "gm_v_norm_g", "gm_w_s", "gm_b_s", "q_norm_g", "k_norm_g", "branch_norm_g",
        "w_out", "xattn_norm_g", "mem_norm_g", "xattn_w_q", "xattn_w_kv", "xattn_w_o", "ffn_norm_g", "w_router",
        "w_gate", "w_up", "w_down", "final_norm_g", "c_2", "w_mod_2", "b_mod_2", "ffn1_w_gate_2", "ffn1_w_up_2",
        "ffn1_w_down_2", "w_in_2", "w_out_2", "q_norm_g_2", "k_norm_g_2", "hgrn_norm_g_2", "hgrn_lb_logits_2",
        "ffn2_w_gate_2", "ffn2_w_up_2", "ffn2_w_down_2"]


def kernel(**inputs):
    import concourse.bacc as bacc
    from concourse.bass_utils import run_bass_kernel_spmd

    nc = bacc.Bacc("TRN2", target_bir_lowering=False, num_devices=1)
    arrays, w = {}, {}
    for name in _INS + ["consts"]:
        a = constant_table() if name == "consts" else np.ascontiguousarray(inputs[name])
        arrays[f"in_{name}"] = a
        w[name] = nc.dram_tensor(f"in_{name}", a.shape, mybir.dt.from_np(a.dtype), kind="ExternalInput").ap()
    out = nc.dram_tensor("out_0", (1, S, D), F32, kind="ExternalOutput").ap()
    two_blocks(nc, w, out)
    r = run_bass_kernel_spmd(nc, [arrays], core_ids=[0])
    return r.results[0]["out_0"]
```

```python
from contextlib import ExitStack

import numpy as np

import concourse.bass as bass
from concourse import mybir

F32 = mybir.dt.float32
F32R = mybir.dt.float32r
U32 = mybir.dt.uint32
ALU = mybir.AluOpType
ACT = mybir.ActivationFunctionType
AX = mybir.AxisListType

P = 128
D = 1024
KT = D // P
S = 256
HALVES = S // P
LAYERS = 2
EPS = 1e-6
GM = 512
HD = 64
QH, KVH = 8, 2
XH, XD = 4, 256
NE, FF = 16, 1024
CAP = 2 * S // NE
GROUP = P // CAP
GROUPS = NE // GROUP
DFF = 2816
NMOD = 9
HH, HK = 4, 128
LB_FLOOR = 1e-30
NEG = -1e30
SLOTS = 4
SKIP = 2
CHUNK = 512
FFC = [min(CHUNK, DFF - c) for c in range(0, DFF, CHUNK)]
FKT = DFF // P
DOWN = [(k, min(KT, FKT - k)) for k in range(0, FKT, KT)]
UNIT = 1024
BUFFERS = 3
LEVELS = 8


CONSTS = {}


def constant_table():
    parts, at = [], 0

    def put(name, a):
        nonlocal at
        a = np.asarray(a, np.float32).reshape(P, -1)
        CONSTS[name] = (at, a.shape[1])
        parts.append(a)
        at += a.shape[1]

    i = np.arange(P)
    put("ident", np.eye(P))
    put("ones", np.ones((P, P)))
    put("iota", np.tile(np.arange(CAP), (P, NE)))
    put("tri_ge", i[:, None] >= i[None, :])
    put("key_before_query", i[:, None] < i[None, :])
    pos = np.arange(S)
    pairs = HD // 4
    freqs = np.exp(np.float32(-np.log(10000.0)) * np.arange(pairs, dtype=np.float32) / pairs).astype(np.float32)
    ang = np.concatenate([(pos // 64).astype(np.float32)[:, None] * freqs, (pos % 64).astype(np.float32)[:, None] * freqs], -1)
    inv = (np.float32(10000.0) ** (-np.arange(HD // 2, dtype=np.float32) * np.float32(2.0) / HD)).astype(np.float32)
    ang2 = pos.astype(np.float32)[:, None] * inv[None, :]
    for name, a in (("cos1", np.cos(ang)), ("sin1", np.sin(ang)), ("cos2", np.cos(ang2)), ("sin2", np.sin(ang2))):
        put(name, a.reshape(HALVES, P, HD // 2).transpose(1, 0, 2))
    dist = pos[:, None] - pos[None, :]
    count = ((dist >= 0) & (dist <= 128)) * 1.0 + ((dist >= 0) & (dist % 4 == 0)) + ((dist >= 0) & (dist % 16 == 0))
    put("dil_count", count.reshape(HALVES, P, S).transpose(1, 0, 2))
    put("dil_neg", np.where(count > 0, 0.0, NEG).reshape(HALVES, P, S).transpose(1, 0, 2))
    mats, masks = [], []
    j, t = i[:, None], i[None, :]
    for b in (64, 32, 16, 8, 4, 2, 1):
        odd = (t // b) % 2 == 1
        start = (t // b) * b
        mats.append(np.where(odd, (j >= start) & (j <= t), (j > t) & (j < start + b)))
        masks.append((i[None, :] // b % 2 == 1) & (i[:, None] // b == i[None, :] // b - 1))
    mats += [j > t, j <= t]
    masks.append(np.eye(P))
    put("decay_sum", np.stack([m.astype(np.float32) for m in mats], 1))
    put("level_mask", np.stack([np.asarray(m, np.float32) for m in masks], 1))
    return np.ascontiguousarray(np.concatenate(parts, 1))


class Order:

    def __init__(self, head, group, tail, step0, pair0, tile0):
        self.parts, self.step0, self.pair0, self.tile0 = [head, group, tail], step0, pair0, tile0
        self.step, self.result, self.tile = {}, {}, {}
        steps, uses, tiles, n = 0, [0] * 4, 0, 0
        self.tiles = []
        self.size, self.use_size = [], []
        for part, items in enumerate(self.parts):
            s0, u0 = steps, list(uses)
            for name, new, tile in items:
                self.step[name] = (part, steps)
                if new:
                    self.result[new if isinstance(new, str) else name] = (part, n % 4, uses[n % 4])
                    uses[n % 4] += 1
                    n += 1
                if tile == SKIP:
                    self.tiles.append((None, part, steps))
                    tiles += 1
                if tile:
                    self.tile[name] = (part, tiles)
                    self.tiles.append((name, part, steps))
                    tiles += 1
                steps += 1
            self.size.append(steps - s0)
            self.use_size.append([a - b for a, b in zip(uses, u0)])
            if part == 1 and items:
                assert len({tuple(self.use_size[1])}) == 1 and n % 4 == 0, "a group uses every pair alike"
                self.group_steps, self.group_uses = self.size[1], list(self.use_size[1])
                steps += (GROUPS - 1) * self.size[1]
                uses = [a + (GROUPS - 1) * b for a, b in zip(uses, self.group_uses)]
                gt = [x for x in self.tiles if x[1] == 1]
                self.group_tiles = len(gt)
                self.head_tiles = tiles - self.group_tiles
                tiles += (GROUPS - 1) * self.group_tiles
        self.steps, self.uses = steps, uses
        self.layer_tiles = tiles + -tiles % SLOTS
        n_head = self.head_tiles if self.parts[1] else tiles
        used = [p for p in range(tiles) if p >= len(self.tiles) or self.tiles[p][0]]
        self.slot_uses = [sum(p % SLOTS == s for p in used) for s in range(SLOTS)]
        self.position = {t[0]: p for p, t in enumerate(self.tiles)}
        self.n_tiles, self.n_head = tiles, n_head

    def done(self, l, name, g=0):
        part, i = self.step[name]
        return self.step0 + l * self.steps + i + 1 + (g * self.group_steps if part == 1 else 0)

    def slot(self, name):
        return self.position[name] % SLOTS

    def landings(self, l, name, g=0):
        p = self.position[name]
        k = sum(q % SLOTS == p % SLOTS and self.tiles[q][0] is not None for q in range(p))
        per_group = self.group_tiles // SLOTS if self.parts[1] else 0
        return 16 * (self.tile0[p % SLOTS] + l * self.slot_uses[p % SLOTS] + k + 1 + g * per_group)

    def slot_free(self, l, name, g=0):
        p = self.position[name]
        part = self.tiles[p][1]
        if part == 1 and p - SLOTS < self.n_head:
            return self.done(l, self.tiles[p - SLOTS + self.group_tiles][0], g - 1)
        if p >= SLOTS:
            before = p - SLOTS if self.tiles[p - SLOTS][0] else p - 2 * SLOTS
            return self.done(l, self.tiles[before][0], g)
        last = max(q for q in range(self.n_tiles) if q % SLOTS == p % SLOTS)
        if self.parts[1]:
            return self.done(l - 1, self.tiles[last - (GROUPS - 1) * self.group_tiles][0], GROUPS - 1)
        return self.done(l - 1, self.tiles[last][0])

    def pair(self, name):
        return self.result[name][1]

    def free(self, l, name, g=0):
        part, q, i = self.result[name]
        return 2 + 2 * (self.pair0[q] + l * self.uses[q] + i + (g * self.group_uses[q] if part == 1 else 0))


def unit_items(name, units, result):
    return [(f"{name}/{u}" if u < units - 1 else name, result if u == 0 else 0, int(u == units - 1)) for u in range(units)]


def ffn_tiles(f):
    tiles = [(f"{f}{gu}{c}", n // P) for c, n in enumerate(FFC) for gu in "gu"]
    return tiles + [(f"{f}d{n}_{i}", nk // 2) for n in range(D // CHUNK) for i, (_, nk) in enumerate(DOWN)]


OUT_TILES = [("out0", 4), ("out1", 4)]
XQ_TILES = [("xq0", 4), ("xq1", 4)]
XO_TILES = [("xo0", 4), ("xo1", 4)]


class Units:

    def __init__(self, stretches, count0, h0):
        self.units = [(name, i, s) for s, tiles in enumerate(stretches) for name, n in tiles for i in range(n)]
        self.number = [i - min(k for k, u in enumerate(self.units) if u[2] == unit[2]) for i, unit in enumerate(self.units)]
        self.tiles = {name: n for tiles in stretches for name, n in tiles}
        self.stretches, self.count0, self.h0 = len(stretches), count0, h0

    def buffer(self, i):
        return self.number[i] % BUFFERS

    def of(self, name):
        return [i for i, unit in enumerate(self.units) if unit[0] == name]

    def step(self, i):
        name, u, _ = self.units[i]
        return f"{name}/{u}" if u < self.tiles[name] - 1 else name

    def before(self, i):
        same = [k for k in range(len(self.units)) if self.buffer(k) == self.buffer(i)]
        at = same.index(i)
        return same[at - 1], at == 0

    def ahead(self, name):
        first, last = self.of(name)[0], self.of(name)[-1]
        end = max(k for k, unit in enumerate(self.units) if unit[2] == self.units[last][2])
        return range(first + BUFFERS, min(last + BUFFERS, end) + 1)

    def counts(self, l, i):
        return self.count0 + l * len(self.units) + i + 1

    def halves(self, l, s, i=1):
        return self.h0 + 2 * (self.stretches * l + s) + i + 1


UNITS_ONE = Units([OUT_TILES, XQ_TILES, XO_TILES], 0, 0)
UNITS_TWO = Units([ffn_tiles("A"), OUT_TILES, ffn_tiles("B")], LAYERS * len(UNITS_ONE.units), 2 * LAYERS * UNITS_ONE.stretches)


def mod_items(m):
    return [(f"m{m}_0", 1, 1), (f"m{m}_1", 0, 1)]


def head_one():
    def tiles(*names):
        return [(n, 1, 1) for n in names]

    def plain(*names):
        return [(n, 1, 0) for n in names]

    def split(tiles_):
        return [item for name, units in tiles_ for item in unit_items(name, units, name)]

    new = plain("T0a", "T0b") + tiles("in_q", "in_kv", "in_v", "in_u") + plain("ws", "qT", "kT", "S0", "S1", "mix")
    new += tiles("xk0") + plain("P0", "V0", "S2") + tiles("xk1") + plain("P1", "V1", "S3") + tiles("xv0")
    new += plain("P2", "P3", "V2", "V3") + tiles("xv1") + plain("Ma", "Mb") + split(OUT_TILES)
    new += mod_items(0) + plain("T1a", "T1b", "mb0") + split(XQ_TILES) + plain("XS0", "XS1")
    new += mod_items(4) + plain("XP0", "XP1", "mb4", "XOa", "XOb") + mod_items(1) + split(XO_TILES[:1]) + plain("mb1")
    new += split(XO_TILES[1:]) + mod_items(6) + plain("T2a", "T2b", "mb6", "route")
    new += mod_items(3) + plain("affT", "mb3") + mod_items(7) + plain("posT", "mb7", "gateT")
    return new


SPARE = 3
N_ROWS = 10
N_SMALL = 10


def group_one():
    items = [("gather", 1, 0)]
    for k in range(KT):
        items += [(f"g{k}", k == 0, 1), (f"u{k}", k == 0, 1)]
    items += [("midT", 1, 0)]
    items += [(f"d{k}", k == 0, 1) for k in range(KT)]
    items += [(f"spare{i}", i < 3, 0) for i in range(SPARE)]
    return items


def ffn_items(f):
    items = []
    for name, units in ffn_tiles(f):
        result = name if "d" not in name or name.endswith("_0") else 0
        items += unit_items(name, units, result)
    return items


def head_two():
    def tiles(*names):
        return [(n, 1, 1) for n in names]

    def plain(*names):
        return [(n, 1, 0) for n in names]

    items = mod_items(2) + plain("T0a", "T0b", "mb2") + ffn_items("A")
    items += mod_items(5) + plain("T1a", "T1b", "mb5")
    items += tiles("in_fh", "in_qka") + plain("SZ0", "SZ1") + tiles("in_qh") + plain("HL", "HE0", "HE1")
    items += tiles("in_vaqd") + plain("SC0", "SC1", "HS0", "HE2", "HS1", "HE3")
    items += [("in_kdvd", 1, SKIP)] + plain("SV", "HS2", "HE4", "HS3", "HE5")
    items += tiles("in_ih") + plain("HS4", "HE6", "HS5", "HE7", "DT")
    items += plain("DS0", "DS1", "HS6", "HS7", "HD", "HO") + tiles("in_gh") + plain("DP0", "DV0", "DP1", "DV1", "Ya", "Yb")
    for name, units in OUT_TILES:
        items += unit_items(name, units, name)
    items += mod_items(8) + plain("T2a", "T2b", "mb8") + ffn_items("B")
    return items


def place(j):
    return 2 * (j % 2) + j // 2


STEP0 = 512


def two_blocks(nc: bass.Bass, w, out):
    ones_order = Order([("G", 1, 0), ("GB", 1, 0), ("T0a", 1, 0), ("T0b", 1, 0)], [], [], STEP0, [0] * 4, [0] * SLOTS)
    pre_steps = ones_order.steps
    one = Order(head_one(), group_one(), [("C0", 1, 0), ("C1", 1, 0)], STEP0 + pre_steps,
                [ones_order.uses[q] for q in range(4)], [0] * SLOTS)
    two = Order(head_two(), [], [], one.step0 + LAYERS * one.steps,
                [one.pair0[q] + LAYERS * one.uses[q] for q in range(4)], [LAYERS * n for n in one.slot_uses])

    with ExitStack() as ctx:
        def sb(name, shape):
            return ctx.enter_context(nc.sbuf_tensor(name, shape, F32))

        def over(name, shapes, words):
            views = []
            for group in shapes if isinstance(shapes[0], list) else [shapes]:
                with ExitStack() as inner:
                    views += [inner.enter_context(nc.sbuf_tensor(n, shape, F32R)) for n, shape in group]
                assert sum(int(np.prod(shape[1:])) for _, shape in group) <= words
            return views + [sb(name, [P, words])]

        def sem(name):
            return ctx.enter_context(nc.semaphore(name))

        n_const = sum(n for _, n in CONSTS.values())
        consts = sb("consts", [P, n_const])

        def const(name, *dims):
            a, n = CONSTS[name]
            ap = consts[:, a:a + n]
            if len(dims) == 2:
                ap = ap.rearrange("p (a b) -> p a b", a=dims[0])
            return ap

        ident, ones = const("ident"), const("ones")
        ring = sb("ring", [P, SLOTS, KT * CHUNK])
        x = sb("x", [P, HALVES, D])
        xn = sb("xn", [P, HALVES, D])
        split2, hT_ = over("hT", [("split2", [P, 2, UNIT])], KT * S)
        hT = hT_[:, :].rearrange("p (k s) -> p k s", k=KT)
        _, a_hi, a_lo, split0_one, split1_one, hm_hi, hm_lo, split0, split1, work = over("work", [
            [("below", [P, 2048]), ("a_hi", [P, KT, S]), ("a_lo", [P, KT, S]), ("split0_one", [P, 2, UNIT]), ("split1_one", [P, 2, UNIT])],
            [("hm_hi", [P, FKT, S]), ("hm_lo", [P, FKT, S]), ("split0", [P, 2, UNIT]), ("split1", [P, 2, UNIT])]], 15360)
        as_rows = sb("as_rows", [96, 3 * P])
        rows = as_rows[:, 0:P]
        bias_rows = as_rows[0:NMOD * KT, P:3 * P].rearrange("p (l n) -> p l n", l=LAYERS)
        pick = as_rows[0:2 * NMOD * LAYERS, 0:2 * P].rearrange("p (i n) -> p i n", i=2)
        vectors = sb("vectors", [P, 96])
        biases = sb("biases", [P, LAYERS * NMOD * KT])
        g_mem, g_mix, g_xa, g_ffn, g_br, b_s, lbl, cT = (
            vectors[:, a:b] for a, b in ((0, 8), (8, 24), (24, 40), (40, 56), (56, 72), (72, 80), (80, 88), (88, 96)))
        hT_hi, hT_lo, shared = over("shared", [("hT_hi", [P, KT, S]), ("hT_lo", [P, KT, S])], 4096)
        u1, u2 = UNITS_ONE, UNITS_TWO
        order_of = {u1: one, u2: two}
        split = {u1: [split0_one, split1_one, split2], u2: [split0, split1, split2]}
        act_parts = {u1: (a_hi, a_lo), u2: (hT_hi, hT_lo)}
        w_s = shared[:, 0:1024].rearrange("p (l n) -> p l n", l=LAYERS)
        w_s_now = shared[:, 1024:1536]
        g_v = shared[:, 1536:2560].rearrange("p (l n) -> p l n", l=LAYERS)
        g_final = shared[:, 2560:3584]
        router = shared[:, 3584:3840].rearrange("p (k e) -> p k e", e=NE)
        g_q1, g_k1, g_q2, g_k2 = (sb(n, [P, LAYERS, HD]) for n in ("g_q1", "g_k1", "g_q2", "g_k2"))
        g_h = sb("g_h", [P, LAYERS, HK])
        lb_ln, lb_ln1m, lb_1m = (sb(n, [P, LAYERS * HH]) for n in ("lb_ln", "lb_ln1m", "lb_1m"))
        lbt, quarter = sb("lbt", [P, 4, HH]), sb("quarter", [P, LAYERS * HH])
        c32 = sb("c32", [P, KT, 32])
        gate_bias = sb("gate_bias", [2 * NMOD * LAYERS, CHUNK])
        part = sb("part", [P, 2, CHUNK])
        mcol = sb("mcol", [P, LAYERS * NMOD * KT])
        gate_b = sb("gate_b", [P, 3, D])
        eps = sb("eps", [P, 2])
        ss, ms, rstd = sb("ss", [P, 2]), sb("ms", [P, 2]), sb("rstd", [P, 2])
        mhalf = sb("mhalf", [P, 32])
        var, inv = sb("var", [P, 32]), sb("inv", [P, 32])
        smax, ssum, rsum = sb("smax", [P, 4, 4]), sb("ssum", [P, 4, 4]), sb("rsum", [P, 4, 4])
        nmax = sb("nmax", [P, 4, 4])
        small = sb("small", [P, 64])

        def cut(at, *dims):
            n = int(np.prod(dims))
            ap = work[:, at:at + n]
            if len(dims) == 2:
                return ap.rearrange("p (a b) -> p a b", a=dims[0])
            if len(dims) == 3:
                return ap.rearrange("p (a b c) -> p a b c", a=dims[0], b=dims[1])
            return ap

        memT = gate_b[:, 0:2, :].rearrange("p a b -> p (a b)").rearrange("p (k s) -> p k s", k=KT)
        ug, vg = cut(0, HALVES, GM), cut(1024, HALVES, GM)
        qk, vv = cut(2048, HALVES, 640), cut(3328, HALVES, KVH * HD)
        rq, kdup = cut(3584, HALVES, 640), cut(4864, HALVES, 256)
        t1, t2 = cut(5376, HALVES, 320), cut(6016, HALVES, 320)
        qkT = cut(5376, 6, S)
        pr, pTr = cut(6912, 2, 1024), cut(8960, 2, 1024)
        sq1 = cut(6912, 1280)
        kxT, vx = cut(11008, KT, S), cut(13056, HALVES, D)
        qxT, px, pxT, oxT = cut(0, KT, S), cut(2048, HALVES, 1024), cut(4096, XH, 2, S), cut(0, KT, S)
        sel, selg = cut(0, HALVES, NE * CAP), cut(1024, HALVES, NE * CAP)
        gateT = cut(2048, GROUPS, HALVES, P)
        aw = [work[0:NE, 3072 + 256 * i:3328 + 256 * i] for i in range(6)]
        xsT, act_mid, mid, midT = cut(4608, KT, P), cut(5632, FF), cut(6656, FF), cut(7680, KT, P)
        ys = cut(8704, GROUPS, D)
        aff, posn = cut(12800, HALVES, NE), cut(12832, HALVES, NE)
        sg, tmp = xn, xn[:, :, 0:CHUNK]
        qkaT, dq, va_vd = cut(0, 4, S), cut(1024, HALVES, 512), cut(2048, HALVES, 512)
        dpT = cut(0, 2, 1024)
        qhT, lfT, khT = cut(3072, HH, S), cut(4096, HH, S), cut(5120, HH, S)
        dT = cut(4096, 4, S)
        ih, gh = cut(6144, HALVES, 512), cut(7168, HALVES, 512)
        fz, fa, fm, fs, fx, fd = (cut(8192 + 1024 * i, 1024) for i in range(6))
        he, hq, lfn = cut(8192, 2, 1024), cut(10240, 2, 1024), cut(12288, HALVES, 512)
        at_, at2 = cut(13312, 8, P), cut(14336, HH, P)
        ho, hsq = cut(8192, HALVES, 512), cut(9216, 1024)
        z_both, sp_both = shared[:, 0:1536], shared[:, 1536:3072]
        (z0, z1), (sp0, sp1) = ((t[:, 0:1024].rearrange("p (a b) -> p a b", a=4),
                                 t[:, 1024:1536].rearrange("p (a b) -> p a b", a=4)) for t in (z_both, sp_both))
        dr = shared[:, 3072:4096].rearrange("p (h n) -> p h n", h=HALVES)
        dp = shared[:, 0:2048].rearrange("p (h n) -> p h n", h=HALVES)
        dt1, dt2 = part[:, 0, :].rearrange("p (h n) -> p h n", h=HALVES), part[:, 1, :].rearrange("p (h n) -> p h n", h=HALVES)
        dsq = part[:, :, :].rearrange("p a b -> p (a b)")

        ps = [ctx.enter_context(nc.psum_tensor(f"ps{q}", [P, 2, CHUNK], F32)) for q in range(4)]

        load_i, load_c, load_x, load_m, load_r, load_p, stored = (
            sem(n) for n in ("load_i", "load_c", "load_x", "load_m", "load_r", "load_p", "stored"))
        landed = [sem(f"landed{i}") for i in range(SLOTS)]
        pe_step = sem("pe_step")
        pair_free = [sem(f"pair_free{q}") for q in range(4)]
        ss_ready, rstd_ready, xn_ready, x_ready = (sem(n) for n in ("ss_ready", "rstd_ready", "xn_ready", "x_ready"))
        var_ready, inv_ready, setup = sem("var_ready"), sem("inv_ready"), sem("setup")
        names = """ws_now v_ready rope_ready smax_ready merged xmax_ready xpn_ready rmax_ready aff_ready
        pos_ready sel_ready pick_ready c_ready c_silu lb_exp lb_sum lb_floor lb_root lb_log fab_ready flog fd_ready fl2 kh_ready
        sp_in st_log sp_ready w_arg w_exp dexp w_ready drope_ready dmax_ready dp_ready lf_ready hq_ready
        y_dve h_hi h_lo w_hi w_lo m_ready m_hi m_lo""".split()
        sm = {n: sem(n) for n in names}
        begin = ones_order

        def mcol_of(l, m, k, n=1):
            return mcol[:, bass.ds((l * NMOD + m) * KT + k, n)]

        def unit_source(eng, u, l, i):
            name, n, _ = u.units[i]
            order = order_of[u]
            eng.wait_ge(landed[order.slot(name)], order.landings(l, name))
            at = ring[:, order.slot(name), :]
            if name[:2] in ("Ag", "Au", "Bg", "Bu", "xq"):
                cols = P * u.tiles[name]
                return at[:, 0:KT * cols].rearrange("p (k n) -> p k n", n=cols)[:, :, n * P:(n + 1) * P]
            return at[:, n * UNIT:(n + 1) * UNIT].rearrange("p (k n) -> p k n", n=CHUNK)

        def unit_part(u, i, part_, n):
            return split[u][u.buffer(i)][:, part_, :].rearrange("p (k n) -> p k n", n=n)

        block = ctx.enter_context(nc.Block())

        def read_out(eng, order, l, *names, g=0):
            for name in names:
                eng.wait_ge(pair_free[order.pair(name)], order.free(l, name, g) + 2)

        def finished(eng, order, l, name, g=0):
            eng.wait_ge(pe_step, order.done(l, name, g))

        @block.sync
        def _(sp):
            sp.dma_start(consts[:, 0:2 * P], w["consts"][:, 0:2 * P]).then_inc(load_i, 16)
            sp.dma_start(xn[:, :, :], w["mem"][0].rearrange("(h p) d -> p h d", p=P)).then_inc(load_m, 16)
            sp.dma_start(x[:, :, :], w["x"][0].rearrange("(h p) d -> p h d", p=P)).then_inc(load_x, 16)
            sp.wait_ge(load_r, 16 * N_ROWS)

            def tile(order, l, name, src, g=0):
                slot, cols = order.slot(name), src.shape[2]
                sp.wait_ge(pe_step, order.slot_free(l, name, g))
                sp.dma_start(ring[:, slot, 0:src.shape[1] * cols].rearrange("p (k n) -> p k n", n=cols),
                             src).then_inc(landed[slot], 16)

            def columns(name, l, c0, n, k0=0, nk=KT):
                return w[name][bass.ds(l, 1), k0 * P:(k0 + nk) * P, c0:c0 + n].rearrange("l (k p) n -> p (l k) n", p=P)

            def first_columns(name, l):
                rows_ = w[name].rearrange("l k n -> (l k) n")
                return rows_[bass.ds(l * D, D), 0:CHUNK].rearrange("(k p) n -> p k n", p=P)

            def mod_tiles(order, l, m):
                for i in range(2):
                    tile(order, l, f"m{m}_{i}", columns("w_mod_2", l, m * D + i * CHUNK, CHUNK))

            with sp.Fori(0, LAYERS) as l:
                for n, c0, width in (("in_q", 1024, 512), ("in_kv", 1536, 256), ("in_v", 512, 512), ("in_u", 0, 512)):
                    tile(one, l, n, columns("w_in", l, c0, width) if c0 else first_columns("w_in", l))
                for i, n in enumerate(("xk0", "xk1", "xv0", "xv1")):
                    tile(one, l, n, columns("xattn_w_kv", l, 512 * i, CHUNK))
                for i in range(2):
                    tile(one, l, f"out{i}", columns("w_out", l, 512 * i, CHUNK))
                mod_tiles(one, l, 0)
                for i in range(2):
                    tile(one, l, f"xq{i}", columns("xattn_w_q", l, 512 * i, CHUNK))
                mod_tiles(one, l, 4)
                mod_tiles(one, l, 1)
                for i in range(2):
                    tile(one, l, f"xo{i}", columns("xattn_w_o", l, 512 * i, CHUNK))
                for m in (6, 3, 7):
                    mod_tiles(one, l, m)
                with sp.Fori(0, GROUPS) as g:
                    def experts(name, k):
                        return w[name][bass.ds(l, 1), bass.ds(g * GROUP, GROUP), k * P:(k + 1) * P, :].rearrange(
                            "l e p n -> p (l e) n")
                    for k in range(KT):
                        tile(one, l, f"g{k}", experts("w_gate", k), g)
                        tile(one, l, f"u{k}", experts("w_up", k), g)
                    for k in range(KT):
                        tile(one, l, f"d{k}", experts("w_down", k), g)

            def stream_ffn(l, f, name):
                for c, n in enumerate(FFC):
                    tile(two, l, f"{f}g{c}", columns(name + "_w_gate_2", l, c * CHUNK, n))
                    tile(two, l, f"{f}u{c}", columns(name + "_w_up_2", l, c * CHUNK, n))
                for n in range(D // CHUNK):
                    for i, (k0, nk) in enumerate(DOWN):
                        tile(two, l, f"{f}d{n}_{i}", columns(name + "_w_down_2", l, n * CHUNK, CHUNK, k0, nk))

            finished(sp, one, LAYERS - 1, f"d{KT - 1}", GROUPS - 1)
            with sp.Fori(0, LAYERS) as l:
                mod_tiles(two, l, 2)
                stream_ffn(l, "A", "ffn1")
                mod_tiles(two, l, 5)
                for i, n in ((4, "in_fh"), (0, "in_qka"), (3, "in_qh"), (1, "in_vaqd"), (2, "in_kdvd"), (5, "in_ih"), (6, "in_gh")):
                    tile(two, l, n, columns("w_in_2", l, 512 * i, CHUNK) if i else first_columns("w_in_2", l))
                for i in range(2):
                    tile(two, l, f"out{i}", columns("w_out_2", l, 512 * i, CHUNK))
                mod_tiles(two, l, 8)
                stream_ffn(l, "B", "ffn2")
            sp.wait_ge(x_ready, 8 + 3 * LAYERS)
            sp.dma_start(out[0].rearrange("(h p) d -> p h d", p=P), x[:, :, :]).then_inc(stored, 16)
            sp.wait_ge(stored, 16)

        @block.tensor
        def _(pe):
            pe.sem_inc(pe_step, STEP0)
            for q in range(4):
                pe.sem_inc(pair_free[q], 2)

            def result(order, l, name, g=0):
                pe.wait_ge(pair_free[order.pair(name)], order.free(l, name, g))
                return ps[order.pair(name)]

            def weights(order, l, name, cols=CHUNK, g=0, nk=KT):
                pe.wait_ge(landed[order.slot(name)], order.landings(l, name, g))
                return ring[:, order.slot(name), 0:nk * cols].rearrange("p (k n) -> p k n", n=cols)

            def step(ins, n=1):
                ins.then_inc(pe_step, n)

            def transposes(order, l, name, pieces, width=P, g=0):
                ps_ = result(order, l, name, g)
                for src, m, bank, col in pieces:
                    rows = src.shape[0]
                    last = pe.transpose(ps_[0:m, bank, col:col + rows], src, ident[0:rows, 0:rows])
                step(last)

            def rows_to_hT(order, l, ab, src=xn):
                for i in range(2):
                    transposes(order, l, ab[i], [
                        (src[:, h, (4 * i + 2 * b + kk) * P:(4 * i + 2 * b + kk + 1) * P], P, b, kk * S + h * P)
                        for b in range(2) for kk in range(2) for h in range(HALVES)])

            def by_token(order, l, name, aT, cols=CHUNK, first=True):
                w_, ps_ = weights(order, l, name, cols), result(order, l, name)
                for h in range(HALVES):
                    for k in range(KT):
                        last = pe.matmul(ps_[:, h, 0:cols], aT[:, k, h * P:(h + 1) * P], w_[:, k, :],
                                         start=(k == 0), stop=(k == KT - 1))
                step(last)

            def by_feature(order, l, name, aT, cols=CHUNK):
                w_, ps_ = weights(order, l, name, cols), result(order, l, name)
                for b in range(cols // P):
                    for k in range(KT):
                        last = pe.matmul(ps_[:, b // 2, (b % 2) * S:(b % 2 + 1) * S], w_[:, k, b * P:(b + 1) * P],
                                         aT[:, k, :], start=(k == 0), stop=(k == KT - 1))
                step(last)

            def mod(order, l, m):
                for i in range(2):
                    w_ = weights(order, l, f"m{m}_{i}")
                    ps_ = result(order, l, f"m{m}_0") if i == 0 else ps_
                    for r in range(2):
                        for j in range(4):
                            k = 4 * r + j
                            last = pe.matmul(ps_[32 * j:32 * j + 32, i, :], c32[:, k, :], w_[:, k, :],
                                             start=(r == 0), stop=(r == 1))
                    step(last)

            def mod_sum(order, l, m):
                read_out(pe, order, l, f"m{m}_0")
                if m % 3 == 2:
                    pe.wait_ge(sm["pick_ready"], 3 * l + m // 3 + 1)
                ps_ = result(order, l, f"mb{m}")
                for i in range(2):
                    if m % 3 == 2:
                        pe.matmul(ps_[:, i, :], ones, part[:, i, :], start=True, stop=False)
                        last = pe.matmul(ps_[:, i, :], pick[:, i, :], gate_bias[:, :], start=False, stop=True)
                    else:
                        for b in range(4):
                            c = 4 * i + b
                            last = pe.matmul(ps_[:, 0, c:c + 1], part[:, i, b * P:(b + 1) * P], ones[:, 0:1],
                                             start=True, stop=True)
                step(last)

            def unit(u, l, i):
                pe.wait_ge(sm["w_lo"], u.counts(l, i))

            def parts(out_, w_hi, w_lo, a_hi, a_lo, first, last, weights_stationary):
                for i, (w_, a_) in enumerate(((w_hi, a_hi), (w_hi, a_lo), (w_lo, a_hi))):
                    l_, r_ = (w_, a_) if weights_stationary else (a_, w_)
                    ins = pe.matmul(out_, l_, r_, start=first and i == 0, stop=last and i == 2)
                return ins

            def features_by_parts(u, l, name):
                ps_, (a_hi_, a_lo_) = result(order_of[u], l, name), act_parts[u]
                for b, i in enumerate(u.of(name)):
                    unit(u, l, i)
                    hi, lo = unit_part(u, i, 0, P), unit_part(u, i, 1, P)
                    for k in range(KT):
                        last = parts(ps_[:, b // 2, (b % 2) * S:(b % 2 + 1) * S], hi[:, k, :], lo[:, k, :],
                                     a_hi_[:, k, :], a_lo_[:, k, :], k == 0, k == KT - 1, True)
                    step(last)

            def tokens_by_parts(u, l, name, ps_, a_hi_, a_lo_, k0, of):
                for n, i in enumerate(u.of(name)):
                    unit(u, l, i)
                    hi, lo = unit_part(u, i, 0, CHUNK), unit_part(u, i, 1, CHUNK)
                    for h in range(HALVES):
                        for kk in range(2):
                            k, t = k0 + 2 * n + kk, slice(h * P, (h + 1) * P)
                            last = parts(ps_[:, h, :], hi[:, kk, :], lo[:, kk, :], a_hi_[:, k, t], a_lo_[:, k, t],
                                         k == 0, k == of - 1, False)
                    step(last)

            pe.wait_ge(load_i, 16)
            pe.wait_ge(load_r, 16 * N_ROWS)
            transposes(begin, 0, "G", [(rows[:, :], P, 0, 0)])
            transposes(begin, 0, "GB", [(bias_rows[:, j, :], P, 0, j * NMOD * KT) for j in range(LAYERS)])
            pe.wait_ge(xn_ready, 2)
            rows_to_hT(begin, 0, ("T0a", "T0b"))
            read_out(pe, begin, 0, "T0a", "T0b")

            with pe.Fori(0, LAYERS) as l:
                def norm_T(j, ab, split_=False):
                    pe.wait_ge(xn_ready, 2 * (1 + 3 * l + j) + 2)
                    rows_to_hT(one, l, ab)
                    if not split_:
                        read_out(pe, one, l, *ab)

                norm_T(0, ("T0a", "T0b"))
                for n, cols in (("in_q", 512), ("in_kv", 256), ("in_v", 512), ("in_u", 512)):
                    by_token(one, l, n, hT, cols)
                pe.wait_ge(sm["ws_now"], l + 1)
                transposes(one, l, "ws", [(w_s_now[:, i * P:(i + 1) * P], P, 0, i * P) for i in range(4)])
                pe.wait_ge(sm["rope_ready"], l + 1)
                transposes(one, l, "qT", [(rq[:, h, b * P:(b + 1) * P], P, b // 2, (b % 2) * S + h * P)
                                          for b in range(4) for h in range(HALVES)])
                transposes(one, l, "kT", [(kdup[:, h, b * P:(b + 1) * P], P, 0, b * S + h * P)
                                          for b in range(KVH) for h in range(HALVES)])

                def att_scores(b):
                    h, hg = b // 2, b % 2
                    if b == 0:
                        read_out(pe, one, l, "qT", "kT")
                    ps_ = result(one, l, f"S{b}")
                    for j in range(4):
                        hd, at = 4 * hg + j, HD * (j % 2)
                        last = pe.matmul(ps_[:, j % 2, (j // 2) * S:(j // 2 + 1) * S],
                                         qkT[at:at + HD, hd // 2, h * P:(h + 1) * P],
                                         qkT[at:at + HD, 4 + hd // 4, :], start=True, stop=True)
                    step(last)

                def att_turn(b):
                    read_out(pe, one, l, f"S{b}")
                    transposes(one, l, f"P{b}", [(pr[:, b % 2, j * S + t * P:j * S + (t + 1) * P], P, j // 2, (j % 2) * S + t * P)
                                                 for j in range(4) for t in range(2)])

                def att_values(b):
                    hg = b % 2
                    read_out(pe, one, l, f"P{b}", *(["in_kv"] if b == 0 else []))
                    ps_ = result(one, l, f"V{b}")
                    for j in range(4):
                        for t in range(2):
                            last = pe.matmul(ps_[:, 0, j * HD:(j + 1) * HD],
                                             pTr[:, b % 2, j * S + t * P:j * S + (t + 1) * P],
                                             vv[:, t, hg * HD:(hg + 1) * HD], start=(t == 0), stop=(t == 1))
                    step(last)

                att_scores(0)
                att_scores(1)
                pe.wait_ge(sm["v_ready"], l + 1)
                read_out(pe, one, l, "ws")
                ps_ = result(one, l, "mix")
                for h in range(HALVES):
                    for i in range(4):
                        last = pe.matmul(ps_[:, h, i * P:(i + 1) * P], w_s_now[:, i * P:(i + 1) * P],
                                         vg[:, h, i * P:(i + 1) * P], start=True, stop=True)
                step(last)
                by_feature(one, l, "xk0", memT)
                att_turn(0)
                att_values(0)
                att_scores(2)
                by_feature(one, l, "xk1", memT)
                att_turn(1)
                att_values(1)
                att_scores(3)
                by_token(one, l, "xv0", memT)
                att_turn(2)
                att_turn(3)
                att_values(2)
                att_values(3)
                by_token(one, l, "xv1", memT)
                pe.wait_ge(sm["merged"], l + 1)
                rows_to_hT(one, l, ("Ma", "Mb"))
                pe.wait_ge(sm["h_lo"], u1.halves(l, 0))
                for n in ("out0", "out1"):
                    tokens_by_parts(u1, l, n, result(one, l, n), a_hi, a_lo, 0, KT)
                pe.wait_ge(sm["c_ready"], 1)
                mod(one, l, 0)
                norm_T(1, ("T1a", "T1b"), True)
                mod_sum(one, l, 0)
                pe.wait_ge(sm["h_lo"], u1.halves(l, 1))
                for n in ("xq0", "xq1"):
                    features_by_parts(u1, l, n)
                read_out(pe, one, l, "xq0", "xq1", "xk0", "xk1")
                for h in range(HALVES):
                    ps_ = result(one, l, f"XS{h}")
                    for j in range(XH):
                        for t in range(2):
                            last = pe.matmul(ps_[:, j // 2, (j % 2) * S:(j % 2 + 1) * S],
                                             qxT[:, 2 * j + t, h * P:(h + 1) * P], kxT[:, 2 * j + t, :],
                                             start=(t == 0), stop=(t == 1))
                    step(last)
                mod(one, l, 4)
                for h in range(HALVES):
                    pe.wait_ge(sm["xpn_ready"], 2 * l + h + 1)
                    transposes(one, l, f"XP{h}", [(px[:, h, j * S + t * P:j * S + (t + 1) * P], P, j // 2, (j % 2) * S + t * P)
                                                  for j in range(XH) for t in range(2)])
                mod_sum(one, l, 4)
                read_out(pe, one, l, "XP0", "XP1", "xv0", "xv1")
                for a in range(2):
                    ps_ = result(one, l, ("XOa", "XOb")[a])
                    for b in range(4):
                        d = 4 * a + b
                        for t in range(2):
                            last = pe.matmul(ps_[:, b // 2, (b % 2) * S:(b % 2 + 1) * S],
                                             vx[:, t, d * P:(d + 1) * P], pxT[:, d // 2, t, :],
                                             start=(t == 0), stop=(t == 1))
                    step(last)
                mod(one, l, 1)
                pe.wait_ge(sm["h_lo"], u1.halves(l, 2))
                tokens_by_parts(u1, l, "xo0", result(one, l, "xo0"), a_hi, a_lo, 0, KT)
                mod_sum(one, l, 1)
                tokens_by_parts(u1, l, "xo1", result(one, l, "xo1"), a_hi, a_lo, 0, KT)
                mod(one, l, 6)
                norm_T(2, ("T2a", "T2b"))
                mod_sum(one, l, 6)
                ps_ = result(one, l, "route")
                for h in range(HALVES):
                    for k in range(KT):
                        last = pe.matmul(ps_[:, 0, h * NE:(h + 1) * NE], hT[:, k, h * P:(h + 1) * P],
                                         router[:, bass.ds(l * KT + k, 1), :].rearrange("p a e -> p (a e)"),
                                         start=(k == 0), stop=(k == KT - 1))
                step(last)
                mod(one, l, 3)
                pe.wait_ge(sm["aff_ready"], l + 1)
                transposes(one, l, "affT", [(aff[:, h, :], NE, 0, h * P) for h in range(HALVES)])
                mod_sum(one, l, 3)
                mod(one, l, 7)
                pe.wait_ge(sm["pos_ready"], l + 1)
                ps_ = result(one, l, "posT")
                for h in range(HALVES):
                    last = pe.matmul(ps_[:, 0, h * NE:(h + 1) * NE], aw[5][:, h * P:(h + 1) * P], ident[0:NE, 0:NE],
                                     start=True, stop=True)
                step(last)
                mod_sum(one, l, 7)
                pe.wait_ge(sm["sel_ready"], l + 1)
                transposes(one, l, "gateT", [(selg[:, h, g * P:(g + 1) * P], P, g // 2, (g % 2) * S + h * P)
                                             for g in range(GROUPS) for h in range(HALVES)])
                with pe.Fori(0, GROUPS) as g:
                    ps_ = result(one, l, "gather", g)
                    for k in range(KT):
                        for h in range(HALVES):
                            last = pe.matmul(ps_[:, k // 4, (k % 4) * P:(k % 4 + 1) * P], xn[:, h, k * P:(k + 1) * P],
                                             sel[:, h, bass.ds(g * P, P)], start=(h == 0), stop=(h == 1))
                    step(last)
                    read_out(pe, one, l, "gather", g=g)

                    def experts(name, k, ps_, lhs, more=1):
                        w_ = weights(one, l, name, FF, g, GROUP)
                        for n in range(FF // CHUNK):
                            for e in range(GROUP):
                                last = pe.matmul(ps_[e * CAP:(e + 1) * CAP, n, :], lhs[:, k, e * CAP:(e + 1) * CAP],
                                                 w_[:, e, n * CHUNK:(n + 1) * CHUNK],
                                                 start=(k == 0), stop=(k == KT - 1))
                        step(last, more)

                    pg, pu = result(one, l, "g0", g), result(one, l, "u0", g)
                    for k in range(KT):
                        experts(f"g{k}", k, pg, xsT)
                        experts(f"u{k}", k, pu, xsT)
                    read_out(pe, one, l, "u0", g=g)
                    transposes(one, l, "midT", [(mid[:, k * P:(k + 1) * P], P, k // 4, (k % 4) * P) for k in range(KT)], g=g)
                    read_out(pe, one, l, "midT", g=g)
                    pd = result(one, l, "d0", g)
                    for k in range(KT):
                        experts(f"d{k}", k, pd, midT, 1 if k < KT - 1 else 1 + SPARE)
                    for i in range(3):
                        pe.sem_inc(pair_free[one.pair(f"spare{i}")], 2)
                read_out(pe, one, l, "gateT")
                read_out(pe, one, l, "d0", g=GROUPS - 1)
                for h in range(HALVES):
                    ps_ = result(one, l, f"C{h}")
                    for n in range(D // CHUNK):
                        for g in range(GROUPS):
                            last = pe.matmul(ps_[:, n, :], gateT[:, g, h, :], ys[:, g, n * CHUNK:(n + 1) * CHUNK],
                                             start=(g == 0), stop=(g == GROUPS - 1))
                    step(last)

            with pe.Fori(0, LAYERS) as l:
                def norm_T2(j, ab, m, h=None):
                    mod(two, l, m)
                    pe.wait_ge(xn_ready, 2 * (8 + 3 * l + j) + 2)
                    rows_to_hT(two, l, ab)
                    mod_sum(two, l, m)
                    if h is None:
                        read_out(pe, two, l, *ab)
                    else:
                        pe.wait_ge(sm["h_lo"], u2.halves(l, h))

                def ffn(f, j):
                    for c in range(len(FFC)):
                        features_by_parts(u2, l, f"{f}g{c}")
                        features_by_parts(u2, l, f"{f}u{c}")
                    for n in range(D // CHUNK):
                        ps_ = result(two, l, f"{f}d{n}_0")
                        for i, (k0, nk) in enumerate(DOWN):
                            pe.wait_ge(sm["m_lo"], (2 * l + j) * len(FFC) + -(-(k0 + nk) * P // CHUNK))
                            tokens_by_parts(u2, l, f"{f}d{n}_{i}", ps_, hm_hi, hm_lo, k0, FKT)

                norm_T2(0, ("T0a", "T0b"), 2, 0)
                ffn("A", 0)
                norm_T2(1, ("T1a", "T1b"), 5)
                decay = const("decay_sum", LEVELS + 1, P)

                def decays(i):
                    ps_ = result(two, l, f"HE{i}")
                    for j in range(HH):
                        for h in range(HALVES):
                            m = i if i < LEVELS - 1 else i + h
                            last = pe.matmul(ps_[:, j // 2, (j % 2) * S + h * P:(j % 2) * S + (h + 1) * P],
                                             lfn[:, h, j * HK:(j + 1) * HK], decay[:, m, :], start=True, stop=True)
                    step(last)

                def level(i):
                    pe.wait_ge(sm["hq_ready"], LEVELS * l + i + 1)
                    q_ = hq[:, i % 2, :].rearrange("p (j s) -> p j s", j=HH)
                    ps_ = result(two, l, f"HS{i}")
                    if i < LEVELS - 1:
                        for j in range(HH):
                            for h in range(HALVES):
                                both = q_[:, j, h * P:(h + 1) * P]
                                last = pe.matmul(ps_[:, j // 2, (j % 2) * S + h * P:(j % 2) * S + (h + 1) * P],
                                                 both, both, start=True, stop=True)
                    else:
                        for j in range(HH):
                            last = pe.matmul(ps_[:, 0, j * P:(j + 1) * P], q_[:, j, 0:P], q_[:, j, P:S],
                                             start=True, stop=True)
                    step(last)

                def dilated_out(h):
                    pe.wait_ge(sm["dp_ready"], 2 * l + h + 1)
                    transposes(two, l, f"DP{h}", [(dp[:, h, j * S + t * P:j * S + (t + 1) * P], P, j // 2, (j % 2) * S + t * P)
                                                  for j in range(4) for t in range(2)])
                    read_out(pe, two, l, f"DP{h}", *(["in_kdvd"] if h == 0 else []))
                    ps_ = result(two, l, f"DV{h}")
                    for i in range(4):
                        j = place(i)
                        for t in range(2):
                            last = pe.matmul(ps_[:, 0, i * HD:(i + 1) * HD], dpT[:, h, i * S + t * P:i * S + (t + 1) * P],
                                             va_vd[:, t, 256 + j * HD:256 + (j + 1) * HD], start=(t == 0), stop=(t == 1))
                    step(last)

                by_feature(two, l, "in_fh", hT)
                by_feature(two, l, "in_qka", hT)
                read_out(pe, two, l, "in_qka")
                ps_ = result(two, l, "SZ0")
                for j in range(4):
                    at = HD * (j % 2)
                    last = pe.matmul(ps_[:, j % 2, (j // 2) * S:(j // 2 + 1) * S], qkaT[at:at + HD, 2 + j // 2, 0:P],
                                     qkaT[at:at + HD, j // 2, :], start=True, stop=True)
                step(last)
                ps_ = result(two, l, "SZ1")
                for j in range(4):
                    at = HD * (j % 2)
                    last = pe.matmul(ps_[:, j % 2, (j // 2) * P:(j // 2 + 1) * P], qkaT[at:at + HD, 2 + j // 2, P:S],
                                     qkaT[at:at + HD, j // 2, P:S], start=True, stop=True)
                step(last)
                by_feature(two, l, "in_qh", hT)
                pe.wait_ge(sm["lf_ready"], l + 1)
                transposes(two, l, "HL", [(lfT[:, j, h * P:(h + 1) * P], P, h, j * P) for h in range(HALVES) for j in range(HH)])
                read_out(pe, two, l, "HL")
                decays(0)
                decays(1)
                by_token(two, l, "in_vaqd", hT)
                pe.wait_ge(sm["sp_ready"], l + 1)
                ps_ = result(two, l, "SC0")
                for j in range(4):
                    bank, col = j // 2, (j % 2) * S
                    pe.matmul(ps_[:, bank, col:col + S], const("tri_ge"), sp0[:, j, :], start=True, stop=True)
                    last = pe.matmul(ps_[:, bank, col + P:col + S], ones, sp1[:, j, :], start=False, stop=True,
                                     skip_group_check=True)
                step(last)
                ps_ = result(two, l, "SC1")
                for j in range(4):
                    last = pe.matmul(ps_[:, 0, j * P:(j + 1) * P], const("tri_ge"), sp1[:, j, :], start=True, stop=True)
                step(last)
                level(0)
                decays(2)
                level(1)
                decays(3)
                by_token(two, l, "in_kdvd", hT)
                pe.wait_ge(sm["w_ready"], l + 1)
                read_out(pe, two, l, "in_vaqd")
                ps_ = result(two, l, "SV")
                for j in range(4):
                    cols = slice(j * HD, (j + 1) * HD)
                    i = place(j)
                    pe.matmul(ps_[:, 0, cols], z0[:, i, 0:P], va_vd[:, 0, cols], start=True, stop=True)
                    pe.matmul(ps_[:, 1, cols], z0[:, i, P:S], va_vd[:, 0, cols], start=True, stop=False)
                    last = pe.matmul(ps_[:, 1, cols], z1[:, i, :], va_vd[:, 1, cols], start=False, stop=True)
                step(last)
                level(2)
                decays(4)
                level(3)
                decays(5)
                by_token(two, l, "in_ih", hT)
                level(4)
                decays(6)
                level(5)
                decays(7)
                pe.wait_ge(sm["drope_ready"], l + 1)
                transposes(two, l, "DT", [(dr[:, h, b * P:(b + 1) * P], P, b // 2, (b % 2) * S + h * P)
                                          for b in range(4) for h in range(HALVES)])
                read_out(pe, two, l, "DT")
                for h in range(HALVES):
                    ps_ = result(two, l, f"DS{h}")
                    for j in range(4):
                        at = HD * (j % 2)
                        last = pe.matmul(ps_[:, j % 2, (j // 2) * S:(j // 2 + 1) * S],
                                         dT[at:at + HD, j // 2, h * P:(h + 1) * P], dT[at:at + HD, 2 + j // 2, :],
                                         start=True, stop=True)
                    step(last)
                level(6)
                level(7)
                pe.wait_ge(sm["kh_ready"], l + 1)
                read_out(pe, two, l, "in_qh")
                ps_ = result(two, l, "HD")
                for j in range(HH):
                    for h in range(HALVES):
                        last = pe.matmul(ps_[:, j // 2, (j % 2) * S + h * P:(j % 2) * S + (h + 1) * P],
                                         khT[:, j, h * P:(h + 1) * P], qhT[:, j, h * P:(h + 1) * P], start=True, stop=True)
                step(last)
                read_out(pe, two, l, "HD", f"HS{LEVELS - 1}", "in_ih")
                ps_ = result(two, l, "HO")
                for j in range(HH):
                    cols = slice(j * HK, (j + 1) * HK)
                    pe.matmul(ps_[:, 0, cols], at_[:, 2 * j, :], ih[:, 0, cols], start=True, stop=True)
                    pe.matmul(ps_[:, 1, cols], at_[:, 2 * j + 1, :], ih[:, 1, cols], start=True, stop=False)
                    last = pe.matmul(ps_[:, 1, cols], at2[:, j, :], ih[:, 0, cols], start=False, stop=True)
                step(last)
                by_token(two, l, "in_gh", hT)
                dilated_out(0)
                dilated_out(1)
                pe.wait_ge(sm["y_dve"], l + 1)
                read_out(pe, two, l, "SV")
                rows_to_hT(two, l, ("Ya", "Yb"))
                pe.wait_ge(sm["h_lo"], u2.halves(l, 1))
                for n in ("out0", "out1"):
                    tokens_by_parts(u2, l, n, result(two, l, n), hT_hi, hT_lo, 0, KT)
                norm_T2(2, ("T2a", "T2b"), 8, 2)
                ffn("B", 1)

        @block.scalar
        def _(act):
            at = 0
            for n in ("mem_norm_g", "mix_norm_g", "xattn_norm_g", "ffn_norm_g", "branch_norm_g", "gm_b_s",
                      "hgrn_lb_logits_2", "c_2"):
                names = "abc"[:len(w[n].shape)]
                flat_ = w[n] if len(names) == 1 else w[n].rearrange(f"{' '.join(names)} -> ({' '.join(names)})")
                src = flat_.rearrange("(n p) -> n p", p=P)
                act.dma_start(rows[at:at + src.shape[0], :], src).then_inc(load_r, 16)
                at += src.shape[0]
            for j in range(LAYERS):
                act.dma_start(bias_rows[:, j, :], w["b_mod_2"][j].rearrange("(n p) -> n p", p=P)).then_inc(load_r, 16)
            small_loads = [
                (g_q1[:, :, :], w["q_norm_g"].partition_broadcast(P)),
                (g_k1[:, :, :], w["k_norm_g"].partition_broadcast(P)),
                (g_v, w["gm_v_norm_g"].partition_broadcast(P)),
                (w_s, w["gm_w_s"].rearrange("l g i j -> i (l g) j").rearrange("i (l g) j -> i l g j", l=LAYERS)),
                (router, w["w_router"].rearrange("l (k p) e -> p (l k) e", p=P)),
                (gate_bias[:, :], w["b_mod_2"].rearrange("l (u n) -> (l u) n", n=CHUNK)),
                (g_final, w["final_norm_g"].partition_broadcast(P)),
                (g_q2[:, :, :], w["q_norm_g_2"].partition_broadcast(P)),
                (g_k2[:, :, :], w["k_norm_g_2"].partition_broadcast(P)),
                (g_h[:, :, :], w["hgrn_norm_g_2"].partition_broadcast(P)),
            ]
            assert len(small_loads) == N_SMALL
            act.dma_start(consts[:, 2 * P:], w["consts"][:, 2 * P:]).then_inc(load_c, 16)
            for dst, src in small_loads:
                if len(dst.shape) == 3 and len(src.shape) == 4:
                    dst = dst.rearrange("p l (g j) -> p l g j", g=4)
                act.dma_start(dst, src, allow_slow_non_contiguous=True).then_inc(load_p, 16)

            def squares(r, src, scratch):
                for h in range(HALVES):
                    last = act.activation(scratch[:, h, :], src[:, h, :], ACT.Square, scale=D ** -0.5,
                                          accum_out=ss[:, h:h + 1])
                last.then_inc(ss_ready, 1)

            def copy(order, l, name, dst, src, func=ACT.Copy, after=None, n=2, g=0, **kw):
                finished(act, order, l, after or name, g)
                act.activation(dst, src(ps[order.pair(name)]), func, **kw).then_inc(pair_free[order.pair(name)], n)

            def flat(p):
                return p[:, :, :].rearrange("p a b -> p (a b)")

            def second_bank(order, l, name, dst, after=None, g=0):
                copy(order, l, name, dst, lambda p: p[:, 1, :], after=after, n=1, g=g)

            def hT_bank(order, l, ab, scale, bias=None, dst=hT):
                for i in range(2):
                    finished(act, order, l, ab[i])
                    p = ps[order.pair(ab[i])]
                    for kk in range(2):
                        k = 4 * i + 2 + kk
                        if bias is None:
                            last = act.activation(dst[:, k, :], p[:, 1, kk * S:(kk + 1) * S], ACT.Copy, scale=scale(k))
                        else:
                            last = act.activation(dst[:, k, :], p[:, 1, kk * S:(kk + 1) * S], ACT.Identity,
                                                  scale=scale(k), bias=bias(k))
                    last.then_inc(pair_free[order.pair(ab[i])], 1)

            def exps(order, l, name, b, dst):
                scale = {"S": HD ** -0.5, "X": XD ** -0.5}[name[0]]
                p = flat(ps[order.pair(name)])
                for j in range(4):
                    last = act.activation(dst[:, j * S:(j + 1) * S], p[:, j * S:(j + 1) * S], ACT.Exp,
                                          bias=nmax[:, b, j:j + 1], scale=scale, accum_out=ssum[:, b, j:j + 1])
                last.then_inc(pair_free[order.pair(name)], 2)

            act.wait_ge(sm["lb_exp"], 1)
            act.activation(lbl[:, :], lbl[:, :], ACT.Exp).then_inc(sm["lb_sum"], 1)
            act.wait_ge(load_m, 16)
            squares(0, xn, cut(0, HALVES, D))
            act.wait_ge(sm["c_silu"], 1)
            act.activation(c32[:, :, 0:1].rearrange("p k o -> p (k o)"), cT[:, :], ACT.Silu).then_inc(sm["c_ready"], 1)
            act.wait_ge(sm["lb_root"], 1)
            act.activation(lb_ln[:, :], lb_ln[:, :], ACT.Ln)
            act.activation(lb_ln1m[:, :], lb_1m[:, :], ACT.Ln).then_inc(sm["lb_log"], 1)
            hT_bank(begin, 0, ("T0a", "T0b"), lambda k: g_mem[:, k:k + 1], dst=memT)

            def high_parts(u, l, units):
                for i in units:
                    if u.buffer(i) == BUFFERS - 1:
                        act.wait_ge(sm["h_lo"], u.halves(l, u.units[i][2]))
                    k, wraps = u.before(i)
                    finished(act, order_of[u], l - 1 if wraps else l, u.step(k))
                    src = unit_source(act, u, l, i)
                    act.activation(unit_part(u, i, 0, src.shape[2]), src, ACT.Copy).then_inc(sm["w_hi"], 1)

            def high_activations(u, l, ab, src=hT):
                for i in range(2):
                    read_out(act, order_of[u], l, ab[i])
                    k = slice(4 * i, 4 * i + 4)
                    act.activation(act_parts[u][0][:, k, :], src[:, k, :], ACT.Copy).then_inc(sm["h_hi"], 1)

            def mod(order, l, m, before):
                if before is not None:
                    finished(act, order, l, f"mb{before}")
                copy(order, l, f"m{m}_0", part[:, :, :], lambda p: p[:, :, :], after=f"m{m}_1")

            with act.Fori(0, LAYERS) as l:
                def norm(j, ab, gain, m=None, before=None):
                    act.wait_ge(x_ready, 1 + 3 * l + j)
                    squares(1 + 3 * l + j, x, xn)
                    if m is not None:
                        mod(one, l, m, before)
                    hT_bank(one, l, ab, lambda k: gain[:, bass.ds(l * KT + k, 1)])

                norm(0, ("T0a", "T0b"), g_mix)
                copy(one, l, "in_q", qk[:, :, 0:512], lambda p: p[:, :, :])
                finished(act, one, l, "in_kv")
                p = ps[one.pair("in_kv")]
                act.activation(qk[:, :, 512:640], p[:, :, 0:P], ACT.Copy)
                act.activation(vv[:, :, :], p[:, :, P:2 * P], ACT.Copy).then_inc(pair_free[one.pair("in_kv")], 2)
                copy(one, l, "in_v", vg[:, :, :], lambda p: p[:, :, :], ACT.Gelu_apprx_tanh)
                copy(one, l, "in_u", ug[:, :, :], lambda p: p[:, :, :], ACT.Gelu_apprx_tanh)
                copy(one, l, "ws", w_s_now, lambda p: p[:, 0, :])
                second_bank(one, l, "qT", qkT[:, 2:4, :].rearrange("p a b -> p (a b)"))
                copy(one, l, "kT", qkT[:, 4:6, :].rearrange("p a b -> p (a b)"), lambda p: p[:, 0, :])

                def keys(i):
                    copy(one, l, f"xk{i}", kxT[:, 4 * i:4 * i + 4, :].rearrange("p k s -> p (k s)"), flat)

                def values(i):
                    copy(one, l, f"xv{i}", vx[:, :, i * 512:(i + 1) * 512], lambda p: p[:, :, :])

                def att_exp(b):
                    act.wait_ge(sm["smax_ready"], 4 * l + b + 1)
                    exps(one, l, f"S{b}", b, pr[:, b % 2, :])

                def att_turn(b):
                    second_bank(one, l, f"P{b}", pTr[:, b % 2, 512:1024])

                att_exp(0)
                att_exp(1)
                keys(0)
                att_turn(0)
                att_exp(2)
                keys(1)
                att_turn(1)
                att_exp(3)
                values(0)
                att_turn(2)
                att_turn(3)
                values(1)
                finished(act, one, l, "V3")
                high_parts(u1, l, u1.of("out0")[0:2])
                hT_bank(one, l, ("Ma", "Mb"), lambda k: g_br[:, bass.ds(l * KT + k, 1)])
                high_activations(u1, l, ("Ma", "Mb"))
                high_parts(u1, l, u1.of("out0")[2:BUFFERS])
                high_parts(u1, l, u1.ahead("out0"))
                high_parts(u1, l, u1.ahead("out1"))
                high_parts(u1, l, u1.of("xq0")[0:2])
                norm(1, ("T1a", "T1b"), g_xa, 0)
                high_activations(u1, l, ("T1a", "T1b"))
                high_parts(u1, l, u1.of("xq0")[2:BUFFERS])
                for i in range(2):
                    high_parts(u1, l, u1.ahead(f"xq{i}"))
                    copy(one, l, f"xq{i}", qxT[:, 4 * i:4 * i + 4, :].rearrange("p k s -> p (k s)"), flat)
                for h in range(HALVES):
                    act.wait_ge(sm["xmax_ready"], 2 * l + h + 1)
                    exps(one, l, f"XS{h}", h, px[:, h, :])
                mod(one, l, 4, 0)
                for h in range(HALVES):
                    copy(one, l, f"XP{h}", pxT[:, 2:4, :, h * P:(h + 1) * P],
                         lambda p: p[:, 1, :].rearrange("p (j t q) -> p j t q", j=2, t=2), n=1)
                for i in range(2):
                    second_bank(one, l, ("XOa", "XOb")[i], oxT[:, 4 * i + 2:4 * i + 4, :].rearrange("p a b -> p (a b)"))
                high_activations(u1, l, ("XOa", "XOb"), oxT)
                high_parts(u1, l, u1.of("xo0")[0:BUFFERS])
                mod(one, l, 1, 4)
                high_parts(u1, l, u1.ahead("xo0"))
                high_parts(u1, l, u1.ahead("xo1"))
                norm(2, ("T2a", "T2b"), g_ffn, 6, 1)
                act.wait_ge(sm["rmax_ready"], l + 1)
                p = ps[one.pair("route")]
                for h in range(HALVES):
                    last = act.activation(aff[:, h, :], p[:, 0, h * NE:(h + 1) * NE], ACT.Exp,
                                          bias=nmax[:, 0, h:h + 1], accum_out=ssum[:, 0, h:h + 1])
                last.then_inc(pair_free[one.pair("route")], 2)
                mod(one, l, 3, 6)
                mod(one, l, 7, 3)
                second_bank(one, l, "gateT", gateT[:, 2:4, :, :].rearrange("p g h t -> p (g h t)"))
                with act.Fori(0, GROUPS) as g:
                    copy(one, l, "g0", act_mid[:, :], flat, ACT.Silu, after=f"g{KT - 1}", g=g)
                    second_bank(one, l, "midT", midT[:, 4:8, :].rearrange("p a b -> p (a b)"), g=g)
                    copy(one, l, "d0", ys[:, bass.ds(g, 1), :].rearrange("p a d -> p (a d)"), flat, after=f"d{KT - 1}", g=g)
            act.wait_ge(x_ready, 1 + 3 * LAYERS)
            squares(1 + 3 * LAYERS, x, xn)

            finished(act, one, LAYERS - 1, "C1")
            with act.Fori(0, LAYERS) as l:
                def norm2(j, ab, m, before):
                    act.wait_ge(x_ready, 8 + 3 * l + j)
                    squares(8 + 3 * l + j, x, xn)
                    mod(two, l, m, before)
                    hT_bank(two, l, ab, lambda k: mcol_of(l, 3 * j + 1, k), lambda k: mcol_of(l, 3 * j, k))

                def ffn(f, j):
                    for c, n in enumerate(FFC):
                        high_parts(u2, l, u2.ahead(f"{f}g{c}"))
                        if c >= 2:
                            act.wait_ge(sm["m_lo"], (2 * l + j) * len(FFC) + c - 1)
                        copy(two, l, f"{f}g{c}", sg[:, c % 2, 0:2 * n], lambda p: flat(p)[:, 0:2 * n], ACT.Silu)
                        high_parts(u2, l, u2.ahead(f"{f}u{c}"))
                        act.wait_ge(sm["m_ready"], (2 * l + j) * len(FFC) + c + 1)
                        act.activation(hm_hi[:, 4 * c:4 * c + n // P, :].rearrange("p a b -> p (a b)"),
                                       sg[:, c % 2, 0:2 * n], ACT.Copy).then_inc(sm["m_hi"], 1)
                    for n in range(D // CHUNK):
                        for i in range(len(DOWN)):
                            high_parts(u2, l, u2.ahead(f"{f}d{n}_{i}"))

                high_parts(u2, l, u2.of("Ag0")[0:2])
                norm2(0, ("T0a", "T0b"), 2, None)
                high_activations(u2, l, ("T0a", "T0b"))
                high_parts(u2, l, u2.of("Ag0")[2:BUFFERS])
                ffn("A", 0)
                norm2(1, ("T1a", "T1b"), 5, 2)
                def decays(i):
                    if i >= 2:
                        act.wait_ge(sm["hq_ready"], LEVELS * l + i - 1)
                    copy(two, l, f"HE{i}", he[:, i % 2, :], flat, ACT.Exp)

                def two_parts(name, dst_a, dst_b):
                    finished(act, two, l, name)
                    p = ps[two.pair(name)]
                    act.activation(dst_a, p[:, :, 0:256], ACT.Copy)
                    act.activation(dst_b, p[:, :, 256:512], ACT.Copy).then_inc(pair_free[two.pair(name)], 2)

                copy(two, l, "in_fh", fz, flat)
                act.wait_ge(sm["fab_ready"], l + 1)
                act.activation(fa, fa, ACT.Exp, scale=-1.0)
                act.drain()
                act.activation(fa, fa, ACT.Ln, bias=1.0).then_inc(sm["flog"], 1)
                copy(two, l, "in_qka", qkaT[:, :, :].rearrange("p a b -> p (a b)"), flat)
                act.wait_ge(sm["fd_ready"], l + 1)
                act.activation(fd, fd, ACT.Exp, scale=-1.0)
                act.activation(khT[:, :, :].rearrange("p a b -> p (a b)"), fs, ACT.Exp, scale=-1.0)
                act.drain()
                act.activation(fd, fd, ACT.Ln, bias=1.0).then_inc(sm["fl2"], 1)
                act.wait_ge(sm["sp_in"], l + 1)
                act.activation(sp_both, sp_both, ACT.Exp, scale=-1.0)
                act.drain()
                act.activation(sp_both, sp_both, ACT.Ln, bias=1.0).then_inc(sm["st_log"], 1)
                copy(two, l, "in_qh", qhT[:, :, :].rearrange("p a b -> p (a b)"), flat, ACT.Silu)
                copy(two, l, "HL", lfn[:, :, :], lambda p: p[:, :, :])
                decays(0)
                decays(1)
                two_parts("in_vaqd", va_vd[:, :, 0:256], dq[:, :, 0:256])
                act.wait_ge(sm["w_arg"], l + 1)
                act.activation(z_both, z_both, ACT.Exp).then_inc(sm["w_exp"], 1)
                decays(2)
                decays(3)
                two_parts("in_kdvd", dq[:, :, 256:512], va_vd[:, :, 256:512])
                copy(two, l, "SV", xn[:, :, 0:256], lambda p: p[:, :, 0:256])
                decays(4)
                decays(5)
                copy(two, l, "in_ih", ih[:, :, :], lambda p: p[:, :, :])
                decays(6)
                decays(7)
                second_bank(two, l, "DT", dT[:, 2:4, :].rearrange("p a b -> p (a b)"))
                for h in range(HALVES):
                    act.wait_ge(sm["dmax_ready"], 2 * l + h + 1)
                    for j in range(4):
                        last = act.activation(dp[:, h, j * S:(j + 1) * S], dp[:, h, j * S:(j + 1) * S], ACT.Exp,
                                              bias=nmax[:, h, j:j + 1], scale=HD ** -0.5)
                    last.then_inc(sm["dexp"], 1)
                copy(two, l, f"HS{LEVELS - 1}", at2[:, :, :].rearrange("p a b -> p (a b)"), lambda p: p[:, 0, :])
                copy(two, l, "in_gh", gh[:, :, :], lambda p: p[:, :, :], ACT.Silu)
                for h in range(HALVES):
                    second_bank(two, l, f"DP{h}", dpT[:, h, 512:1024])
                finished(act, two, l, "HO")
                high_parts(u2, l, u2.of("out0")[0:2])
                for i in range(2):
                    second_bank(two, l, ("Ya", "Yb")[i], hT[:, 4 * i + 2:4 * i + 4, :].rearrange("p a b -> p (a b)"))
                high_activations(u2, l, ("Ya", "Yb"))
                high_parts(u2, l, u2.of("out0")[2:BUFFERS])
                high_parts(u2, l, u2.ahead("out0"))
                high_parts(u2, l, u2.ahead("out1"))
                high_parts(u2, l, u2.of("Bg0")[0:2])
                norm2(2, ("T2a", "T2b"), 8, 5)
                high_activations(u2, l, ("T2a", "T2b"))
                high_parts(u2, l, u2.of("Bg0")[2:BUFFERS])
                ffn("B", 1)

        @block.gpsimd
        def _(pool):
            pool.memset(mhalf[:, :], -0.5)
            pool.memset(eps[:, :], EPS)
            pool.memset(quarter[:, :], 0.25)
            pool.memset(c32[:, :, :], 0.0).then_inc(sm["c_silu"], 1)

            def rms(r):
                pool.wait_ge(ss_ready, r + 1)
                pool.tensor_tensor(ms[:, :], ss[:, :], eps[:, :], ALU.add)
                pool.drain()
                pool.tensor_tensor(rstd[:, :], ms[:, :], mhalf[:, 0:2], ALU.pow).then_inc(rstd_ready, 1)

            def root(n, width):
                pool.wait_ge(var_ready, n + 1)
                pool.tensor_tensor(inv[:, 0:width], var[:, 0:width], mhalf[:, 0:width], ALU.pow).then_inc(inv_ready, 1)

            pool.drain()
            rms(0)
            pool.wait_ge(sm["lb_floor"], 1)
            pool.tensor_tensor(lb_ln[:, :], lb_ln[:, :], quarter[:, :], ALU.pow).then_inc(sm["lb_root"], 1)
            with pool.Fori(0, LAYERS) as l:
                rms(1 + 3 * l)
                pool.wait_ge(load_p, 16 * N_SMALL)
                finished(pool, one, l - 1, "mix")
                pool.tensor_copy(w_s_now, w_s[:, bass.ds(l, 1), :].rearrange("p a b -> p (a b)")).then_inc(sm["ws_now"], 1)
                root(3 * l, 20)
                root(3 * l + 1, 2)
                root(3 * l + 2, 4)
                rms(2 + 3 * l)
                rms(3 + 3 * l)
            rms(1 + 3 * LAYERS)
            with pool.Fori(0, LAYERS) as l:
                rms(8 + 3 * l)
                rms(9 + 3 * l)
                root(3 * LAYERS + 2 * l, 16)
                root(3 * LAYERS + 2 * l + 1, 8)
                rms(10 + 3 * l)

        @block.vector
        def _(v):
            def flat(p):
                return p[:, :, :].rearrange("p a b -> p (a b)")

            def free(order, name, ins, n=2):
                ins.then_inc(pair_free[order.pair(name)], n)

            def norm_rows(r, src):
                v.wait_ge(rstd_ready, r + 1)
                for h in range(HALVES):
                    last = v.tensor_scalar(xn[:, h, :], src[:, h, :], rstd[:, h:h + 1], None, ALU.mult)
                last.then_inc(xn_ready, 2)

            def hT_bank(order, l, ab, scale, bias=None, dst=hT):
                for i in range(2):
                    finished(v, order, l, ab[i])
                    p = ps[order.pair(ab[i])]
                    for kk in range(2):
                        k = 4 * i + kk
                        if bias is None:
                            last = v.tensor_scalar(dst[:, k, :], p[:, 0, kk * S:(kk + 1) * S], scale(k), None, ALU.mult)
                        else:
                            last = v.tensor_scalar(dst[:, k, :], p[:, 0, kk * S:(kk + 1) * S], scale(k), bias(k), ALU.mult, ALU.add)
                    free(order, ab[i], last, 1)

            def first_bank(order, l, name, dst, g=0):
                finished(v, order, l, name, g)
                free(order, name, v.tensor_copy(dst, ps[order.pair(name)][:, 0, :]), 1)

            def low_parts(u, l, units):
                for i in units:
                    v.wait_ge(sm["w_hi"], u.counts(l, i))
                    src = unit_source(v, u, l, i)
                    n = src.shape[2]
                    v.tensor_tensor(unit_part(u, i, 1, n), src, unit_part(u, i, 0, n).bitcast(F32), ALU.subtract).then_inc(sm["w_lo"], 1)

            def low_activations(u, l, s, src=hT):
                hi, lo = act_parts[u]
                for i in range(2):
                    v.wait_ge(sm["h_hi"], u.halves(l, s, i))
                    k = slice(4 * i, 4 * i + 4)
                    v.tensor_tensor(lo[:, k, :], src[:, k, :], hi[:, k, :].bitcast(F32), ALU.subtract).then_inc(sm["h_lo"], 1)

            def add_to_x(order, l, names, between=None):
                for i, n in enumerate(names):
                    low_parts(u1, l, u1.ahead(n))
                    finished(v, order, l, n)
                    cols = slice(i * CHUNK, (i + 1) * CHUNK)
                    free(order, n, v.tensor_tensor(x[:, :, cols], x[:, :, cols], ps[order.pair(n)][:, :, :], ALU.add))
                    if i == 0 and between is not None:
                        shift_or_scale(l, between)
                v.drain().then_inc(x_ready, 1)

            def add_gated(order, l, names, last_steps, gate):
                for i, n in enumerate(names):
                    finished(v, order, l, last_steps[i])
                    cols = slice(i * CHUNK, (i + 1) * CHUNK)
                    g_ = gate_b[:, gate:gate + 1, cols].broadcast_to([P, HALVES, CHUNK])
                    free(order, n, v.tensor_tensor(tmp[:, :, :], ps[order.pair(n)][:, :, :], g_, ALU.mult))
                    v.drain()
                    v.tensor_tensor(x[:, :, cols], x[:, :, cols], tmp[:, :, :], ALU.add)
                    v.drain()
                v.drain().then_inc(x_ready, 1)

            def inverse_root(n, width, count):
                v.drain()
                v.tensor_scalar(var[:, 0:count], var[:, 0:count], 1.0 / width, EPS, ALU.mult, ALU.add).then_inc(var_ready, 1)
                v.wait_ge(inv_ready, n + 1)

            def sum_squares(src, scratch, out_):
                v.tensor_tensor(scratch, src, src, ALU.mult)
                v.drain()
                v.tensor_reduce(out_, scratch, AX.X, ALU.add)

            def rope(dst, src, cos, sin, a, b, ta, tb):
                heads = src.shape[1]
                c = cos.rearrange("p (o n) -> p o n", o=1).broadcast_to([P, heads, HD // 2])
                s_ = sin.rearrange("p (o n) -> p o n", o=1).broadcast_to([P, heads, HD // 2])
                v.tensor_tensor(ta, a(src), c, ALU.mult)
                v.tensor_tensor(tb, b(src), s_, ALU.mult)
                v.drain()
                v.tensor_tensor(a(dst), ta, tb, ALU.subtract)
                v.drain()
                v.tensor_tensor(ta, a(src), s_, ALU.mult)
                v.tensor_tensor(tb, b(src), c, ALU.mult)
                v.drain()
                v.tensor_tensor(b(dst), ta, tb, ALU.add)
                v.drain()

            def by_place(r):
                return r.rearrange("p (b a o) -> p b a o", b=2, o=1).broadcast_to([P, 2, 2, HD])

            def row_max(order, l, name, b, scale, ready):
                finished(v, order, l, name)
                v.tensor_reduce(smax[:, b, :], flat(ps[order.pair(name)]).rearrange("p (j s) -> p j s", j=4), AX.X, ALU.max)
                v.drain()
                v.tensor_scalar(nmax[:, b, :], smax[:, b, :], -scale, None, ALU.mult).then_inc(ready, 1)

            finished(v, begin, 0, "G")
            free(begin, "G", v.tensor_copy(vectors[:, :], ps[begin.pair("G")][:, 0, 0:96]))
            finished(v, begin, 0, "GB")
            free(begin, "GB", v.tensor_copy(biases[:, :], ps[begin.pair("GB")][:, 0, 0:LAYERS * NMOD * KT]))
            v.drain()
            a0, a1 = lbl[:, 0:HH], lbl[:, HH:2 * HH]
            v.tensor_tensor(lbt[:, 0, :], a0, a1, ALU.max)
            v.drain()
            v.tensor_tensor(a0, a0, lbt[:, 0, :], ALU.subtract)
            v.tensor_tensor(a1, a1, lbt[:, 0, :], ALU.subtract).then_inc(sm["lb_exp"], 1)
            v.wait_ge(sm["lb_sum"], 1)
            v.tensor_tensor(lbt[:, 0, :], a0, a1, ALU.add)
            v.drain()
            v.reciprocal(lbt[:, 1, :], lbt[:, 0, :])
            v.drain()
            v.tensor_tensor(a0, a0, lbt[:, 1, :], ALU.mult)
            v.tensor_tensor(a1, a1, lbt[:, 1, :], ALU.mult)
            v.drain()
            v.tensor_tensor(lbt[:, 2, :], a0, a1, ALU.add)
            v.drain()
            v.tensor_tensor(lb_ln[:, 0:HH], a0, a0, ALU.subtract)
            v.tensor_tensor(lb_ln[:, HH:2 * HH], lbt[:, 2, :], a0, ALU.subtract)
            v.drain()
            v.tensor_scalar(lb_ln[:, :], lb_ln[:, :], 0.0, 1.0 - EPS, ALU.max, ALU.min)
            v.drain()
            v.tensor_scalar(lb_1m[:, :], lb_ln[:, :], -1.0, 1.0, ALU.mult, ALU.add)
            v.tensor_scalar(lb_ln[:, :], lb_ln[:, :], LB_FLOOR, None, ALU.max).then_inc(sm["lb_floor"], 1)
            norm_rows(0, xn)
            hT_bank(begin, 0, ("T0a", "T0b"), lambda k: g_mem[:, k:k + 1], dst=memT)
            v.wait_ge(load_x, 16)
            v.drain().then_inc(x_ready, 1)

            def shift_or_scale(l, m):
                finished(v, one, l, f"mb{m}")
                free(one, f"mb{m}", v.scalar_tensor_tensor(
                    mcol_of(l, m, 0, KT), ps[one.pair(f"mb{m}")][:, 0, 0:KT], 1.0 if m % 3 else 0.0,
                    biases[:, bass.ds((l * NMOD + m) * KT, KT)], ALU.add, ALU.add))

            with v.Fori(0, LAYERS) as l:
                def norm(j, ab, gain):
                    norm_rows(1 + 3 * l + j, x)
                    hT_bank(one, l, ab, lambda k: gain[:, bass.ds(l * KT + k, 1)])

                norm(0, ("T0a", "T0b"), g_mix)
                v.wait_ge(load_p, 16 * N_SMALL)
                v.wait_ge(load_c, 16)
                read_out(v, one, l, "in_q", "in_kv")
                heads = QH + KVH
                qk4 = qk[:, :, :].rearrange("p h (n d) -> p (h n) d", d=HD)
                sum_squares(qk4, sq1.rearrange("p (n d) -> p n d", d=HD), var[:, 0:2 * heads])
                inverse_root(3 * l, HD, 2 * heads)
                v.tensor_tensor(qk4, qk4, inv[:, 0:2 * heads].rearrange("p (n o) -> p n o", o=1).broadcast_to([P, 2 * heads, HD]), ALU.mult)
                v.drain()
                for h in range(HALVES):
                    q3, k3 = (qk[:, h, a:b].rearrange("p (n d) -> p n d", d=HD) for a, b in ((0, 512), (512, 640)))
                    v.tensor_tensor(q3, q3, g_q1[:, bass.ds(l, 1), :].broadcast_to([P, QH, HD]), ALU.mult)
                    v.tensor_tensor(k3, k3, g_k1[:, bass.ds(l, 1), :].broadcast_to([P, KVH, HD]), ALU.mult)
                v.drain()
                for h in range(HALVES):
                    rope(rq[:, h, :].rearrange("p (n d) -> p n d", d=HD), qk[:, h, :].rearrange("p (n d) -> p n d", d=HD),
                         const("cos1", 2, 32)[:, h, :], const("sin1", 2, 32)[:, h, :],
                         lambda t: t[:, :, 0:HD:2], lambda t: t[:, :, 1:HD:2],
                         t1[:, h, :].rearrange("p (n d) -> p n d", d=HD // 2), t2[:, h, :].rearrange("p (n d) -> p n d", d=HD // 2))
                for h in range(HALVES):
                    for j in range(KVH):
                        last = v.tensor_copy(kdup[:, h, j * P:(j + 1) * P].rearrange("p (n d) -> p n d", d=HD),
                                             rq[:, h, 512 + j * HD:512 + (j + 1) * HD].rearrange("p (o d) -> p o d", o=1).broadcast_to([P, 2, HD]))
                last.then_inc(sm["rope_ready"], 1)
                read_out(v, one, l, "in_v")
                sq_ = sq1[:, 0:1024].rearrange("p (h n) -> p h n", h=HALVES)
                sum_squares(vg[:, :, :], sq_, var[:, 0:2])
                inverse_root(3 * l + 1, GM, 2)
                for h in range(HALVES):
                    v.scalar_tensor_tensor(vg[:, h, :], vg[:, h, :], inv[:, h:h + 1],
                                           g_v[:, bass.ds(l, 1), :].rearrange("p a n -> p (a n)"), ALU.mult, ALU.mult)
                v.drain().then_inc(sm["v_ready"], 1)
                first_bank(one, l, "qT", qkT[:, 0:2, :].rearrange("p a b -> p (a b)"))

                def att_max(b):
                    row_max(one, l, f"S{b}", b, HD ** -0.5, sm["smax_ready"])

                def att_turn(b):
                    first_bank(one, l, f"P{b}", pTr[:, b % 2, 0:512])

                def att_out(b):
                    h, hg = b // 2, b % 2
                    read_out(v, one, l, f"S{b}")
                    v.reciprocal(rsum[:, b, :], ssum[:, b, :])
                    v.drain()
                    finished(v, one, l, f"V{b}")
                    free(one, f"V{b}", v.tensor_tensor(
                        xn[:, h, 512 + 256 * hg:768 + 256 * hg].rearrange("p (a b d) -> p b a d", b=2, d=HD),
                        ps[one.pair(f"V{b}")][:, 0, 0:256].rearrange("p (b a d) -> p b a d", b=2, d=HD),
                        by_place(rsum[:, b, :]), ALU.mult))

                att_max(0)
                att_max(1)
                read_out(v, one, l, "in_u")
                finished(v, one, l, "mix")
                for h in range(HALVES):
                    for i in range(4):
                        cols = slice(i * P, (i + 1) * P)
                        last = v.scalar_tensor_tensor(ug[:, h, cols], ps[one.pair("mix")][:, h, cols],
                                                      b_s[:, bass.ds(l * 4 + i, 1)], ug[:, h, cols], ALU.add, ALU.mult)
                free(one, "mix", last)
                v.drain()
                sum_squares(ug[:, :, :], qk[:, :, 0:512], var[:, 0:2])
                att_turn(0)
                att_out(0)
                att_max(2)
                att_turn(1)
                att_out(1)
                att_max(3)
                att_turn(2)
                att_turn(3)
                att_out(2)
                att_out(3)
                v.drain()
                sum_squares(xn[:, :, 512:1024], qk[:, :, 0:512], var[:, 2:4])
                inverse_root(3 * l + 2, GM, 4)
                for h in range(HALVES):
                    v.tensor_scalar(xn[:, h, 0:512], ug[:, h, :], inv[:, h:h + 1], None, ALU.mult)
                    v.tensor_scalar(xn[:, h, 512:1024], xn[:, h, 512:1024], inv[:, 2 + h:3 + h], None, ALU.mult)
                v.drain().then_inc(sm["merged"], 1)
                low_parts(u1, l, u1.of("out0")[0:2])
                hT_bank(one, l, ("Ma", "Mb"), lambda k: g_br[:, bass.ds(l * KT + k, 1)])
                low_activations(u1, l, 0)
                low_parts(u1, l, u1.of("out0")[2:BUFFERS])
                add_to_x(one, l, ("out0", "out1"))
                low_parts(u1, l, u1.of("xq0")[0:2])
                norm(1, ("T1a", "T1b"), g_xa)
                low_activations(u1, l, 1)
                low_parts(u1, l, u1.of("xq0")[2:BUFFERS])
                low_parts(u1, l, u1.ahead("xq0"))
                shift_or_scale(l, 0)
                low_parts(u1, l, u1.ahead("xq1"))
                for h in range(HALVES):
                    row_max(one, l, f"XS{h}", h, XD ** -0.5, sm["xmax_ready"])
                for h in range(HALVES):
                    read_out(v, one, l, f"XS{h}")
                    v.reciprocal(rsum[:, h, :], ssum[:, h, :])
                    v.drain()
                    for j in range(XH):
                        last = v.tensor_scalar(px[:, h, j * S:(j + 1) * S], px[:, h, j * S:(j + 1) * S],
                                               rsum[:, h, j:j + 1], None, ALU.mult)
                    last.then_inc(sm["xpn_ready"], 1)
                for h in range(HALVES):
                    finished(v, one, l, f"XP{h}")
                    free(one, f"XP{h}", v.tensor_copy(pxT[:, 0:2, :, h * P:(h + 1) * P],
                                                      ps[one.pair(f"XP{h}")][:, 0, :].rearrange("p (j t q) -> p j t q", j=2, t=2)), 1)
                shift_or_scale(l, 4)
                for i in range(2):
                    first_bank(one, l, ("XOa", "XOb")[i], oxT[:, 4 * i:4 * i + 2, :].rearrange("p a b -> p (a b)"))
                low_activations(u1, l, 2, oxT)
                low_parts(u1, l, u1.of("xo0")[0:BUFFERS])
                add_to_x(one, l, ("xo0", "xo1"), 1)
                norm(2, ("T2a", "T2b"), g_ffn)
                shift_or_scale(l, 6)
                finished(v, one, l, "route")
                v.tensor_reduce(smax[:, 0, 0:2], ps[one.pair("route")][:, 0, 0:2 * NE].rearrange("p (h e) -> p h e", h=2), AX.X, ALU.max)
                v.drain()
                v.tensor_scalar(nmax[:, 0, 0:2], smax[:, 0, 0:2], -1.0, None, ALU.mult).then_inc(sm["rmax_ready"], 1)
                read_out(v, one, l, "route")
                v.reciprocal(rsum[:, 0, 0:2], ssum[:, 0, 0:2])
                v.drain()
                v.tensor_tensor(aff[:, :, :], aff[:, :, :],
                                rsum[:, 0, 0:2].rearrange("p (n o) -> p n o", o=1).broadcast_to([P, HALVES, NE]), ALU.mult).then_inc(sm["aff_ready"], 1)
                finished(v, one, l, "affT")
                free(one, "affT", v.tensor_copy(aw[0], ps[one.pair("affT")][0:NE, 0, 0:S]))
                v.drain()
                for i in range(CAP // 8):
                    src, dst = aw[i % 2], aw[(i + 1) % 2]
                    v.max(small[0:NE, 8 * i:8 * i + 8], src)
                    v.drain()
                    v.match_replace(dst, small[0:NE, 8 * i:8 * i + 8], src, -1.0)
                    v.drain()
                taken, ones_, count = aw[2], aw[3], aw[4]
                v.tensor_scalar(taken, aw[(CAP // 8) % 2], -1.0, None, ALU.is_equal)
                v.memset(ones_, 1.0)
                v.drain()
                v.tensor_tensor_scan(count, ones_, taken, 0.0, ALU.mult, ALU.add)
                v.drain()
                v.tensor_tensor(count, count, taken, ALU.mult)
                v.drain()
                v.tensor_scalar(aw[5], count, -1.0, None, ALU.add).then_inc(sm["pos_ready"], 1)
                shift_or_scale(l, 3)
                finished(v, one, l, "posT")
                free(one, "posT", v.tensor_copy(posn[:, :, :], ps[one.pair("posT")][:, 0, 0:2 * NE].rearrange("p (h e) -> p h e", h=2)))
                v.drain()
                for h in range(HALVES):
                    v.tensor_tensor(sel[:, h, :].rearrange("p (e c) -> p e c", e=NE),
                                    posn[:, h, :].rearrange("p (e o) -> p e o", o=1).broadcast_to([P, NE, CAP]),
                                    const("iota", NE, CAP), ALU.is_equal)
                v.drain()
                for h in range(HALVES):
                    v.tensor_tensor(selg[:, h, :].rearrange("p (e c) -> p e c", e=NE), sel[:, h, :].rearrange("p (e c) -> p e c", e=NE),
                                    aff[:, h, :].rearrange("p (e o) -> p e o", o=1).broadcast_to([P, NE, CAP]), ALU.mult)
                v.drain().then_inc(sm["sel_ready"], 1)
                shift_or_scale(l, 7)
                first_bank(one, l, "gateT", gateT[:, 0:2, :, :].rearrange("p g h t -> p (g h t)"))
                with v.Fori(0, GROUPS) as g:
                    finished(v, one, l, "gather", g)
                    for b in range(2):
                        last = v.tensor_tensor(xsT[:, 4 * b:4 * b + 4, :], ps[one.pair("gather")][:, b, :].rearrange("p (k s) -> p k s", k=4),
                                               g_ffn[:, bass.ds(l * KT + 4 * b, 4)].rearrange("p (k o) -> p k o", o=1).broadcast_to([P, 4, P]), ALU.mult)
                    free(one, "gather", last)
                    read_out(v, one, l, "g0", g=g)
                    finished(v, one, l, f"u{KT - 1}", g)
                    free(one, "u0", v.tensor_tensor(mid[:, :], act_mid[:, :], flat(ps[one.pair("u0")]), ALU.mult))
                    first_bank(one, l, "midT", midT[:, 0:4, :].rearrange("p a b -> p (a b)"), g)
                for h in range(HALVES):
                    finished(v, one, l, f"C{h}")
                    free(one, f"C{h}", v.tensor_tensor(x[:, h, :], x[:, h, :], flat(ps[one.pair(f"C{h}")]), ALU.add))
                v.drain().then_inc(x_ready, 1)
            v.wait_ge(sm["lb_log"], 1)
            v.tensor_scalar(lb_ln[:, :], lb_ln[:, :], 4.0, None, ALU.mult)
            r = 1 + 3 * LAYERS
            v.wait_ge(rstd_ready, r + 1)
            for h in range(HALVES):
                v.scalar_tensor_tensor(x[:, h, :], x[:, h, :], rstd[:, h:h + 1], g_final[:, :], ALU.mult, ALU.mult)
            v.drain().then_inc(xn_ready, 2)
            v.drain().then_inc(x_ready, 1)

            with v.Fori(0, LAYERS) as l:
                def norm2(j, ab):
                    norm_rows(8 + 3 * l + j, x)
                    hT_bank(two, l, ab, lambda k: mcol_of(l, 3 * j + 1, k), lambda k: mcol_of(l, 3 * j, k))

                def pick_bias(m):
                    rows_ = 2 * NMOD * LAYERS
                    for i in range(2):
                        last = v.tensor_copy(pick[:, i, :], ident[0:rows_, bass.ds(l * 2 * NMOD + 2 * m + i, 1)].broadcast_to([rows_, P]))
                    last.then_inc(sm["pick_ready"], 1)

                def mod(m):
                    finished(v, two, l, f"mb{m}")
                    free(two, f"mb{m}", v.tensor_scalar(gate_b[:, m // 3, :], flat(ps[two.pair(f"mb{m}")]),
                                                        1.0 if m == 5 else 0.5, None, ALU.mult))

                def ffn(f, j, gate):
                    for c, n in enumerate(FFC):
                        low_parts(u2, l, u2.ahead(f"{f}g{c}"))
                        low_parts(u2, l, u2.ahead(f"{f}u{c}"))
                        read_out(v, two, l, f"{f}g{c}")
                        finished(v, two, l, f"{f}u{c}")
                        m = sg[:, c % 2, 0:2 * n]
                        free(two, f"{f}u{c}", v.tensor_tensor(m, m, flat(ps[two.pair(f"{f}u{c}")])[:, 0:2 * n], ALU.mult))
                        v.drain().then_inc(sm["m_ready"], 1)
                        v.wait_ge(sm["m_hi"], (2 * l + j) * len(FFC) + c + 1)
                        hi, lo = (t[:, 4 * c:4 * c + n // P, :].rearrange("p a b -> p (a b)") for t in (hm_hi, hm_lo))
                        v.tensor_tensor(lo, m, hi.bitcast(F32), ALU.subtract).then_inc(sm["m_lo"], 1)
                    for n in range(D // CHUNK):
                        for i in range(len(DOWN)):
                            low_parts(u2, l, u2.ahead(f"{f}d{n}_{i}"))
                    v.drain()
                    add_gated(two, l, (f"{f}d0_0", f"{f}d1_0"), [f"{f}d{n}_{len(DOWN) - 1}" for n in range(2)], gate)

                pick_bias(2)
                low_parts(u2, l, u2.of("Ag0")[0:2])
                norm2(0, ("T0a", "T0b"))
                low_activations(u2, l, 0)
                low_parts(u2, l, u2.of("Ag0")[2:BUFFERS])
                mod(2)
                ffn("A", 0, 0)
                pick_bias(5)
                norm2(1, ("T1a", "T1b"))
                mod(5)
                pick_bias(8)
                read_out(v, two, l, "in_fh")
                v.scalar_tensor_tensor(fa, fz, -1.0, fz, ALU.mult, ALU.max).then_inc(sm["fab_ready"], 1)
                v.wait_ge(sm["flog"], l + 1)
                v.scalar_tensor_tensor(fm, fz, 0.0, fa, ALU.min, ALU.subtract)
                v.scalar_tensor_tensor(fs, fz, 0.0, fa, ALU.max, ALU.add)
                v.drain()
                for j in range(HH):
                    one_, ln_a, ln_b = (t[:, bass.ds(l * HH + j, 1)] for t in (lb_1m, lb_ln, lb_ln1m))
                    c = slice(j * S, (j + 1) * S)
                    v.tensor_scalar(fx[:, c], fm[:, c], ln_b, ln_a, ALU.add, ALU.max)
                    v.tensor_scalar(fd[:, c], fm[:, c], ln_b, ln_a, ALU.add, ALU.subtract)
                v.drain()
                v.scalar_tensor_tensor(fd, fd, -1.0, fd, ALU.mult, ALU.max).then_inc(sm["fd_ready"], 1)
                v.wait_ge(sm["fl2"], l + 1)
                v.tensor_tensor(lfT[:, :, :].rearrange("p a b -> p (a b)"), fx, fd, ALU.add)
                for j in range(HH):
                    v.tensor_scalar(khT[:, j, :], khT[:, j, :], lb_1m[:, bass.ds(l * HH + j, 1)], None, ALU.mult)
                v.drain().then_inc(sm["lf_ready"], 1)
                v.drain().then_inc(sm["kh_ready"], 1)
                def dilated_out(h):
                    first_bank(two, l, f"DP{h}", dpT[:, h, 0:512])
                    finished(v, two, l, f"DV{h}")
                    free(two, f"DV{h}", v.tensor_tensor(
                        xn[:, h, 256:512].rearrange("p (a b d) -> p b a d", b=2, d=HD),
                        ps[two.pair(f"DV{h}")][:, 0, 0:256].rearrange("p (b a d) -> p b a d", b=2, d=HD),
                        by_place(rsum[:, h, :]), ALU.mult))

                q_all, k_all = (t[:, :, :].rearrange("p a b -> p (a b)") for t in (qhT, khT))
                masks = const("level_mask", LEVELS, P).bitcast(U32)

                def products(i):
                    read_out(v, two, l, f"HE{i}", *(["in_qh"] if i == 0 else []))
                    b = 64 >> i if i < LEVELS - 1 else P
                    e_, o_, q_, k_ = (t.rearrange("p (n two b) -> p n two b", two=2, b=b)
                                      for t in (he[:, i % 2, :], hq[:, i % 2, :], q_all, k_all))
                    v.tensor_tensor(o_[:, :, 0, :], e_[:, :, 0, :], k_[:, :, 0, :], ALU.mult)
                    v.tensor_tensor(o_[:, :, 1, :], e_[:, :, 1, :], q_[:, :, 1, :], ALU.mult)
                    v.drain().then_inc(sm["hq_ready"], 1)

                def take(name, i):
                    finished(v, two, l, name)
                    free(two, name, v.copy_predicated(
                        at_[:, :, :], masks[:, i:i + 1, :].broadcast_to([P, 8, P]),
                        flat(ps[two.pair(name)]).rearrange("p (n t) -> p n t", n=8)))
                    v.drain()

                finished(v, two, l, "SZ0")
                free(two, "SZ0", v.tensor_scalar(z0[:, :, :].rearrange("p a b -> p (a b)"), flat(ps[two.pair("SZ0")]), HD ** -0.5, None, ALU.mult))
                finished(v, two, l, "SZ1")
                free(two, "SZ1", v.tensor_scalar(z1[:, :, :].rearrange("p (b a) q -> p b (a q)", b=2), ps[two.pair("SZ1")][:, :, 0:2 * P], HD ** -0.5, None, ALU.mult))
                v.drain()
                v.scalar_tensor_tensor(sp_both, z_both, -1.0, z_both, ALU.mult, ALU.max).then_inc(sm["sp_in"], 1)
                v.wait_ge(sm["st_log"], l + 1)
                v.scalar_tensor_tensor(sp_both, z_both, 0.0, sp_both, ALU.max, ALU.add)
                v.drain()
                before = const("key_before_query").rearrange("p (o q) -> p o q", o=1).broadcast_to([P, 4, P])
                v.tensor_tensor(sp0[:, :, 0:P], sp0[:, :, 0:P], before, ALU.mult)
                v.tensor_tensor(sp1[:, :, :], sp1[:, :, :], before, ALU.mult)
                v.drain().then_inc(sm["sp_ready"], 1)
                products(0)
                products(1)
                v.memset(at_[:, :, :], 0.0)
                v.drain()
                for name, z_ in (("SC0", z0), ("SC1", z1)):
                    finished(v, two, l, name)
                    zf = z_[:, :, :].rearrange("p a b -> p (a b)")
                    p = flat(ps[two.pair(name)])[:, 0:zf.shape[1]]
                    free(two, name, v.tensor_tensor(zf, zf, p, ALU.subtract))
                v.drain()
                v.tensor_scalar(z_both, z_both, 0.0, None, ALU.min).then_inc(sm["w_arg"], 1)
                take("HS0", 0)
                products(2)
                v.wait_ge(sm["w_exp"], l + 1)
                v.tensor_tensor(z0[:, :, 0:P], z0[:, :, 0:P], before, ALU.mult)
                v.tensor_tensor(z1[:, :, :], z1[:, :, :], before, ALU.mult)
                v.drain().then_inc(sm["w_ready"], 1)
                take("HS1", 1)
                products(3)
                take("HS2", 2)
                products(4)
                take("HS3", 3)
                products(5)
                read_out(v, two, l, "in_vaqd", "in_kdvd")
                dq4 = dq[:, :, :].rearrange("p h (n d) -> p (h n) d", d=HD)
                sum_squares(dq4, dsq.rearrange("p (n d) -> p n d", d=HD), var[:, 0:16])
                inverse_root(3 * LAYERS + 2 * l, HD, 16)
                v.tensor_tensor(dq4, dq4, inv[:, 0:16].rearrange("p (n o) -> p n o", o=1).broadcast_to([P, 16, HD]), ALU.mult)
                v.drain()
                for h in range(HALVES):
                    for a, gain in ((0, g_q2), (256, g_k2)):
                        t3 = dq[:, h, a:a + 256].rearrange("p (n d) -> p n d", d=HD)
                        v.tensor_tensor(t3, t3, gain[:, bass.ds(l, 1), :].broadcast_to([P, 4, HD]), ALU.mult)
                v.drain()
                for h in range(HALVES):
                    rope(dr[:, h, :].rearrange("p (n d) -> p n d", d=HD), dq[:, h, :].rearrange("p (n d) -> p n d", d=HD),
                         const("cos2", 2, 32)[:, h, :], const("sin2", 2, 32)[:, h, :],
                         lambda t: t[:, :, 0:HD // 2], lambda t: t[:, :, HD // 2:HD],
                         dt1[:, h, :].rearrange("p (n d) -> p n d", d=HD // 2), dt2[:, h, :].rearrange("p (n d) -> p n d", d=HD // 2))
                v.drain().then_inc(sm["drope_ready"], 1)
                take("HS4", 4)
                products(6)
                take("HS5", 5)
                products(7)
                first_bank(two, l, "DT", dT[:, 0:2, :].rearrange("p a b -> p (a b)"))
                finished(v, two, l, "SV")
                for h in range(HALVES):
                    finished(v, two, l, f"DS{h}")
                    d3 = dp[:, h, :].rearrange("p (j s) -> p j s", j=4)
                    neg = const("dil_neg", HALVES, S)[:, h:h + 1, :].broadcast_to([P, 4, S])
                    free(two, f"DS{h}", v.tensor_tensor(d3, flat(ps[two.pair(f"DS{h}")]).rearrange("p (j s) -> p j s", j=4), neg, ALU.add))
                    v.drain()
                    v.tensor_reduce(smax[:, h, :], d3, AX.X, ALU.max)
                    v.drain()
                    v.tensor_scalar(nmax[:, h, :], smax[:, h, :], -HD ** -0.5, None, ALU.mult).then_inc(sm["dmax_ready"], 1)
                take("HS6", 6)
                take("HD", LEVELS - 1)
                for h in range(HALVES):
                    v.wait_ge(sm["dexp"], 2 * l + h + 1)
                    d3 = dp[:, h, :].rearrange("p (j s) -> p j s", j=4)
                    v.tensor_tensor(d3, d3, const("dil_count", HALVES, S)[:, h:h + 1, :].broadcast_to([P, 4, S]), ALU.mult)
                    v.drain().then_inc(sm["dp_ready"], 1)
                    v.tensor_reduce(ssum[:, h, :], d3, AX.X, ALU.add)
                    v.drain()
                    v.reciprocal(rsum[:, h, :], ssum[:, h, :])
                    v.drain()
                finished(v, two, l, "HO")
                free(two, "HO", v.tensor_copy(ho[:, :, :], ps[two.pair("HO")][:, :, :]))
                v.drain()
                ho4 = ho[:, :, :].rearrange("p h (n d) -> p (h n) d", d=HK)
                sum_squares(ho4, hsq.rearrange("p (n d) -> p n d", d=HK), var[:, 0:8])
                inverse_root(3 * LAYERS + 2 * l + 1, HK, 8)
                v.tensor_tensor(ho4, ho4, inv[:, 0:8].rearrange("p (n o) -> p n o", o=1).broadcast_to([P, 8, HK]), ALU.mult)
                v.drain()
                v.tensor_tensor(ho4, ho4, g_h[:, bass.ds(l, 1), :].broadcast_to([P, 8, HK]), ALU.mult)
                v.drain()
                dilated_out(0)
                dilated_out(1)
                read_out(v, two, l, "in_gh")
                v.tensor_tensor(xn[:, :, 512:1024], ho[:, :, :], gh[:, :, :], ALU.mult).then_inc(sm["y_dve"], 1)
                for i in range(2):
                    first_bank(two, l, ("Ya", "Yb")[i], hT[:, 4 * i:4 * i + 2, :].rearrange("p a b -> p (a b)"))
                low_parts(u2, l, u2.of("out0")[0:2])
                low_activations(u2, l, 1)
                low_parts(u2, l, u2.of("out0")[2:BUFFERS])
                low_parts(u2, l, u2.ahead("out0"))
                low_parts(u2, l, u2.ahead("out1"))
                add_gated(two, l, ("out0", "out1"), ("out0", "out1"), 1)
                low_parts(u2, l, u2.of("Bg0")[0:2])
                norm2(2, ("T2a", "T2b"))
                low_activations(u2, l, 2)
                low_parts(u2, l, u2.of("Bg0")[2:BUFFERS])
                mod(8)
                ffn("B", 1, 2)


_INS = ["x", "mem", "mix_norm_g", "w_in", "gm_v_norm_g", "gm_w_s", "gm_b_s", "q_norm_g", "k_norm_g", "branch_norm_g",
        "w_out", "xattn_norm_g", "mem_norm_g", "xattn_w_q", "xattn_w_kv", "xattn_w_o", "ffn_norm_g", "w_router",
        "w_gate", "w_up", "w_down", "final_norm_g", "c_2", "w_mod_2", "b_mod_2", "ffn1_w_gate_2", "ffn1_w_up_2",
        "ffn1_w_down_2", "w_in_2", "w_out_2", "q_norm_g_2", "k_norm_g_2", "hgrn_norm_g_2", "hgrn_lb_logits_2",
        "ffn2_w_gate_2", "ffn2_w_up_2", "ffn2_w_down_2"]


def kernel(**inputs):
    import concourse.bacc as bacc
    from concourse.bass_utils import run_bass_kernel_spmd

    nc = bacc.Bacc("TRN2", target_bir_lowering=False, num_devices=1)
    arrays, w = {}, {}
    for name in _INS + ["consts"]:
        a = constant_table() if name == "consts" else np.ascontiguousarray(inputs[name])
        arrays[f"in_{name}"] = a
        w[name] = nc.dram_tensor(f"in_{name}", a.shape, mybir.dt.from_np(a.dtype), kind="ExternalInput").ap()
    out = nc.dram_tensor("out_0", (1, S, D), F32, kind="ExternalOutput").ap()
    two_blocks(nc, w, out)
    r = run_bass_kernel_spmd(nc, [arrays], core_ids=[0])
    return r.results[0]["out_0"]
```
